# Optimizing a Trainium2 kernel written in Bass

```python
import jax, jax.numpy as jnp
from jax import lax
import numpy as np

D_MODEL = 1024
BATCH = 1
SEQ = 1024
DEPTH = 1

D_MIX = D_MODEL
M_HEADS = 4
M_DH = 96
M_W = M_HEADS * M_DH
M_CHUNK = 64
M_CONV = 4
A_HEADS = 6
A_KV = 2
A_DH = 64
A_W = A_HEADS * A_DH
A_KVW = A_KV * A_DH
WINDOW = 128
S_HEADS = 4
S_DH = 64
S_W = S_HEADS * S_DH
S_BLOCK = 128
EPS = 1e-6

SPLITS = (M_W, M_W, M_HEADS, M_HEADS, M_W,
          A_W, A_KVW, A_KVW, A_W,
          S_W, S_W, S_W, S_W)
N_IN = int(sum(SPLITS))
OFFSETS = tuple(int(o) for o in np.cumsum(SPLITS)[:-1])


def rmsnorm(x, g):
    xf = x.astype(jnp.float32)
    y = xf * lax.rsqrt(jnp.mean(xf * xf, axis=-1, keepdims=True) + EPS)
    return (y * g.astype(jnp.float32)).astype(x.dtype)

def alibi_slopes():
    return jnp.asarray(2.0 ** (-8.0 * np.arange(1, A_HEADS + 1) / A_HEADS), dtype=jnp.float32)

def causal_conv(u, w, b):
    C = u.shape[-1]
    out = lax.conv_general_dilated(u, w.reshape(M_CONV, 1, C).astype(u.dtype), window_strides=(1,),
                                   padding=[(M_CONV - 1, 0)], dimension_numbers=('NWC', 'WIO', 'NWC'),
                                   feature_group_count=C)
    return out + b

def mlstm_branch(u, v, i_pre, f_pre, conv_w, conv_b, wq, wk, b_i, b_f, hn_g, skip):
    B, S, _ = u.shape
    f32 = jnp.float32
    cu = jax.nn.silu(causal_conv(u, conv_w, conv_b))
    ch = cu.reshape(B, S, M_HEADS, M_DH)
    q = jnp.einsum('bshd,hde->bhse', ch, wq).astype(f32) * (M_DH ** -0.5)
    k = jnp.einsum('bshd,hde->bhse', ch, wk).astype(f32)
    vh = v.reshape(B, S, M_HEADS, M_DH).transpose(0, 2, 1, 3).astype(f32)
    log_i = (i_pre + b_i).astype(f32).transpose(0, 2, 1)
    log_f = jax.nn.log_sigmoid((f_pre + b_f).astype(f32)).transpose(0, 2, 1)
    nc = S // M_CHUNK

    def chunks(t):
        return jnp.moveaxis(t.reshape(B, M_HEADS, nc, M_CHUNK, *t.shape[3:]), 2, 0)

    causal = jnp.tril(jnp.ones((M_CHUNK, M_CHUNK), dtype=bool))

    def step(carry, inp):
        C, n, m = carry
        qb, kb, vb, li, lf = inp
        b = jnp.cumsum(lf, axis=-1)
        g = b[..., -1]
        dmat = jnp.where(causal, b[..., :, None] - b[..., None, :] + li[..., None, :], -jnp.inf)
        inter = b + m[..., None]
        m_t = jnp.maximum(inter, jnp.max(dmat, axis=-1))
        w_inter = jnp.exp(inter - m_t)
        s = jnp.einsum('bhtd,bhsd->bhts', qb, kb) * jnp.exp(dmat - m_t[..., None])
        num = w_inter[..., None] * jnp.einsum('bhed,bhtd->bhte', C, qb) + jnp.einsum('bhts,bhse->bhte', s, vb)
        den = w_inter * jnp.einsum('bhd,bhtd->bht', n, qb) + jnp.sum(s, axis=-1)
        h = num / jnp.maximum(jnp.abs(den), jnp.exp(-m_t))[..., None]
        decay_s = g[..., None] - b + li
        m_next = jnp.maximum(g + m, jnp.max(decay_s, axis=-1))
        ws = jnp.exp(decay_s - m_next[..., None])
        carry_scale = jnp.exp(g + m - m_next)
        C_next = carry_scale[..., None, None] * C + jnp.einsum('bhs,bhse,bhsd->bhed', ws, vb, kb)
        n_next = carry_scale[..., None] * n + jnp.einsum('bhs,bhsd->bhd', ws, kb)
        return (C_next, n_next, m_next), h

    init = (jnp.zeros((B, M_HEADS, M_DH, M_DH), f32), jnp.zeros((B, M_HEADS, M_DH), f32),
            jnp.zeros((B, M_HEADS), f32))
    _, hs = lax.scan(step, init, (chunks(q), chunks(k), chunks(vh), chunks(log_i), chunks(log_f)))
    h = jnp.moveaxis(hs, 0, 2).reshape(B, M_HEADS, S, M_DH).transpose(0, 2, 1, 3)
    h = h * lax.rsqrt(jnp.mean(h * h, axis=-1, keepdims=True) + EPS)
    h = h.reshape(B, S, M_W) * hn_g.astype(f32)
    return (h + skip.astype(f32) * cu.astype(f32)).astype(u.dtype)

def swa_branch(q, k, v, sinks):
    B, S, _ = q.shape
    nb = S // WINDOW
    G = A_HEADS // A_KV
    qb = q.reshape(B, nb, WINDOW, A_KV, G, A_DH)
    kh = k.reshape(B, nb, WINDOW, A_KV, A_DH)
    vh = v.reshape(B, nb, WINDOW, A_KV, A_DH)
    pad = jnp.zeros_like(kh[:, :1])
    kk = jnp.concatenate([jnp.concatenate([pad, kh[:, :-1]], 1), kh], 2)
    vv = jnp.concatenate([jnp.concatenate([pad, vh[:, :-1]], 1), vh], 2)
    scores = jnp.einsum('bnqkgd,bnskd->bnkgqs', qb, kk).astype(jnp.float32) * (A_DH ** -0.5)
    qi = jnp.arange(WINDOW)[:, None]
    si = jnp.arange(2 * WINDOW)[None, :]
    rel = WINDOW + qi - si
    band = (rel >= 0) & (rel < WINDOW)
    valid = band[None] & ((jnp.arange(nb)[:, None, None] - 1) * WINDOW + si[None] >= 0)
    alibi = -alibi_slopes().reshape(A_KV, G)[:, :, None, None] * rel.astype(jnp.float32)
    scores = jnp.where(valid[None, :, None, None], scores + alibi[None, None], -jnp.inf)
    sink = jnp.broadcast_to(sinks.astype(jnp.float32).reshape(A_KV, G)[None, None, :, :, None, None],
                            scores.shape[:-1] + (1,))
    probs = jax.nn.softmax(jnp.concatenate([scores, sink], axis=-1), axis=-1)[..., :-1]
    out = jnp.einsum('bnkgqs,bnskd->bnqkgd', probs.astype(v.dtype), vv)
    return out.reshape(B, S, A_W)

def stickbreak_branch(q, k, v):
    B, S, _ = q.shape
    nb = S // S_BLOCK
    qh = q.reshape(B, nb, S_BLOCK, S_HEADS, S_DH).transpose(1, 0, 3, 2, 4)
    kh = k.reshape(B, S, S_HEADS, S_DH).transpose(0, 2, 1, 3)
    vh = v.reshape(B, S, S_HEADS, S_DH).transpose(0, 2, 1, 3)
    kpos = jnp.arange(S)

    def block(args):
        qb, n = args
        z = jnp.einsum('bhqd,bhsd->bhqs', qb, kh).astype(jnp.float32) * (S_DH ** -0.5)
        tpos = n * S_BLOCK + jnp.arange(S_BLOCK)
        strict = kpos[None, :] < tpos[:, None]
        log_keep = jnp.where(strict, jax.nn.log_sigmoid(-z), 0.0)
        suffix = lax.cumsum(log_keep, axis=log_keep.ndim - 1, reverse=True) - log_keep
        a = jnp.where(strict, jnp.exp(jax.nn.log_sigmoid(z) + suffix), 0.0)
        return jnp.einsum('bhqs,bhsd->bhqd', a.astype(vh.dtype), vh)

    out = lax.map(block, (qh, jnp.arange(nb)))
    return out.transpose(1, 0, 3, 2, 4).reshape(B, S, S_W)

def hybrid_layer(x, c_act, w_mod, b_mod, g_pre, g_post, w_in, m_conv_w, m_conv_b, m_wq, m_wk,
                 m_b_i, m_b_f, m_norm_g, m_skip, a_sinks, w_out):
    mod = c_act @ w_mod + b_mod
    shift, scale, gate = jnp.split(mod, 3, axis=-1)
    h = rmsnorm(x, g_pre) * (1.0 + scale[:, None]) + shift[:, None]
    proj = h @ w_in
    (mu, mv, mi, mf, mz, aq, ak, av, az, sq, sk, sv, sz) = jnp.split(proj, OFFSETS, axis=-1)
    y_m = mlstm_branch(mu, mv, mi, mf, m_conv_w, m_conv_b, m_wq, m_wk, m_b_i, m_b_f, m_norm_g, m_skip) * jax.nn.silu(mz)
    y_a = swa_branch(aq, ak, av, a_sinks) * jax.nn.silu(az)
    y_s = stickbreak_branch(sq, sk, sv) * jax.nn.silu(sz)
    y = jnp.concatenate([y_m, y_a, y_s], axis=-1) @ w_out
    return x + gate[:, None] * rmsnorm(y, g_post)

def first_inputs(seed: int = 0) -> dict:
    key = jax.random.key(seed)
    ks = jax.random.split(key, 20)
    nrm = jax.random.normal
    f32 = jnp.float32
    d = D_MODEL
    return {
        "x": nrm(ks[0], (BATCH, SEQ, d), f32),
        "c": nrm(ks[1], (BATCH, d), f32),
        "w_mod": nrm(ks[2], (DEPTH, d, 3 * d), f32) * (0.5 * d ** -0.5),
        "b_mod": nrm(ks[3], (DEPTH, 3 * d), f32) * 0.02,
        "g_pre": 1.0 + 0.05 * nrm(ks[4], (DEPTH, d), f32),
        "g_post": 1.0 + 0.05 * nrm(ks[5], (DEPTH, d), f32),
        "w_in": nrm(ks[6], (DEPTH, d, N_IN), f32) * d ** -0.5,
        "m_conv_w": nrm(ks[7], (DEPTH, M_CONV, M_W), f32) * M_CONV ** -0.5,
        "m_conv_b": nrm(ks[8], (DEPTH, M_W), f32) * 0.02,
        "m_wq": nrm(ks[9], (DEPTH, M_HEADS, M_DH, M_DH), f32) * M_DH ** -0.5,
        "m_wk": nrm(ks[10], (DEPTH, M_HEADS, M_DH, M_DH), f32) * M_DH ** -0.5,
        "m_b_i": nrm(ks[11], (DEPTH, M_HEADS), f32) * 0.1,
        "m_b_f": 3.0 + 0.5 * nrm(ks[12], (DEPTH, M_HEADS), f32),
        "m_norm_g": 1.0 + 0.05 * nrm(ks[13], (DEPTH, M_W), f32),
        "m_skip": 1.0 + 0.05 * nrm(ks[14], (DEPTH, M_W), f32),
        "a_sinks": nrm(ks[15], (DEPTH, A_HEADS), f32) * 0.5,
        "w_out": nrm(ks[16], (DEPTH, D_MIX, d), f32) * D_MIX ** -0.5,
    }

def first_block(x, c, w_mod, b_mod, g_pre, g_post, w_in, m_conv_w, m_conv_b, m_wq, m_wk,
              m_b_i, m_b_f, m_norm_g, m_skip, a_sinks, w_out):
    c_act = jax.nn.silu(c)
    for l in range(DEPTH):
        x = hybrid_layer(x, c_act, w_mod[l], b_mod[l], g_pre[l], g_post[l], w_in[l], m_conv_w[l], m_conv_b[l],
                         m_wq[l], m_wk[l], m_b_i[l], m_b_f[l], m_norm_g[l], m_skip[l], a_sinks[l], w_out[l])
    return x


DEPTH_2 = 2

N_EVEN = (DEPTH_2 + 1) // 2
N_ODD = DEPTH_2 // 2

NSA_HEADS = 8
HEAD_DIM = 64
KV_GROUPS = 2
HEADS_PER_GROUP = NSA_HEADS // KV_GROUPS
N_BRANCH = 3
CMP_BLOCK = 32
CMP_STRIDE = 16
CMP_HIDDEN = 128
SEL_BLOCK = 64
SEL_TOPK = 8
WINDOW_2 = 512
Q_BLOCK = 128
FORCE_BONUS = 1e4
NEG = -1e30

POOL_WIDTH = D_MODEL // 2
POOL_WINDOWS = (2, 4, 8, 16)
POOL_GROUPS = len(POOL_WINDOWS)
POOL_GROUP_DIM = POOL_WIDTH // POOL_GROUPS

NSA_WIDTH = NSA_HEADS * HEAD_DIM
KV_WIDTH = KV_GROUPS * HEAD_DIM
GATE_WIDTH = NSA_HEADS * N_BRANCH
IN_WIDTH = NSA_WIDTH + N_BRANCH * 2 * KV_WIDTH + GATE_WIDTH + POOL_WIDTH
MIX_WIDTH = NSA_WIDTH + POOL_WIDTH

CONV_WIDTH = 31

FFN_HIDDEN = -(-8 * D_MODEL // (3 * 256)) * 256


def rmsnorm_2(x, g, eps=1e-6):
    xf = x.astype(jnp.float32)
    y = xf * lax.rsqrt(jnp.mean(xf * xf, axis=-1, keepdims=True) + eps)
    return (y * g.astype(jnp.float32)).astype(x.dtype)

def layernorm(x, g, b, eps=1e-5):
    xf = x.astype(jnp.float32)
    mu = jnp.mean(xf, axis=-1, keepdims=True)
    xc = xf - mu
    var = jnp.mean(xc * xc, axis=-1, keepdims=True)
    y = xc * lax.rsqrt(var + eps) * g.astype(jnp.float32) + b.astype(jnp.float32)
    return y.astype(x.dtype)

def alibi_slopes_2():
    h = jnp.arange(1, NSA_HEADS + 1, dtype=jnp.float32)
    return jnp.exp2(-8.0 * h / NSA_HEADS).reshape(KV_GROUPS, HEADS_PER_GROUP)

def compress_blocks(kv, pos, w1, w2):
    b, g, s, dh = kv.shape
    r = CMP_BLOCK // CMP_STRIDE
    n_cmp = s // CMP_STRIDE - r + 1
    sub = kv.reshape(b, g, s // CMP_STRIDE, CMP_STRIDE, dh)
    blocks = jnp.concatenate([sub[:, :, j:j + n_cmp] for j in range(r)], axis=3)
    blocks = (blocks + pos).reshape(b, g, n_cmp, CMP_BLOCK * dh)
    return jax.nn.gelu(blocks @ w1) @ w2

def compressed_branch(q, kc, vc, slopes):
    s = q.shape[3]
    n_cmp = kc.shape[2]
    t = jnp.arange(s, dtype=jnp.int32)[:, None]
    end = jnp.arange(n_cmp, dtype=jnp.int32)[None, :] * CMP_STRIDE + (CMP_BLOCK - 1)
    dist = (t - end).astype(jnp.float32)
    valid = dist >= 0
    logits = jnp.einsum('bgrtd,bgnd->bgrtn', q, kc).astype(jnp.float32)
    logits = logits - slopes[:, :, None, None] * dist
    logits = jnp.where(valid, logits, NEG)
    p = jax.nn.softmax(logits, axis=-1) * valid
    o = jnp.einsum('bgrtn,bgnd->bgrtd', p.astype(vc.dtype), vc)
    return o, p

def selection_indices(p_cmp, s):
    n_cmp = p_cmp.shape[-1]
    n_sel = s // SEL_BLOCK
    c0 = np.arange(n_cmp)[:, None] * CMP_STRIDE
    s0 = np.arange(n_sel)[None, :] * SEL_BLOCK
    overlap = np.clip(np.minimum(c0 + CMP_BLOCK, s0 + SEL_BLOCK) - np.maximum(c0, s0), 0, None) / CMP_BLOCK
    imp = jnp.einsum('bgtn,nj->bgtj', p_cmp.sum(axis=2), jnp.asarray(overlap, jnp.float32))
    t_blk = (jnp.arange(s, dtype=jnp.int32) // SEL_BLOCK)[:, None]
    j = jnp.arange(n_sel, dtype=jnp.int32)[None, :]
    forced = (j == 0) | (j == t_blk) | (j == t_blk - 1)
    imp = jnp.where(forced, imp + FORCE_BONUS, imp)
    imp = jnp.where(j > t_blk, NEG, imp)
    _, idx = lax.top_k(imp, min(SEL_TOPK, n_sel))
    return idx

def selected_branch(q, ks, vs, idx, slopes):
    b, g, r, s, dh = q.shape
    k = idx.shape[-1]
    n_sel = s // SEL_BLOCK
    nq = s // Q_BLOCK
    kb = ks.reshape(b, g, n_sel, SEL_BLOCK, dh)
    vb = vs.reshape(b, g, n_sel, SEL_BLOCK, dh)
    qc = jnp.moveaxis(q.reshape(b, g, r, nq, Q_BLOCK, dh), 3, 0)
    ic = jnp.moveaxis(idx.reshape(b, g, nq, Q_BLOCK, k), 2, 0)
    tc = jnp.arange(s, dtype=jnp.int32).reshape(nq, Q_BLOCK)
    bi = jnp.arange(b)[:, None, None, None]
    gi = jnp.arange(g)[None, :, None, None]
    offs = jnp.arange(SEL_BLOCK, dtype=jnp.int32)

    def one_block(args):
        qq, ii, tt = args
        k_sel = kb[bi, gi, ii].reshape(b, g, Q_BLOCK, k * SEL_BLOCK, dh)
        v_sel = vb[bi, gi, ii].reshape(b, g, Q_BLOCK, k * SEL_BLOCK, dh)
        pos = (ii[..., None] * SEL_BLOCK + offs).reshape(b, g, Q_BLOCK, k * SEL_BLOCK)
        dist = (tt[None, None, :, None] - pos).astype(jnp.float32)[:, :, None]
        logits = jnp.einsum('bgrqd,bgqkd->bgrqk', qq, k_sel).astype(jnp.float32)
        logits = logits - slopes[None, :, :, None, None] * dist
        logits = jnp.where(dist >= 0, logits, NEG)
        p = jax.nn.softmax(logits, axis=-1)
        return jnp.einsum('bgrqk,bgqkd->bgrqd', p.astype(v_sel.dtype), v_sel)

    o = lax.map(one_block, (qc, ic, tc))
    return jnp.moveaxis(o, 0, 3).reshape(b, g, r, s, dh)

def window_branch(q, kw, vw, slopes):
    b, g, r, s, dh = q.shape
    nq = s // Q_BLOCK
    nw = WINDOW_2 // Q_BLOCK
    pad = ((0, 0), (0, 0), (WINDOW_2, 0), (0, 0))
    kp = jnp.pad(kw, pad).reshape(b, g, nq + nw, Q_BLOCK, dh)
    vp = jnp.pad(vw, pad).reshape(b, g, nq + nw, Q_BLOCK, dh)
    k_band = jnp.concatenate([kp[:, :, j:j + nq] for j in range(nw + 1)], axis=3)
    v_band = jnp.concatenate([vp[:, :, j:j + nq] for j in range(nw + 1)], axis=3)
    qb = q.reshape(b, g, r, nq, Q_BLOCK, dh)
    t = jnp.arange(s, dtype=jnp.int32).reshape(nq, Q_BLOCK)
    kpos = (jnp.arange(nq, dtype=jnp.int32)[:, None] - nw) * Q_BLOCK + jnp.arange((nw + 1) * Q_BLOCK, dtype=jnp.int32)[None, :]
    dist = t[:, :, None] - kpos[:, None, :]
    valid = (dist >= 0) & (dist < WINDOW_2) & (kpos[:, None, :] >= 0)
    logits = jnp.einsum('bgrnqd,bgnkd->bgrnqk', qb, k_band).astype(jnp.float32)
    logits = logits - slopes[:, :, None, None, None] * dist.astype(jnp.float32)
    logits = jnp.where(valid, logits, NEG)
    p = jax.nn.softmax(logits, axis=-1)
    o = jnp.einsum('bgrnqk,bgnkd->bgrnqd', p.astype(v_band.dtype), v_band)
    return o.reshape(b, g, r, s, dh)

def multiscale_pool(u, w_pool, scale):
    b, s, c = u.shape
    uf = u.astype(jnp.float32)
    cs = jnp.pad(jnp.cumsum(uf, axis=1), ((0, 0), (1, 0), (0, 0)))
    t = jnp.arange(s, dtype=jnp.float32)
    outs = []
    for gi, w in enumerate(POOL_WINDOWS):
        sl = slice(gi * POOL_GROUP_DIM, (gi + 1) * POOL_GROUP_DIM)
        csg = cs[:, :, sl]
        start = jnp.pad(csg, ((0, 0), (w - 1, 0), (0, 0)))[:, :s]
        mean = (csg[:, 1:] - start) / jnp.minimum(t + 1.0, float(w))[None, :, None]
        outs.append(mean - uf[:, :, sl])
    d = jnp.stack(outs, axis=2).astype(u.dtype)
    y = jnp.einsum('bsgc,gce->bsge', d, w_pool).reshape(b, s, c)
    return y * scale

def nsa_pool_mixer(h, w_in, pos_k, pos_v, k_w1, k_w2, v_w1, v_w2, w_pool, pool_scale, w_out):
    b, s, _ = h.shape
    proj = h @ w_in
    sizes = [NSA_WIDTH] + [KV_WIDTH] * (2 * N_BRANCH) + [GATE_WIDTH]
    cuts = [int(c) for c in np.cumsum(sizes)]
    q, kc, vc, ks, vs, kw, vw, gate, u = jnp.split(proj, cuts, axis=-1)

    def kv_heads(z):
        return z.reshape(b, s, KV_GROUPS, HEAD_DIM).transpose(0, 2, 1, 3)

    q = q.reshape(b, s, KV_GROUPS, HEADS_PER_GROUP, HEAD_DIM).transpose(0, 2, 3, 1, 4) * (HEAD_DIM ** -0.5)
    slopes = alibi_slopes_2()

    kcmp = compress_blocks(kv_heads(kc), pos_k, k_w1, k_w2)
    vcmp = compress_blocks(kv_heads(vc), pos_v, v_w1, v_w2)
    o_cmp, p_cmp = compressed_branch(q, kcmp, vcmp, slopes)
    idx = selection_indices(p_cmp, s)
    o_sel = selected_branch(q, kv_heads(ks), kv_heads(vs), idx, slopes)
    o_win = window_branch(q, kv_heads(kw), kv_heads(vw), slopes)

    g = jax.nn.sigmoid(gate.reshape(b, s, KV_GROUPS, HEADS_PER_GROUP, N_BRANCH)).transpose(0, 2, 3, 1, 4)
    o = g[..., 0:1] * o_cmp + g[..., 1:2] * o_sel + g[..., 2:3] * o_win
    o = o.transpose(0, 3, 1, 2, 4).reshape(b, s, NSA_WIDTH)
    y_pool = multiscale_pool(u, w_pool, pool_scale)
    return jnp.concatenate([o, y_pool], axis=-1) @ w_out

def conformer_conv(h, w_pw1, b_pw1, w_dw, b_dw, ln_g, ln_b, w_pw2, b_pw2):
    a, gt = jnp.split(h @ w_pw1 + b_pw1, 2, axis=-1)
    z = a * jax.nn.sigmoid(gt)
    z = lax.conv_general_dilated(
        z, w_dw[:, None, :], window_strides=(1,), padding=[(CONV_WIDTH - 1, 0)],
        dimension_numbers=('NWC', 'WIO', 'NWC'), feature_group_count=D_MODEL) + b_dw
    z = jax.nn.silu(layernorm(z, ln_g, ln_b))
    return z @ w_pw2 + b_pw2

def swiglu(h, w_gate, w_up, w_down):
    return (jax.nn.silu(h @ w_gate) * (h @ w_up)) @ w_down

def second_inputs(seed: int = 0) -> dict:
    key = jax.random.key(seed)
    keys = iter(jax.random.split(key, 32))

    def nrm(shape, scale):
        return jax.random.normal(next(keys), shape, jnp.float32) * scale

    def gain(shape):
        return 1.0 + nrm(shape, 0.05)

    dh = HEAD_DIM
    return {
        "x": nrm((BATCH, SEQ, D_MODEL), 1.0),
        "mix_norm": gain((DEPTH_2, D_MODEL)),
        "ffn_norm": gain((DEPTH_2, D_MODEL)),
        "nsa_w_in": nrm((N_EVEN, D_MODEL, IN_WIDTH), D_MODEL ** -0.5),
        "cmp_pos_k": nrm((N_EVEN, CMP_BLOCK, dh), 0.1),
        "cmp_pos_v": nrm((N_EVEN, CMP_BLOCK, dh), 0.1),
        "cmp_k_w1": nrm((N_EVEN, CMP_BLOCK * dh, CMP_HIDDEN), (CMP_BLOCK * dh) ** -0.5),
        "cmp_k_w2": nrm((N_EVEN, CMP_HIDDEN, dh), CMP_HIDDEN ** -0.5),
        "cmp_v_w1": nrm((N_EVEN, CMP_BLOCK * dh, CMP_HIDDEN), (CMP_BLOCK * dh) ** -0.5),
        "cmp_v_w2": nrm((N_EVEN, CMP_HIDDEN, dh), CMP_HIDDEN ** -0.5),
        "pool_w": nrm((N_EVEN, POOL_GROUPS, POOL_GROUP_DIM, POOL_GROUP_DIM), POOL_GROUP_DIM ** -0.5),
        "pool_scale": gain((N_EVEN, POOL_WIDTH)),
        "mix_w_out": nrm((N_EVEN, MIX_WIDTH, D_MODEL), MIX_WIDTH ** -0.5),
        "conv_w_pw1": nrm((N_ODD, D_MODEL, 2 * D_MODEL), D_MODEL ** -0.5),
        "conv_b_pw1": nrm((N_ODD, 2 * D_MODEL), 0.02),
        "conv_w_dw": nrm((N_ODD, CONV_WIDTH, D_MODEL), CONV_WIDTH ** -0.5),
        "conv_b_dw": nrm((N_ODD, D_MODEL), 0.02),
        "conv_ln_g": gain((N_ODD, D_MODEL)),
        "conv_ln_b": nrm((N_ODD, D_MODEL), 0.02),
        "conv_w_pw2": nrm((N_ODD, D_MODEL, D_MODEL), D_MODEL ** -0.5),
        "conv_b_pw2": nrm((N_ODD, D_MODEL), 0.02),
        "ffn_w_gate": nrm((DEPTH_2, D_MODEL, FFN_HIDDEN), D_MODEL ** -0.5),
        "ffn_w_up": nrm((DEPTH_2, D_MODEL, FFN_HIDDEN), D_MODEL ** -0.5),
        "ffn_w_down": nrm((DEPTH_2, FFN_HIDDEN, D_MODEL), FFN_HIDDEN ** -0.5),
        "final_norm": gain((D_MODEL,)),
    }

def second_block(x, mix_norm, ffn_norm, nsa_w_in, cmp_pos_k, cmp_pos_v, cmp_k_w1, cmp_k_w2,
              cmp_v_w1, cmp_v_w2, pool_w, pool_scale, mix_w_out, conv_w_pw1, conv_b_pw1,
              conv_w_dw, conv_b_dw, conv_ln_g, conv_ln_b, conv_w_pw2, conv_b_pw2,
              ffn_w_gate, ffn_w_up, ffn_w_down, final_norm):
    for layer in range(DEPTH_2):
        h = rmsnorm_2(x, mix_norm[layer])
        i = layer // 2
        if layer % 2 == 0:
            x = x + nsa_pool_mixer(h, nsa_w_in[i], cmp_pos_k[i], cmp_pos_v[i], cmp_k_w1[i], cmp_k_w2[i],
                                   cmp_v_w1[i], cmp_v_w2[i], pool_w[i], pool_scale[i], mix_w_out[i])
        else:
            x = x + conformer_conv(h, conv_w_pw1[i], conv_b_pw1[i], conv_w_dw[i], conv_b_dw[i],
                                   conv_ln_g[i], conv_ln_b[i], conv_w_pw2[i], conv_b_pw2[i])
        h = rmsnorm_2(x, ffn_norm[layer])
        x = x + swiglu(h, ffn_w_gate[layer], ffn_w_up[layer], ffn_w_down[layer])
    return rmsnorm_2(x, final_norm)


def setup_inputs(seed=0):
    out = dict(first_inputs(seed))
    for name, value in second_inputs(seed + 1).items():
        if name != "x":
            out[name + "_2"] = value
    return out


def reference(
    x, c, w_mod, b_mod, g_pre, g_post, w_in, m_conv_w, m_conv_b, m_wq, m_wk, m_b_i, m_b_f,
    m_norm_g, m_skip, a_sinks, w_out, mix_norm_2, ffn_norm_2, nsa_w_in_2, cmp_pos_k_2,
    cmp_pos_v_2, cmp_k_w1_2, cmp_k_w2_2, cmp_v_w1_2, cmp_v_w2_2, pool_w_2, pool_scale_2,
    mix_w_out_2, conv_w_pw1_2, conv_b_pw1_2, conv_w_dw_2, conv_b_dw_2, conv_ln_g_2, conv_ln_b_2,
    conv_w_pw2_2, conv_b_pw2_2, ffn_w_gate_2, ffn_w_up_2, ffn_w_down_2, final_norm_2,
):
    x = first_block(
        x, c, w_mod, b_mod, g_pre, g_post, w_in, m_conv_w, m_conv_b, m_wq, m_wk, m_b_i, m_b_f,
        m_norm_g, m_skip, a_sinks, w_out,
    )
    return second_block(
        x, mix_norm_2, ffn_norm_2, nsa_w_in_2, cmp_pos_k_2, cmp_pos_v_2, cmp_k_w1_2, cmp_k_w2_2,
        cmp_v_w1_2, cmp_v_w2_2, pool_w_2, pool_scale_2, mix_w_out_2, conv_w_pw1_2, conv_b_pw1_2,
        conv_w_dw_2, conv_b_dw_2, conv_ln_g_2, conv_ln_b_2, conv_w_pw2_2, conv_b_pw2_2,
        ffn_w_gate_2, ffn_w_up_2, ffn_w_down_2, final_norm_2,
    )


_drawn_inputs = setup_inputs


def setup_inputs(seed=0):
    import zlib

    import numpy as np

    out = dict(_drawn_inputs(seed))
    spreads = {}
    factors = {'g_post': 2.948,
     'm_conv_b': 6.396,
     'm_b_i': 64.0,
     'm_norm_g': 4.623,
     'm_skip': 7.615,
     'a_sinks': 43.937,
     'cmp_pos_k_2': 29.645,
     'conv_b_pw1_2': 6.078,
     'conv_b_dw_2': 3.332,
     'conv_ln_b_2': 6.388,
     'conv_b_pw2_2': 3.951,
     'cmp_pos_v_2': 3.131}
    for name, (base, spread) in spreads.items():
        noise = np.random.default_rng([zlib.crc32(name.encode()), seed]).standard_normal(out[name].shape)
        drawn = base * np.exp(spread * noise) if base else spread * noise
        out[name] = __import__('jax').numpy.asarray(drawn.astype(out[name].dtype))
    for name, factor in factors.items():
        out[name] = (out[name] * factor).astype(out[name].dtype)
    return out
```

```python
import concourse.bass as bass
from concourse import mybir
from contextlib import ExitStack

F32 = mybir.dt.float32
ALU = mybir.AluOpType
ACT = mybir.ActivationFunctionType
AX = mybir.AxisListType

P = 128
S = 1024
D = 1024
KC = D // P
TB = S // P
EPS = 1e-6
LN_EPS = 1e-5
NEG = -1e30
BIGF = 3e38

M_H, M_D, M_CONV = 4, 96, 4
M_W = M_H * M_D
A_H, A_D, A_W, A_KVW = 6, 64, 384, 128
S_H, S_D, S_W = 4, 64, 256
C_MU, C_MVG, C_MZ = 0, M_W, 2 * M_W + 2 * M_H
C_AQ = C_MZ + M_W
C_AK = C_AQ + A_W
C_AZ = C_AK + 2 * A_KVW
C_SQ = C_AZ + A_W
C_SK, C_SV, C_SZ = C_SQ + S_W, C_SQ + 2 * S_W, C_SQ + 3 * S_W
VGW = M_W + 2 * M_H

N_H, N_G, N_D = 8, 2, 64
N_CMP = 63
FF = 2816
FC = FF // P
CONV_W = 31
SLOT = KC * VGW

(V_C, V_BMOD, V_GPRE, V_GPOST, V_MIX, V_FFN, V_BPW1, V_BDW, V_LNG, V_LNB, V_BPW2) = (
    0, 8, 32, 40, 48, 64, 80, 96, 104, 112, 120)
V_WDW, V_FINAL = 128, 376
V_CW, V_CB, V_NG, V_SKIP, V_PS = 384, 400, 404, 408, 412
V_POS = 416
N_COLS = 480


class Signals:
    pass


class Unit:
    pass


def build(nc, x, c, w_mod, b_mod, g_pre, g_post, w_in, m_conv_w, m_conv_b, m_wq, m_wk, m_b_i, m_b_f,
          m_norm_g, m_skip, a_sinks, w_out, mix_norm_2, ffn_norm_2, nsa_w_in_2, cmp_pos_k_2,
          cmp_pos_v_2, cmp_k_w1_2, cmp_k_w2_2, cmp_v_w1_2, cmp_v_w2_2, pool_w_2, pool_scale_2,
          mix_w_out_2, conv_w_pw1_2, conv_b_pw1_2, conv_w_dw_2, conv_b_dw_2, conv_ln_g_2,
          conv_ln_b_2, conv_w_pw2_2, conv_b_pw2_2, ffn_w_gate_2, ffn_w_up_2, ffn_w_down_2,
          final_norm_2, out):
    with ExitStack() as ctx:
        def sb(name, shape):
            return ctx.enter_context(nc.sbuf_tensor(name, shape, F32))

        def sem(name):
            return ctx.enter_context(nc.semaphore(name))

        xt = sb("xt", [P, KC, S])
        ht = sb("ht", [P, KC, S])
        big = sb("big", [P, FC * S])
        ring = sb("ring", [P, 2, SLOT])
        sc = sb("sc", [P, 4, S])
        cols = sb("cols", [P, N_COLS])
        ident = sb("ident", [P, P])
        ones = sb("ones", [P, P])
        dists = sb("dists", [P, S + 640])
        swa_bias = dists[:, 0:256 * A_H]
        causal = dists[:, 0:S]
        band = dists[:, S:S + 640]
        tri = sb("tri", [P, P])
        stat = sb("stat", [P, 16, 4])
        misc = sb("misc", [P, 256])
        ps = ctx.enter_context(nc.psum_tensor("ps", [P, 4096], F32))

        def bank(b, n=1):
            return ps[:, 512 * b:512 * (b + n)]

        def part(a, shape=None, parts=P):
            n = 1
            for s_ in shape:
                n *= s_
            v = big[0:parts, a:a + n]
            if len(shape) == 2:
                return v.rearrange("p (a b) -> p a b", a=shape[0])
            if len(shape) == 3:
                return v.rearrange("p (a b c) -> p a b c", a=shape[0], b=shape[1])
            return v

        az = part(0, (3, S))
        sz = part(3072, (2, S))
        aq = part(5120, (3, S))
        ak = part(8192, (S,))
        av = part(9216, (TB, P))
        sq = part(10240, (2, S))
        sk = part(12288, (2, S))
        sv = part(14336, (TB, S_W))
        ao = part(16384, (TB, A_W))
        so = part(19456, (TB, S_W))
        cu = part(5120, (M_H, S), M_D)
        mz = part(9216, (M_H, S), M_D)
        mu = part(13312, (M_H, S + 3), M_D)
        mq = part(13312, (M_H, S), M_D)
        mv = part(17420, (TB, M_H, M_D + 1))
        gi = part(20524, (TB, 8))
        ct = part(20588, (M_H, M_D + 1), M_D)
        intra = part(20976, (M_H, M_D + 1))
        selr = part(21364, (M_H, P), 4)
        car = part(21876, (M_H, TB))
        mrow = part(21908, (3, TB), 4)
        mst = part(21932, (4, TB, M_H))
        mkt = ht[0:M_D, 0:4, :]
        mk = ht[:, 4:7, :].rearrange("p a b -> p (a b)").rearrange("p (t h d) -> p t h d", t=TB, h=M_H)
        nq = part(0, (4, S))
        kc_t = part(4096, (S,))
        vc_t = part(5120, (S,))
        ks = part(6144, (S,))
        kw = part(7168, (S,))
        vs = part(8192, (TB, P))
        vw = part(9216, (TB, P))
        u = part(10240, (4, S + 16))
        no = part(14400, (TB, 512))
        tg = part(18496, (2, S))
        ng = part(20544, (TB, 24))
        kcmp = part(20736, (N_CMP + 1,))
        vcmp = part(20800, (N_G, N_D), N_CMP)
        hid = part(20928, (2, N_CMP + 1))
        hbias = part(21056, (2,))
        cdist = part(21060, (TB, N_CMP))
        force = part(21568, (TB, 16))
        imp = part(21696, (16 * 6,))
        psum_p = part(21792, (2, 68))
        w2s = misc[:, 64:192].rearrange("p (w d) -> p w d", w=2)
        pw_rc = part(22064, (16,))
        act = part(0, (FC, S))
        zp = part(0, (KC, S + CONV_W - 1))
        zc = part(8432, (KC, S))
        sg = part(16624, (S,))
        ptmp = part(17648, (S,))

        s = Signals()
        s.w_used = sem("w_used")
        s.par_in = sem("par_in")
        s.x_in = sem("x_in")
        s.small_in = sem("small_in")
        s.const_ok = sem("const_ok")
        s.stage_end = sem("stage_end")
        s.tr_done = sem("tr_done")
        s.tr_free = sem("tr_free")
        s.cols_ok = sem("cols_ok")
        s.c_act = sem("c_act")
        s.mod_done = sem("mod_done")
        s.sq_ready = sem("sq_ready")
        s.sq_used = sem("sq_used")
        s.rs_ready = sem("rs_ready")
        s.h_mul = sem("h_mul")
        s.g_out = sem("g_out")
        s.dve_chain = sem("dve_chain")
        s.act_chain = sem("act_chain")
        s.pool_chain = sem("pool_chain")
        s.gate_out = sem("gate_out")
        s.gate_free = sem("gate_free")
        s.up_out = sem("up_out")
        s.up_free = sem("up_free")
        s.down_out = sem("down_out")
        s.down_free = sem("down_free")
        s.s_done = sem("s_done")
        s.l_done = sem("l_done")
        s.e_done = sem("e_done")
        s.pt_done = sem("pt_done")
        s.pt_copied = sem("pt_copied")
        s.pv_done = sem("pv_done")
        s.o_done = sem("o_done")
        s.z_ln = sem("z_ln")
        s.z_sp = sem("z_sp")
        s.z_spm = sem("z_spm")
        s.x_exp = sem("x_exp")
        s.turn_done = sem("turn_done")
        s.turn_copied = sem("turn_copied")
        s.gates_up = sem("gates_up")
        s.rows_a = sem("rows_a")
        s.rows_b = sem("rows_b")
        s.rows_c = sem("rows_c")
        s.rows_d = sem("rows_d")
        s.rowcols = sem("rowcols")
        s.conv_done = sem("conv_done")
        s.qk_done = sem("qk_done")
        s.qk_copied = sem("qk_copied")
        s.ktok_done = sem("ktok_done")
        s.ktok_copied = sem("ktok_copied")
        s.ms_done = sem("ms_done")
        s.md_done = sem("md_done")
        s.mexp_done = sem("mexp_done")
        s.ms_weighted = sem("ms_weighted")
        s.mo_done = sem("mo_done")
        s.mintra = sem("mintra")
        s.mstate = sem("mstate")
        s.ms_sum = sem("ms_sum")
        s.ms_root = sem("ms_root")
        s.ht_ready = sem("ht_ready")
        s.ht_done = sem("ht_done")
        s.ht_copied = sem("ht_copied")
        s.cmp_h1 = sem("cmp_h1")
        s.cmp_bias = sem("cmp_bias")
        s.cmp_hid = sem("cmp_hid")
        s.cmp_h2 = sem("cmp_h2")
        s.cmp_copied = sem("cmp_copied")
        s.pool_d = sem("pool_d")
        s.pool_mm = sem("pool_mm")
        s.pool_copied = sem("pool_copied")
        s.mean_done = sem("mean_done")
        s.mean_copied = sem("mean_copied")
        s.xc_done = sem("xc_done")
        s.ft_done = sem("ft_done")
        s.out_ready = sem("out_ready")
        w_ready = [sem("w_ready0"), sem("w_ready1")]
        g_free = [sem("g_free0"), sem("g_free1")]
        out_done = [sem("out_done0"), sem("out_done1")]

        tiles = [1] * 8
        T_IN = len(tiles)
        tiles += [6, 1, 1, 1, 1, 1, 1, 1, 1, 1]
        T_QK = len(tiles)
        tiles += [2]
        T_OUT = len(tiles)
        tiles += [2] * 4
        T_NIN = len(tiles)
        tiles += [4, 4, 1, 1, 1, 1, 1]
        T_CMP = len(tiles)
        tiles += [2] * 4
        T_POOL = len(tiles)
        tiles += [1]
        T_MIX = len(tiles)
        tiles += [1] * 4
        T_F = []
        T_D = []
        T_F.append(len(tiles)); tiles += [1] * 22
        T_D.append(len(tiles)); tiles += [1] * 8
        T_PW1 = len(tiles)
        tiles += [1] * 8
        T_PW2 = len(tiles)
        tiles += [1] * 4
        T_F.append(len(tiles)); tiles += [1] * 22
        T_D.append(len(tiles)); tiles += [1] * 8
        arrives = [16 * sum(tiles[t % 2:t + 1:2]) for t in range(len(tiles))]

        def slot(t, parts=P):
            return ring[0:parts, t % 2, :]

        def tile_of(t, k, n):
            return slot(t)[:, 0:k * n].rearrange("p (k n) -> p k n", k=k)

        win_v = w_in[0].rearrange("(k p) n -> p k n", p=P)
        nin_v = nsa_w_in_2[0].rearrange("(k p) n -> p k n", p=P)

        STAGES = ("loaded normed_1 attention_in attended turned mlstm_in mlstm_rows mlstm_qk mlstm_scanned mlstm_out "
                  "y_1 x_1 normed_2 mixer_in compressed mixer_attended mixer_turned x_2 normed_3 ffn_act_1 x_3 "
                  "normed_4 convolved conv_normed x_4 normed_5 ffn_act_2 x_5 normed_6").split()
        def stage(eng, name):
            eng.drain().then_inc(s.stage_end, 1)
            eng.wait_ge(s.stage_end, 4 * (STAGES.index(name) + 1))

        J_IN = 0
        J_IN2 = J_IN + 3 + 1 + 1 + 3 + 2 + 2 + 2 + 2
        J_OUT = J_IN2 + 4 + 4 + 4
        J_NIN = J_OUT + 8
        J_MIX = J_NIN + 4 + 2 + 2 + 2 + 3 + 2
        J_PW2 = J_MIX + 8

        def a_slope(h):
            return 2.0 ** (-8.0 * (h + 1) / A_H)

        def n_slope(h):
            return 2.0 ** (-(h + 1))

        def unit(kind, i, h, q, k, w, v, out_, dist=None, slope=1.0, sink=None, gate=None, g=0, first=True):
            un = Unit()
            un.kind, un.i, un.h, un.q, un.k, un.w, un.v, un.out = kind, i, h, q, k, w, v, out_
            un.dist, un.slope, un.sink, un.gate, un.g, un.first = dist, slope, sink, gate, g, first
            return un

        def rows_of(half):
            return slice(64 * half, 64 * half + 64)

        swa_units, stick_units, nsa_units = [], [], []
        for i in range(TB):
            for h in range(A_H):
                half, c_ = h // 3, h % 3
                b0 = max(0, i - 1)
                w = P * (i + 1 - b0)
                swa_units.append(unit(
                    "swa", i, h, aq[rows_of(half), c_, P * i:P * i + P], ak[rows_of(half), P * b0:P * b0 + w], w,
                    lambda b, b0=b0, half=half: av[:, b0 + b, 64 * half:64 * half + 64],
                    ao[:, i, 64 * h:64 * h + 64], swa_bias[:, 256 * h + 256 - w:256 * h + 256], 1.0, sink=True))
            for h in range(S_H):
                half, c_ = h % 2, h // 2
                w = P * (i + 1)
                stick_units.append(unit(
                    "stick", i, h, sq[rows_of(half), c_, P * i:P * i + P], sk[rows_of(half), c_, 0:w], w,
                    lambda b, h=h: sv[:, b, 64 * h:64 * h + 64], so[:, i, 64 * h:64 * h + 64]))
            for kind in ("cmp", "win", "sel"):
                for h in range(N_H):
                    g, c_ = h // 4, h % 4
                    cols_ = slice(64 * g, 64 * g + 64)
                    q = nq[rows_of(g), c_, P * i:P * i + P]
                    branch = ("cmp", "sel", "win").index(kind)
                    args = dict(slope=n_slope(h), gate=ng[:, i, 3 * h + branch:3 * h + branch + 1], g=g,
                                first=kind == "cmp")
                    o = no[:, i, 64 * h:64 * h + 64]
                    if kind == "cmp":
                        un = unit(kind, i, h, q, kcmp[rows_of(g), 0:N_CMP], N_CMP,
                                  lambda b, g=g: vcmp[:, g, :], o, cdist[:, i, :], **args)
                    elif kind == "win":
                        b0 = max(0, i - 4)
                        w = P * (i + 1 - b0)
                        un = unit(kind, i, h, q, kw[rows_of(g), P * b0:P * b0 + w], w,
                                  lambda b, b0=b0, cols_=cols_: vw[:, b0 + b, cols_], o, band[:, 640 - w:640], **args)
                    else:
                        w = P * (i + 1)
                        un = unit(kind, i, h, q, ks[rows_of(g), 0:w], w,
                                  lambda b, cols_=cols_: vs[:, b, cols_], o, tg[:, g, 0:w], **args)
                    nsa_units.append(un)
        N_SWA = len(swa_units)
        N_FIRST = N_SWA + len(stick_units)
        TURNS = [(ao, c_, half) for c_ in range(3) for half in range(2)]
        TURNS += [(so, c_, half) for c_ in range(2) for half in range(2)]
        N_PAR = 23
        N_F, N_PW = (0, FC + KC), FC
        POOL_CONV = (0, 3)
        H_LN = 4 * KC

        def stick_weights(g, i):
            un, n = stick_units[i], N_SWA + i
            g.wait_ge(s.x_exp, i + 1)
            g.affine_select(out=sc[:, n % 2, un.w - P:un.w], in_=sc[:, n % 2, un.w - P:un.w], pattern=[[-1, P]],
                            compare_op=ALU.is_gt, fill=0.0, base=0, channel_multiplier=1).then_inc(s.e_done, 1)

        block = ctx.enter_context(nc.Block())

        @block.sync
        def _(sp):
            def load(dst, src, arrived):
                sp.dma_start(dst, src).then_inc(arrived, 16)

            def rows(v, n, w=P):
                return v.rearrange("(a b) -> a b", b=w)
            pr = sc[:, 0:1, :].rearrange("p a b -> p (a b)")
            r0, r1, r2, r3, r4 = (pr[:, P * i:P * i + P] for i in range(5))
            load(r0[V_C:V_C + 8, :], c[0].rearrange("(a b) -> a b", b=P), s.par_in)
            load(r0[V_BMOD:V_BMOD + 24, :], b_mod[0].rearrange("(a b) -> a b", b=P), s.par_in)
            load(r0[V_GPRE:V_GPRE + 8, :], g_pre[0].rearrange("(a b) -> a b", b=P), s.par_in)
            load(r0[V_GPOST:V_GPOST + 8, :], g_post[0].rearrange("(a b) -> a b", b=P), s.par_in)
            load(r0[V_MIX:V_MIX + 16, :], mix_norm_2.rearrange("l (a b) -> (l a) b", b=P), s.par_in)
            load(r0[V_FFN:V_FFN + 16, :], ffn_norm_2.rearrange("l (a b) -> (l a) b", b=P), s.par_in)
            load(r0[V_BPW1:V_BPW1 + 16, :], conv_b_pw1_2[0].rearrange("(a b) -> a b", b=P), s.par_in)
            load(r0[V_BDW:V_BDW + 8, :], conv_b_dw_2[0].rearrange("(a b) -> a b", b=P), s.par_in)
            load(r0[V_LNG:V_LNG + 8, :], conv_ln_g_2[0].rearrange("(a b) -> a b", b=P), s.par_in)
            load(r0[V_LNB:V_LNB + 8, :], conv_ln_b_2[0].rearrange("(a b) -> a b", b=P), s.par_in)
            load(r0[V_BPW2:V_BPW2 + 8, :], conv_b_pw2_2[0].rearrange("(a b) -> a b", b=P), s.par_in)
            wdw = conv_w_dw_2[0].rearrange("t (a b) -> (t a) b", b=P)
            load(r1, wdw[0:P, :], s.par_in)
            load(r2[0:120, :], wdw[P:248, :], s.par_in)
            load(r2[120:128, :], final_norm_2.rearrange("(a b) -> a b", b=P), s.par_in)
            sp.wait_ge(s.const_ok, 1)
            load(r3[0:16, 0:96], m_conv_w[0].rearrange("t (a b) -> (t a) b", b=96), s.par_in)
            load(r3[16:20, 0:96], m_conv_b[0].rearrange("(a b) -> a b", b=96), s.par_in)
            load(r3[20:24, 0:96], m_norm_g[0].rearrange("(a b) -> a b", b=96), s.par_in)
            load(r3[24:28, 0:96], m_skip[0].rearrange("(a b) -> a b", b=96), s.par_in)
            load(r3[28:32, :], pool_scale_2[0].rearrange("(a b) -> a b", b=P), s.par_in)
            for i, pos in enumerate((cmp_pos_k_2, cmp_pos_v_2)):
                for half in range(2):
                    load(r4[32 * i:32 * i + 32, 64 * half:64 * half + 64], pos[0], s.par_in)
            load(misc[0:4, 0:1], m_b_i[0].rearrange("(h o) -> h o", o=1), s.small_in)
            load(misc[0:4, 1:2], m_b_f[0].rearrange("(h o) -> h o", o=1), s.small_in)
            load(misc[:, 2:8], a_sinks[0:1, :].to_broadcast([P, A_H]), s.small_in)
            load(w2s[:, 0, :], cmp_k_w2_2[0], s.small_in)
            load(w2s[:, 1, :], cmp_v_w2_2[0], s.small_in)
            for half in range(2):
                load(big[:, 4096 * half:4096 * half + 4096].rearrange("p (t d) -> p t d", d=D),
                     x[0].rearrange("(t p) d -> p t d", p=P)[:, 4 * half:4 * half + 4, :], s.x_in)

            def tile(t, *pairs):
                if t >= 2:
                    sp.wait_ge(s.w_used, t - 1)
                for dst, src in pairs:
                    load(dst, src, w_ready[t % 2])

            for k in range(8):
                tile(k, (slot(k)[:, 0:3 * D], w_mod[0][k * P:(k + 1) * P, :]))
            t = T_IN
            aqt = tile_of(t, KC, A_W).rearrange("p k (r two d) -> p k r two d", two=2, d=A_D)
            if t >= 2:
                sp.wait_ge(s.w_used, t - 1)
            aqs = win_v[:, :, C_AQ:C_AQ + A_W].rearrange("p k (two r d) -> p k r two d", two=2, d=A_D)
            for two in range(2):
                for r_ in range(3):
                    load(aqt[:, :, r_, two, :], aqs[:, :, r_, two, :], w_ready[t % 2])
            for i, (c0, n) in enumerate([(C_AK, 256), (C_AZ, A_W), (C_SQ, S_W), (C_SK, S_W), (C_SV, S_W),
                                         (C_SZ, S_W), (C_MU, M_W), (C_MVG, VGW), (C_MZ, M_W)]):
                t = T_IN + 1 + i
                tile(t, (tile_of(t, KC, n), win_v[:, :, c0:c0 + n]))
            t = T_QK
            qk = slot(t, M_D)[:, 0:768].rearrange("p (w h e) -> p w h e", w=2, h=M_H)
            tile(t, (qk[:, 0], m_wq[0].rearrange("h d e -> d h e")), (qk[:, 1], m_wk[0].rearrange("h d e -> d h e")))
            for i in range(4):
                t = T_OUT + i
                tile(t, (slot(t, M_D)[:, 0:1024].rearrange("p (k n) -> p k n", k=4),
                         w_out[0][0:M_W, 256 * i:256 * i + 256].rearrange("(k p) n -> p k n", p=M_D)),
                     (slot(t)[:, 1024:2304].rearrange("p (k n) -> p k n", k=5),
                      w_out[0][M_W:D, 256 * i:256 * i + 256].rearrange("(k p) n -> p k n", p=P)))
            for i in range(2):
                t = T_NIN + i
                qt = tile_of(t, KC, 256).rearrange("p k (r two d) -> p k r two d", two=2, d=N_D)
                sp.wait_ge(s.w_used, t - 1)
                for two in range(2):
                    for r_ in range(2):
                        c0 = 256 * two + 128 * i + 64 * r_
                        load(qt[:, :, r_, two, :], nin_v[:, :, c0:c0 + 64], w_ready[t % 2])
            for i, (c0, n) in enumerate([(512, 256), (768, 256), (1024, 256), (1280, 280), (1560, 256)]):
                t = T_NIN + 2 + i
                tile(t, (tile_of(t, KC, n), nin_v[:, :, c0:c0 + n]))
            for i in range(4):
                t = T_CMP + i
                src = (cmp_k_w1_2, cmp_v_w1_2)[i // 2][0][1024 * (i % 2):1024 * (i % 2) + 1024, :].rearrange(
                    "(i d) n -> d i n", d=N_D)
                dst = slot(t)[:, 0:2048].rearrange("p (i n) -> p i n", n=P)
                tile(t, (dst[0:64], src), (dst[64:128], src))
            t = T_POOL
            tile(t, (slot(t)[:, 0:512].rearrange("p (g e) -> p g e", g=4), pool_w_2[0].rearrange("g c e -> c g e")))
            mo_v = mix_w_out_2[0].rearrange("(k p) n -> p k n", p=P)
            for i in range(4):
                t = T_MIX + i
                tile(t, (tile_of(t, KC, 256), mo_v[:, :, 256 * i:256 * i + 256]))

            def ffn_tiles(l):
                gv = ffn_w_gate_2[l].rearrange("(k p) n -> p k n", p=P)
                uv = ffn_w_up_2[l].rearrange("(k p) n -> p k n", p=P)
                dv = ffn_w_down_2[l].rearrange("(k p) n -> p k n", p=P)
                with nc.sync.Fori(0, FC // 2) as i:
                    for j, v in enumerate((gv, uv)):
                        t = T_F[l] + j
                        sp.wait_ge(s.w_used, i * 2 + (t - 1))
                        load(tile_of(t, KC, 256), v[:, :, bass.ds(i * 256, 256)], w_ready[t % 2])
                with nc.sync.Fori(0, 2) as i:
                    for j in range(4):
                        t = T_D[l] + j
                        sp.wait_ge(s.w_used, i * 4 + (t - 1))
                        load(tile_of(t, 11, 256),
                             dv[:, 11 * (j % 2):11 * (j % 2) + 11, bass.ds(i * 512 + 256 * (j // 2), 256)],
                             w_ready[t % 2])

            ffn_tiles(0)
            p1_v = conv_w_pw1_2[0].rearrange("(k p) n -> p k n", p=P)
            p2_v = conv_w_pw2_2[0].rearrange("(k p) n -> p k n", p=P)
            for i in range(4):
                for j in range(2):
                    t = T_PW1 + 2 * i + j
                    c0 = (D if j == 0 else 0) + 256 * i
                    tile(t, (tile_of(t, KC, 256), p1_v[:, :, c0:c0 + 256]))
            for i in range(4):
                t = T_PW2 + i
                tile(t, (tile_of(t, KC, 256), p2_v[:, :, 256 * i:256 * i + 256]))
            ffn_tiles(1)
            with nc.sync.Fori(0, TB // 2) as i:
                for j in range(2):
                    sp.wait_ge(s.out_ready, i * 2 + (j + 1))
                    sp.dma_start(out[0].rearrange("(t p) d -> p t d", p=P)[:, bass.ds(i * 2 + j, 1), :],
                                 sc[:, j:j + 1, :]).then_inc(out_done[j], 16)
            for j in range(2):
                sp.wait_ge(out_done[j], 16 * TB // 2)
        @block.tensor
        def _(pe):
            mm = pe.matmul

            def need(t):
                pe.wait_ge(w_ready[t % 2], arrives[t])

            def group(j):
                if j >= 2:
                    pe.wait_ge(g_free[j % 2], j // 2)
                return bank(2 * (j % 2), 2)

            def feature_chunk(j, w, kk, src, m):
                o = group(j)
                for half in range(2):
                    for k in range(kk):
                        last = mm(o[0:m, 512 * half:512 * half + 512], w(k), src(k)[:, 512 * half:512 * half + 512],
                                  start=k == 0, stop=k == kk - 1)
                last.then_inc(s.g_out, 1)

            def used():
                pe.drain().then_inc(s.w_used, 1)

            pe.wait_ge(s.const_ok, 2)
            pe.wait_ge(s.par_in, 16 * N_PAR)
            for i, (n, o) in enumerate(((128, 0), (128, 128), (128, 256), (32, V_CW), (64, V_POS))):
                last = pe.transpose(ps[:, o:o + n], sc[0:n, 0, P * i:P * i + P], ident[0:n, 0:n])
            last.then_inc(s.tr_done, 1)
            pe.wait_ge(s.x_in, 32)
            for k in range(KC):
                b = 2 + 2 * (k % 2)
                if k >= 2:
                    pe.wait_ge(s.tr_free, k)
                for t in range(TB):
                    last = pe.transpose(ps[:, 512 * b + P * t:512 * b + P * t + P],
                                        big[:, D * t + P * k:D * t + P * k + P], ident[:, :])
                last.then_inc(s.tr_done, 1)
            pe.wait_ge(s.c_act, 1)
            for k in range(KC):
                need(k)
                for n in range(24):
                    last = mm(ps[:, 3072 + n:3073 + n], slot(k)[:, P * n:P * n + P], misc[:, 8 + k:9 + k],
                              start=k == 0 and n == 0, stop=k == KC - 1, skip_group_check=True)
                last.then_inc(s.w_used, 1)
            pe.drain().then_inc(s.mod_done, 1)
            stage(pe, "loaded")

            def norm_stats(k):
                for c_ in range(KC):
                    pe.wait_ge(s.sq_ready, 8 * k + c_ + 1)
                    for half in range(2):
                        last = mm(bank(6 + half), ones[:, :], sc[:, c_ % 2, 512 * half:512 * half + 512],
                                  start=c_ == 0, stop=c_ == KC - 1)
                    last.then_inc(s.sq_used, 1)

            norm_stats(0)
            stage(pe, "normed_1")
            hs = lambda k: ht[:, k, :]
            j = [J_IN]

            def wide(t, n, c0, m, count):
                w = tile_of(t, KC, n)
                for i in range(count):
                    feature_chunk(j[0], lambda k: w[:, k, c0 + m * i:c0 + m * i + m], KC, hs, m)
                    j[0] += 1

            def tokens(t, n, c0, m, per, stride):
                w = tile_of(t, KC, n)
                for i in range(TB // per):
                    o = group(j[0])
                    for b in range(per):
                        for k in range(KC):
                            last = mm(o[:, stride * b:stride * b + m], ht[:, k, P * (per * i + b):P * (per * i + b) + P],
                                      w[:, k, c0:c0 + m], start=k == 0, stop=k == KC - 1)
                    last.then_inc(s.g_out, 1)
                    j[0] += 1

            need(T_IN); wide(T_IN, A_W, 0, P, 3); used()
            need(T_IN + 1); wide(T_IN + 1, 256, 0, P, 1); tokens(T_IN + 1, 256, P, P, 8, P); used()
            need(T_IN + 2); wide(T_IN + 2, A_W, 0, P, 3); used()
            need(T_IN + 3); wide(T_IN + 3, S_W, 0, P, 2); used()
            need(T_IN + 4); wide(T_IN + 4, S_W, 0, P, 2); used()
            need(T_IN + 5); tokens(T_IN + 5, S_W, 0, S_W, 4, S_W); used()
            need(T_IN + 6); wide(T_IN + 6, S_W, 0, P, 2); used()
            stage(pe, "attention_in")

            def attention(units, n0, lag):
                N = len(units)
                for i in range(N + lag + 1):
                    if i < N:
                        un, n = units[i], n0 + i
                        if i >= 2:
                            pe.wait_ge(s.l_done, n - 1)
                        for a in range(0, un.w, 512):
                            e = min(512, un.w - a)
                            last = mm(ps[:, 1024 * (n % 2) + a:1024 * (n % 2) + a + e], un.q, un.k[:, a:a + e],
                                      start=True, stop=True)
                        last.then_inc(s.s_done, 1)
                    if 0 <= i - lag < N:
                        un, n = units[i - lag], n0 + i - lag
                        pe.wait_ge(s.e_done, n + 1)
                        if n >= 1:
                            pe.wait_ge(s.pt_copied, n)
                        for a in range(0, un.w, P):
                            e = min(P, un.w - a)
                            last = pe.transpose(ps[0:e, 2048 + a:2048 + a + P], sc[:, n % 2, a:a + e], ident[:, :])
                        last.then_inc(s.pt_done, 1)
                    if i - lag - 1 >= 0:
                        un, n = units[i - lag - 1], n0 + i - lag - 1
                        pe.wait_ge(s.pt_copied, n + 1)
                        if n >= 2:
                            pe.wait_ge(s.o_done, n - 1)
                        blocks = (un.w + P - 1) // P
                        for b in range(blocks):
                            e = min(P, un.w - P * b)
                            last = mm(ps[:, 3072 + 512 * (n % 2):3136 + 512 * (n % 2)],
                                      sc[0:e, 2 + n % 2, P * b:P * b + P], un.v(b),
                                      start=b == 0, stop=b == blocks - 1)
                        last.then_inc(s.pv_done, 1)

            attention(swa_units, 0, 1)
            attention(stick_units, N_SWA, 2)
            stage(pe, "attended")
            for n, (src, c_, half) in enumerate(TURNS):
                if n >= 2:
                    pe.wait_ge(s.turn_copied, n - 1)
                for b in range(4):
                    last = pe.transpose(ps[:, 512 * (n % 2) + P * b:512 * (n % 2) + P * b + P],
                                        src[:, 4 * half + b, P * c_:P * c_ + P], ident[:, :])
                last.then_inc(s.turn_done, 1)
            stage(pe, "turned")
            assert j[0] == J_IN2
            need(T_IN + 7); wide(T_IN + 7, M_W, 0, M_D, 4); used()
            need(T_IN + 8); tokens(T_IN + 8, VGW, 0, VGW, 2, 512); used()
            need(T_IN + 9); wide(T_IN + 9, M_W, 0, M_D, 4); used()
            assert j[0] == J_OUT
            stage(pe, "mlstm_in")
            for g in range(2):
                for t in range(TB):
                    last = pe.transpose(ps[0:4, 1024 * g + P * t:1024 * g + P * t + P], gi[:, t, 4 * g:4 * g + 4],
                                        ident[:, :])
            last.then_inc(s.gates_up, 1)
            pe.wait_ge(s.rows_d, 1)
            for t in range(TB):
                pe.transpose(ps[:, 2048 + P * t:2048 + P * t + P], sc[:, 0, P * t:P * t + P], ident[:, :])
            for h in range(M_H):
                last = mm(ps[:, 3072 + TB * h:3072 + TB * h + TB], selr[:, h, :], mrow[:, 2, :], start=True, stop=True)
            last.then_inc(s.rowcols, 1)
            stage(pe, "mlstm_rows")
            need(T_QK)
            qk = slot(T_QK, M_D)[:, 0:768].rearrange("p (w h e) -> p w h e", w=2, h=M_H)
            for n in range(2 * M_H):
                w, h = n // M_H, n % M_H
                if n >= 2:
                    pe.wait_ge(s.qk_copied, n - 1)
                for half in range(2):
                    last = mm(ps[0:M_D, 1024 * (n % 2) + 512 * half:1024 * (n % 2) + 512 * half + 512],
                              qk[:, w, h, :], cu[:, h, 512 * half:512 * half + 512], start=True, stop=True)
                last.then_inc(s.qk_done, 1)
            for t in range(TB):
                if t >= 2:
                    pe.wait_ge(s.ktok_copied, t - 1)
                for h in range(M_H):
                    last = mm(ps[:, 2048 + 512 * (t % 2) + M_D * h:2048 + 512 * (t % 2) + M_D * h + M_D],
                              cu[:, h, P * t:P * t + P], qk[:, 1, h, :], start=True, stop=True)
                last.then_inc(s.ktok_done, 1)
            used()
            stage(pe, "mlstm_qk")
            for t in range(TB):
                if t >= 2:
                    pe.wait_ge(s.ms_weighted, t - 1)
                for h in range(M_H):
                    mm(ps[:, 512 * (t % 2) + P * h:512 * (t % 2) + P * h + P], mkt[:, h, P * t:P * t + P],
                       mq[:, h, P * t:P * t + P], start=True, stop=True)
                for h in range(M_H):
                    last = mm(ps[:, 1024 + 512 * (t % 2) + P * h:1024 + 512 * (t % 2) + P * h + P], selr[:, h, :],
                              sc[0:4, 1, P * t:P * t + P], start=True, stop=True)
                last.then_inc(s.ms_done, 1)
                if t >= 1:
                    pe.wait_ge(s.mstate, t)
                for h in range(M_H):
                    mm(ps[:, 2048 + 97 * h:2048 + 97 * h + 97], mq[:, h, P * t:P * t + P], ct[:, h, :],
                       start=True, stop=True)
                for h in range(M_H):
                    mm(ps[0:M_D, 3072 + 97 * h:3072 + 97 * h + 97], mk[:, t, h, :], mv[:, t, h, :],
                       start=True, stop=True)
                pe.wait_ge(s.ms_weighted, t + 1)
                for h in range(M_H):
                    last = mm(ps[:, 2560 + 97 * h:2560 + 97 * h + 97], sc[:, 3 * (t % 2), P * h:P * h + P],
                              mv[:, t, h, :], start=True, stop=True)
                last.then_inc(s.mo_done, 1)
            stage(pe, "mlstm_scanned")
            pe.wait_ge(s.ht_ready, 1)
            for n in range(2 * M_H):
                h, half = n // 2, n % 2
                if n >= 2:
                    pe.wait_ge(s.ht_copied, n - 1)
                for b in range(4):
                    last = pe.transpose(ps[0:M_D, 512 * (n % 2) + P * b:512 * (n % 2) + P * b + P],
                                        mv[:, 4 * half + b, h, 0:M_D], ident[:, :])
                last.then_inc(s.ht_done, 1)
            stage(pe, "mlstm_out")
            for i in range(4):
                t = T_OUT + i
                need(t)
                wa = slot(t, M_D)[:, 0:1024].rearrange("p (k n) -> p k n", k=4)
                wb = slot(t)[:, 1024:2304].rearrange("p (k n) -> p k n", k=5)
                for m in range(2):
                    feature_chunk(
                        J_OUT + 2 * i + m,
                        lambda k: wa[:, k, P * m:P * m + P] if k < 4 else wb[:, k - 4, P * m:P * m + P], 9,
                        lambda k: mz[:, k, :] if k < 4 else (az[:, k - 4, :] if k < 7 else sz[:, k - 7, :]), P)
                used()
            stage(pe, "y_1")
            norm_stats(1)
            stage(pe, "x_1")
            norm_stats(2)
            stage(pe, "normed_2")
            j[0] = J_NIN
            for i in range(2):
                need(T_NIN + i); wide(T_NIN + i, 256, 0, P, 2); used()
            t = T_NIN + 2
            need(t); wide(t, 256, 0, P, 2); used()
            need(t + 1); wide(t + 1, 256, 0, P, 1); tokens(t + 1, 256, P, P, 8, P); used()
            need(t + 2); wide(t + 2, 256, 0, P, 1); tokens(t + 2, 256, P, P, 8, P); used()
            need(t + 3); tokens(t + 3, 280, 0, 24, 8, 32); wide(t + 3, 280, 24, P, 2); used()
            need(t + 4); wide(t + 4, 256, 0, P, 2); used()
            assert j[0] == J_MIX
            stage(pe, "mixer_in")
            for kv in range(2):
                src = (kc_t, vc_t)[kv]
                t = T_CMP + 2 * kv
                need(t)
                need(t + 1)
                if kv:
                    pe.wait_ge(s.cmp_hid, 2)
                w1 = [slot(t + i)[:, 0:2048].rearrange("p (i n) -> p i n", n=P) for i in range(2)]
                for i in range(32):
                    last = mm(ps[:, 512:513], w1[i // 16][0:64, i % 16, :],
                              cols[0:64, V_POS + 32 * kv + i:V_POS + 32 * kv + i + 1], start=i == 0, stop=i == 31)
                for g in range(2):
                    rows = slice(64 * g, 64 * g + 64)
                    for i in range(32):
                        last = mm(ps[:, 1024 * g:1024 * g + N_CMP], w1[i // 16][rows, i % 16, :],
                                  src[rows, i:i + 16 * (N_CMP - 1) + 1:16], start=i == 0, stop=i == 31)
                last.then_inc(s.cmp_h1, 1)
                used()
                used()
                for g in range(2):
                    pe.wait_ge(s.cmp_hid, 2 * kv + g + 1)
                    if kv:
                        pe.wait_ge(s.cmp_copied, g + 1)
                    if kv == 0:
                        last = mm(ps[0:64, 2048 + 512 * g:2048 + 512 * g + N_CMP], w2s[:, 0, :], hid[:, g, 0:N_CMP],
                                  start=True, stop=True)
                    else:
                        last = mm(ps[0:N_CMP, 2048 + 512 * g:2048 + 512 * g + 64], hid[:, g, 0:N_CMP], w2s[:, 1, :],
                                  start=True, stop=True)
                    last.then_inc(s.cmp_h2, 1)
            stage(pe, "compressed")
            attention(nsa_units, N_FIRST, 1)
            stage(pe, "mixer_attended")
            for n in range(8):
                c_, half = n // 2, n % 2
                if n >= 2:
                    pe.wait_ge(s.turn_copied, len(TURNS) + n - 1)
                for b in range(4):
                    last = pe.transpose(ps[:, 512 * (n % 2) + P * b:512 * (n % 2) + P * b + P],
                                        no[:, 4 * half + b, P * c_:P * c_ + P], ident[:, :])
                last.then_inc(s.turn_done, 1)
            need(T_POOL)
            pe.wait_ge(s.pool_d, 1)
            wp = slot(T_POOL)[:, 0:512].rearrange("p (g e) -> p g e", g=4)
            for g in range(4):
                if g >= 2:
                    pe.wait_ge(s.pool_copied, g - 1)
                for half in range(2):
                    o = 2048 + 1024 * (g % 2) + 512 * half
                    last = mm(ps[:, o:o + 512], wp[:, g, :], u[:, g, 16 + 512 * half:16 + 512 * half + 512],
                              start=True, stop=True)
                last.then_inc(s.pool_mm, 1)
            used()
            stage(pe, "mixer_turned")

            def product(t0, j0):
                for i in range(4):
                    t = t0 + i
                    need(t)
                    w = tile_of(t, KC, 256)
                    for m in range(2):
                        feature_chunk(j0 + 2 * i + m, lambda k: w[:, k, P * m:P * m + P], KC, hs, P)
                    used()

            def two_kinds(t, m, kind, n, ready):
                o_sem, f_sem = ((s.gate_out, s.gate_free), (s.up_out, s.up_free))[kind]
                if m == 0:
                    pe.wait_ge(w_ready[t % 2], ready)
                pe.wait_ge(f_sem, n + 1)
                w = tile_of(t, KC, 256)
                for half in range(2):
                    for k in range(KC):
                        last = mm(bank(2 * kind + half), w[:, k, P * m:P * m + P],
                                  ht[:, k, 512 * half:512 * half + 512], start=k == 0, stop=k == KC - 1)
                last.then_inc(o_sem, 1)
                if m == 1:
                    used()

            product(T_MIX, J_MIX)
            stage(pe, "x_2")

            def ffn(l):
                with nc.tensor.Fori(0, FC // 2) as i:
                    for m in range(2):
                        for kind in range(2):
                            t = T_F[l] + kind
                            two_kinds(t, m, kind, i * 2 + (N_F[l] + m), i * 16 + arrives[t])
                stage(pe, "ffn_act_%d" % (l + 1))
                with nc.tensor.Fori(0, 2) as i:
                    for pair in range(2):
                        for piece in range(2):
                            t = T_D[l] + 2 * pair + piece
                            pe.wait_ge(w_ready[t % 2], i * 32 + arrives[t])
                            w = tile_of(t, FC // 2, 256)
                            for m in range(2):
                                b = bank(4 * pair + 2 * m, 2)
                                if piece == 0:
                                    pe.wait_ge(s.down_free, i * 4 + (8 * l + 2 * pair + m + 1))
                                for half in range(2):
                                    for k in range(FC // 2):
                                        last = mm(b[:, 512 * half:512 * half + 512], w[:, k, P * m:P * m + P],
                                                  act[:, FC // 2 * piece + k, 512 * half:512 * half + 512],
                                                  start=piece == 0 and k == 0, stop=piece == 1 and k == FC // 2 - 1)
                                if piece == 1:
                                    last.then_inc(s.down_out, 1)
                            used()
                stage(pe, ("x_3", "x_5")[l])

            norm_stats(3)
            stage(pe, "normed_3")
            ffn(0)
            norm_stats(4)
            stage(pe, "normed_4")
            for i in range(4):
                for m in range(2):
                    for kind in range(2):
                        t = T_PW1 + 2 * i + kind
                        two_kinds(t, m, kind, N_PW + 2 * i + m, arrives[t])
            stage(pe, "convolved")
            for k in range(KC):
                for half in range(2):
                    last = mm(bank(half), ones[:, :], zc[:, k, 512 * half:512 * half + 512],
                              start=k == 0, stop=k == KC - 1)
            last.then_inc(s.mean_done, 1)
            norm_stats(5)
            stage(pe, "conv_normed")
            product(T_PW2, J_PW2)
            stage(pe, "x_4")
            norm_stats(6)
            stage(pe, "normed_5")
            ffn(1)
            norm_stats(7)
            stage(pe, "normed_6")
            for t in range(TB):
                if t >= 2:
                    pe.wait_ge(s.out_ready, t - 1)
                for k in range(KC):
                    last = pe.transpose(ps[:, 1024 * (t % 2) + P * k:1024 * (t % 2) + P * k + P],
                                        ht[:, k, P * t:P * t + P], ident[:, :])
                last.then_inc(s.ft_done, 1)

        @block.scalar
        def _(a):
            f = a.activation
            chained = [0]

            def chain(ins):
                chained[0] += 1
                ins.then_inc(s.act_chain, 1)
                a.wait_ge(s.act_chain, chained[0])

            a.wait_ge(s.cols_ok, 1)
            f(misc[:, 8:16], cols[:, V_C:V_C + 8], ACT.Silu).then_inc(s.c_act, 1)
            stage(a, "loaded")

            def squares(n, src, eps):
                for k in range(KC):
                    if 8 * n + k >= 2:
                        a.wait_ge(s.sq_used, 8 * n + k - 1)
                    f(sc[:, k % 2, :], src[:, k, :], ACT.Square).then_inc(s.sq_ready, 1)
                a.wait_ge(s.sq_used, 8 * n + 8)
                if n == 5:
                    a.wait_ge(s.xc_done, 1)
                f(sc[:, 2, :], bank(6, 2), ACT.Sqrt, bias=eps, scale=1.0 / D).then_inc(s.rs_ready, 1)

            squares(0, xt, EPS)
            for k in range(KC):
                a.wait_ge(s.h_mul, k + 1)
                f(ht[:, k, :], ht[:, k, :], ACT.Identity, bias=misc[:, 16 + k:17 + k])
            stage(a, "normed_1")

            def copy_out(j, jobs):
                for o, m, per, stride, width, func, scale in jobs:
                    a.wait_ge(s.g_out, j + 1)
                    src = bank(2 * (j % 2), 2)[0:m, :]
                    if per:
                        src = src[:, 0:per * stride].rearrange("p (b n) -> p b n", b=per)[:, :, width[0]:width[1]]
                    if len(o[0].shape) == 4:
                        src = src.rearrange("p b (h d) -> p b h d", h=M_H)
                    if len(o) == 1:
                        f(o[0], src, func, scale=scale).then_inc(g_free[j % 2], 1)
                    else:
                        f(o[0], src, func, scale=scale)
                        s2 = bank(2 * (j % 2), 2)[:, 0:per * stride].rearrange("p (b n) -> p b n", b=per)
                        f(o[1], s2[:, :, width[1]:width[1] + 8], func).then_inc(g_free[j % 2], 1)
                    j += 1
                return j

            w8 = A_D ** -0.5
            cp = lambda o, fn=ACT.Copy, sc_=1.0, m=P: ([o], m, 0, 0, None, fn, sc_)
            jobs = [cp(aq[:, i, :], sc_=w8) for i in range(3)] + [cp(ak), ([av], P, 8, P, (0, P), ACT.Copy, 1.0)]
            jobs += [cp(az[:, i, :], ACT.Silu) for i in range(3)]
            jobs += [cp(sq[:, i, :], sc_=w8) for i in range(2)] + [cp(sk[:, i, :]) for i in range(2)]
            jobs += [([sv[:, 4 * i:4 * i + 4, :]], P, 4, S_W, (0, S_W), ACT.Copy, 1.0) for i in range(2)]
            jobs += [cp(sz[:, i, :], ACT.Silu) for i in range(2)]
            assert copy_out(J_IN, jobs) == J_IN2
            stage(a, "attention_in")

            def copy_pt(n, un):
                a.wait_ge(s.pt_done, n + 1)
                if n >= 2:
                    a.wait_ge(s.pv_done, n - 1)
                e = min(P, un.w)
                blocks = (un.w + P - 1) // P
                f(sc[0:e, 2 + n % 2, 0:P * blocks], ps[0:e, 2048:2048 + P * blocks], ACT.Copy).then_inc(s.pt_copied, 1)

            def soft_attention(units, n0):
                N = len(units)
                for i in range(N + 1):
                    if i < N:
                        un, n = units[i], n0 + i
                        a.wait_ge(s.l_done, n + 1)
                        r = stat[:, n % 16, :]
                        if un.sink is not None:
                            f(r[:, 3:4], misc[:, 2 + un.h:3 + un.h], ACT.Exp, bias=r[:, 0:1])
                        f(sc[:, n % 2, 0:un.w], sc[:, n % 2, 0:un.w], ACT.Exp, bias=r[:, 0:1], scale=-1.0,
                          accum_out=r[:, 1:2]).then_inc(s.e_done, 1)
                    if i >= 1:
                        copy_pt(n0 + i - 1, units[i - 1])

            def stick_attention(units, n0):
                N = len(units)
                for i in range(N + 2):
                    if i < N:
                        un, n = units[i], n0 + i
                        a.wait_ge(s.s_done, n + 1)
                        a.wait_ge(s.pt_done, n - 1)
                        row = sc[:, n % 2, 0:un.w]
                        chain(f(row, ps[:, 1024 * (n % 2):1024 * (n % 2) + un.w], ACT.Abs))
                        chain(f(row, row, ACT.Exp, scale=-1.0))
                        f(row, row, ACT.Ln, bias=1.0).then_inc(s.z_ln, 1)
                    if 0 <= i - 1 < N:
                        un, n = units[i - 1], n0 + i - 1
                        a.wait_ge(s.l_done, n + 1)
                        row = sc[:, n % 2, 0:un.w]
                        f(row, row, ACT.Exp).then_inc(s.x_exp, 1)
                    if i - 2 >= 0:
                        copy_pt(n0 + i - 2, units[i - 2])

            soft_attention(swa_units, 0)
            stick_attention(stick_units, N_SWA)
            stage(a, "attended")
            stage(a, "turned")
            jobs = [cp(mu[:, h, 3:S + 3], m=M_D) for h in range(M_H)]
            jobs += [([mv[:, 2 * i:2 * i + 2, :, 0:M_D], gi[:, 2 * i:2 * i + 2, :]], P, 2, 512, (0, M_W), ACT.Copy, 1.0)
                     for i in range(4)]
            jobs += [cp(mz[:, h, :], ACT.Silu, m=M_D) for h in range(M_H)]
            assert copy_out(J_IN2, jobs) == J_OUT
            stage(a, "mlstm_in")
            hr = lambda i: ht[0:4, i, :]
            a.wait_ge(s.rows_a, 1)
            chain(f(hr(2), hr(1), ACT.Abs))
            chain(f(hr(2), hr(2), ACT.Exp, scale=-1.0))
            f(hr(2), hr(2), ACT.Ln, bias=1.0).then_inc(s.rows_b, 1)
            a.wait_ge(s.rows_c, 1)
            f(sc[32:36, 0, :], sc[32:36, 0, :], ACT.Exp)
            f(sc[64:68, 0, :], hr(6), ACT.Exp, scale=-1.0)
            f(sc[96:100, 0, :], sc[96:100, 0, :], ACT.Exp)
            f(mrow[:, 2, :], mrow[:, 2, :], ACT.Exp).then_inc(s.rows_d, 1)
            for h in range(M_H):
                a.wait_ge(s.conv_done, h + 1)
                f(cu[:, h, :], cu[:, h, :], ACT.Silu, bias=cols[0:M_D, V_CB + h:V_CB + h + 1])
            stage(a, "mlstm_rows")
            for n in range(2 * M_H):
                a.wait_ge(s.qk_done, n + 1)
                dst = mq[:, n, :] if n < M_H else mkt[:, n - M_H, :]
                f(dst, ps[0:M_D, 1024 * (n % 2):1024 * (n % 2) + 1024], ACT.Copy,
                  scale=M_D ** -0.5 if n < M_H else 1.0).then_inc(s.qk_copied, 1)
            stage(a, "mlstm_qk")
            for t in range(TB):
                a.wait_ge(s.md_done, t + 1)
                for h in range(M_H):
                    row = sc[:, 3 * (t % 2), P * h:P * h + P]
                    last = f(row, row, ACT.Exp, bias=sc[:, 2, P * t + h:P * t + h + 1])
                last.then_inc(s.mexp_done, 1)
                a.wait_ge(s.mo_done, t + 1)
                if t >= 1:
                    a.wait_ge(s.mstate, t)
                f(intra, ps[:, 2560:2560 + 388], ACT.Copy).then_inc(s.mintra, 1)
            stage(a, "mlstm_scanned")
            for h in range(M_H):
                f(cu[:, h, :], cu[:, h, :], ACT.Copy, scale=cols[0:M_D, V_SKIP + h:V_SKIP + h + 1])
            a.wait_ge(s.ms_sum, 1)
            f(mst[:, 3], mst[:, 2], ACT.Sqrt, bias=EPS, scale=1.0 / M_D).then_inc(s.ms_root, 1)
            stage(a, "mlstm_out")
            copy_out(J_OUT, [cp(ht[:, i, :]) for i in range(KC)])
            stage(a, "y_1")
            squares(1, ht, EPS)
            stage(a, "x_1")
            squares(2, xt, EPS)
            stage(a, "normed_2")
            jobs = []
            for i in range(4):
                jobs.append(([nq[:, i, :]], P, 0, 0, None, ACT.Copy, None))
            jobs += [cp(kc_t), cp(vc_t), cp(ks), ([vs], P, 8, P, (0, P), ACT.Copy, 1.0)]
            jobs += [cp(kw), ([vw], P, 8, P, (0, P), ACT.Copy, 1.0), ([ng], P, 8, 32, (0, 24), ACT.Sigmoid, 1.0)]
            jobs += [cp(u[:, i, 16:S + 16]) for i in range(4)]
            for i in range(4):
                j = J_NIN + i
                a.wait_ge(s.g_out, j + 1)
                src = bank(2 * (j % 2), 2)
                f(nq[0:64, i, :], src[0:64, :], ACT.Copy, scale=N_D ** -0.5 / n_slope(i))
                f(nq[64:128, i, :], src[64:128, :], ACT.Copy, scale=N_D ** -0.5 / n_slope(i + 4)).then_inc(g_free[j % 2], 1)
            assert copy_out(J_NIN + 4, jobs[4:]) == J_MIX
            stage(a, "mixer_in")
            for kv in range(2):
                a.wait_ge(s.cmp_bias, kv + 1)
                if kv:
                    a.wait_ge(s.cmp_h2, 2)
                for g in range(2):
                    f(hid[:, g, 0:N_CMP], ps[:, 1024 * g:1024 * g + N_CMP], ACT.Gelu_apprx_tanh,
                      bias=hbias[:, kv:kv + 1]).then_inc(s.cmp_hid, 1)
            stage(a, "compressed")
            soft_attention(nsa_units, N_FIRST)
            stage(a, "mixer_attended")
            for g in range(4):
                a.wait_ge(s.pool_mm, g + 1)
                f(ht[:, 4 + g, :], ps[:, 2048 + 1024 * (g % 2):3072 + 1024 * (g % 2)], ACT.Copy,
                  scale=cols[:, V_PS + g:V_PS + g + 1]).then_inc(s.pool_copied, 1)
            stage(a, "mixer_turned")
            stage(a, "x_2")

            def gates(l):
                with nc.scalar.Fori(0, FC // 2) as i:
                    for m in range(2):
                        a.wait_ge(s.gate_out, i * 2 + (N_F[l] + m + 1))
                        f(act[:, bass.ds(i * 2 + m, 1), :], bank(0, 2), ACT.Silu).then_inc(s.gate_free, 1)
                stage(a, "ffn_act_%d" % (l + 1))
                stage(a, ("x_3", "x_5")[l])

            a.nop().then_inc(s.gate_free, 1)
            squares(3, xt, EPS)
            stage(a, "normed_3")
            gates(0)
            squares(4, xt, EPS)
            stage(a, "normed_4")
            for n in range(KC):
                a.wait_ge(s.gate_out, N_PW + n + 1)
                a.wait_ge(s.up_free, N_PW + n + 1)
                f(sg, bank(0, 2), ACT.Sigmoid, bias=cols[:, V_BPW1 + 8 + n:V_BPW1 + 9 + n]).then_inc(s.gate_free, 1)
            stage(a, "convolved")
            a.wait_ge(s.mean_done, 1)
            f(sc[:, 2, :], bank(0, 2), ACT.Copy, scale=1.0 / D).then_inc(s.mean_copied, 1)
            a.wait_ge(s.xc_done, 1)
            squares(5, zc, LN_EPS)
            for k in range(KC):
                a.wait_ge(s.h_mul, H_LN + k + 1)
                f(ht[:, k, :], zc[:, k, :], ACT.Silu, bias=cols[:, V_LNB + k:V_LNB + k + 1],
                  scale=cols[:, V_LNG + k:V_LNG + k + 1])
            stage(a, "conv_normed")
            stage(a, "x_4")
            squares(6, xt, EPS)
            stage(a, "normed_5")
            gates(1)
            squares(7, xt, EPS)
            stage(a, "normed_6")
            for t in range(TB):
                a.wait_ge(s.ft_done, t + 1)
                if t >= 2:
                    a.wait_ge(out_done[t % 2], 16 * (t // 2))
                f(sc[:, t % 2, :], bank(2 * (t % 2), 2), ACT.Copy).then_inc(s.out_ready, 1)

        @block.vector
        def _(v):
            tt, ts, stt = v.tensor_tensor, v.tensor_scalar, v.scalar_tensor_tensor
            mul, add, sub, mx = ALU.mult, ALU.add, ALU.subtract, ALU.max
            chained = [0]

            def chain(ins):
                chained[0] += 1
                ins.then_inc(s.dve_chain, 1)
                v.wait_ge(s.dve_chain, chained[0])

            v.nop().then_inc(s.up_free, 1)
            for _ in range(4):
                v.nop().then_inc(s.down_free, 1)
            v.wait_ge(s.tr_done, 1)
            v.tensor_copy(cols[:, :], ps[:, 0:N_COLS]).then_inc(s.cols_ok, 1)
            for k in range(KC):
                v.wait_ge(s.tr_done, k + 2)
                v.tensor_copy(xt[:, k, :], bank(2 + 2 * (k % 2), 2)).then_inc(s.tr_free, 1)
            v.wait_ge(s.cols_ok, 1)
            v.wait_ge(s.small_in, 80)
            v.tensor_scalar(misc[:, 56:62], misc[:, 2:8], -1.0, None, mul)
            v.wait_ge(s.mod_done, 1)
            chain(tt(misc[:, 16:40], ps[:, 3072:3096], cols[:, V_BMOD:V_BMOD + 24], add))
            stt(misc[:, 40:48], misc[:, 24:32], 1.0, cols[:, V_GPRE:V_GPRE + 8], add, mul)
            tt(misc[:, 48:56], misc[:, 32:40], cols[:, V_GPOST:V_GPOST + 8], mul)
            stage(v, "loaded")

            def root(n):
                v.wait_ge(s.rs_ready, n + 1)
                chain(v.reciprocal(sc[:, 3, :], sc[:, 2, :]))

            def scaled(src, g0, dst, gains=cols):
                for k in range(KC):
                    stt(dst[:, k, :], src[:, k, :], gains[:, g0 + k:g0 + k + 1], sc[:, 3, :], mul, mul).then_inc(s.h_mul, 1)

            root(0)
            scaled(xt, 40, ht, misc)
            stage(v, "normed_1")
            stage(v, "attention_in")

            def outputs(n, un):
                r = stat[:, n % 16, :]
                src = ps[:, 3072 + 512 * (n % 2):3136 + 512 * (n % 2)]
                v.wait_ge(s.pv_done, n + 1)
                if un.kind == "stick":
                    v.tensor_copy(un.out, src).then_inc(s.o_done, 1)
                    return
                if un.first:
                    ts(un.out, src, r[:, 2:3], None, mul).then_inc(s.o_done, 1)
                else:
                    v.wait_ge(s.o_done, n)
                    stt(un.out, src, r[:, 2:3], un.out, mul, add).then_inc(s.o_done, 1)

            def sums(n, un):
                r = stat[:, n % 16, :]
                v.wait_ge(s.e_done, n + 1)
                if un.sink is not None:
                    chain(tt(r[:, 1:2], r[:, 1:2], r[:, 3:4], add))
                if un.kind == "cmp" and un.i == 0:
                    chain(ts(r[:, 1:2], r[:, 1:2], 1e-30, None, mx))
                chain(v.reciprocal(r[:, 2:3], r[:, 1:2]))
                if un.kind == "cmp":
                    prob = psum_p[:, un.g, 4:4 + N_CMP]
                    if un.h % 4 == 0:
                        chain(ts(prob, sc[:, n % 2, 0:N_CMP], r[:, 2:3], None, mul))
                    else:
                        chain(stt(prob, sc[:, n % 2, 0:N_CMP], r[:, 2:3], prob, mul, add))
                if un.gate is not None:
                    chain(tt(r[:, 2:3], r[:, 2:3], un.gate, mul))

            def selection(un):
                pp = psum_p[:, un.g, :]
                i0, i1, top, rep = (imp[:, 16 * a_:16 * a_ + 16] for a_ in range(4))
                chain(v.tensor_reduce(i0, pp[:, 4:68].rearrange("p (j n) -> p j n", n=4)[:, :, 0:3], AX.X, add))
                chain(tt(i1, pp[:, 7:68:4], pp[:, 3:64:4], add))
                chain(stt(i0, i1, 0.5, i0, mul, add))
                chain(tt(i0, i0, force[:, un.i, :], add))
                chain(v.max(top[:, 0:8], i0))
                chain(v.match_replace(rep, top[:, 0:8], i0, -BIGF))
                chain(ts(rep, rep, -2e38, NEG, ALU.is_gt, mul))
                nb = 2 * (un.i + 1)
                chain(tt(tg[:, un.g, 0:un.w].rearrange("p (b n) -> p b n", b=nb),
                         causal[:, P * (7 - un.i):P * (7 - un.i) + un.w].rearrange("p (b n) -> p b n", b=nb),
                         rep[:, 0:nb].unsqueeze(2).to_broadcast([P, nb, 64]), add))

            def soft_attention(units, n0):
                N = len(units)
                for i in range(N + 2):
                    if i < N:
                        un, n = units[i], n0 + i
                        if un.kind == "sel" and un.h % 4 == 0:
                            selection(un)
                        v.wait_ge(s.s_done, n + 1)
                        if i >= 2:
                            v.wait_ge(s.pt_done, n - 1)
                        r = stat[:, n % 16, :]
                        first = misc[:, 56 + un.h:57 + un.h] if un.sink is not None else (
                            1e20 if un.kind == "cmp" else BIGF)
                        v.tensor_tensor_reduce(sc[:, n % 2, 0:un.w], un.dist, ps[:, 1024 * (n % 2):1024 * (n % 2) + un.w],
                                               -un.slope, first, add, ALU.min, r[:, 0:1]).then_inc(s.l_done, 1)
                    if 0 <= i - 1 < N:
                        sums(n0 + i - 1, units[i - 1])
                    if i >= 2:
                        outputs(n0 + i - 2, units[i - 2])

            def stick_attention(units, n0):
                N = len(units)
                for i in range(N + 3):
                    if i < N:
                        un, n = units[i], n0 + i
                        v.wait_ge(s.z_ln, n - n0 + 1)
                        row = sc[:, n % 2, 0:un.w]
                        stt(row, ps[:, 1024 * (n % 2):1024 * (n % 2) + un.w], 0.0, row, mx, add).then_inc(s.z_sp, 1)
                    if 0 <= i - 1 < N:
                        un, n = units[i - 1], n0 + i - 1
                        v.wait_ge(s.z_spm, n - n0 + 1)
                        row = sc[:, n % 2, 0:un.w]
                        back = row[:, ::-1]
                        chain(v.tensor_tensor_scan(back, ones[:, 0:1].to_broadcast([P, un.w]), back, 0.0, mul, add))
                        tt(row, ps[:, 1024 * (n % 2):1024 * (n % 2) + un.w], row, sub).then_inc(s.l_done, 1)
                    if i - 3 >= 0:
                        outputs(n0 + i - 3, units[i - 3])

            soft_attention(swa_units, 0)
            stick_attention(stick_units, N_SWA)
            stage(v, "attended")
            for n, (src, c_, half) in enumerate(TURNS):
                v.wait_ge(s.turn_done, n + 1)
                dst = (az if n < 6 else sz)[:, c_, 512 * half:512 * half + 512]
                tt(dst, bank(n % 2), dst, mul).then_inc(s.turn_copied, 1)
            stage(v, "turned")
            stage(v, "mlstm_in")
            hr = lambda i: ht[0:4, i, :]
            chunked = lambda ap: ap.rearrange("p (t n) -> p t n", n=P)
            per = lambda ap: ap.unsqueeze(2).to_broadcast([4, TB, P])
            v.wait_ge(s.gates_up, 1)
            ts(hr(0), ps[0:4, 0:1024], misc[0:4, 0:1], None, add)
            ts(hr(1), ps[0:4, 1024:2048], misc[0:4, 1:2], None, add).then_inc(s.rows_a, 1)
            v.memset(hr(4), 1.0)
            chain(v.memset(sc[:, 0, :], 0.0))
            chain(v.memset(hr(4)[:, 0:S:P], 0.0))
            v.wait_ge(s.rows_b, 1)
            chain(stt(hr(3), hr(1), 0.0, hr(2), ALU.min, sub))
            v.tensor_tensor_scan(hr(5), hr(4), hr(3), 0.0, mul, add)
            chain(v.tensor_tensor_scan(hr(6), hr(3), hr(0), 0.0, add, mx))
            chain(tt(sc[0:4, 0, :], hr(0), hr(5), sub))
            tt(sc[0:4, 1, :], hr(5), hr(6), sub)
            v.memset(mrow[:, 0, 0:1], 0.0)
            v.tensor_copy(mrow[:, 0, 1:TB], hr(6)[:, P - 1:S - P:P])
            chain(tt(mrow[:, 1, :], hr(5)[:, P - 1:S:P], hr(6)[:, P - 1:S:P], sub))
            chain(tt(mrow[:, 2, :], mrow[:, 1, :], mrow[:, 0, :], add))
            tt(chunked(sc[32:36, 0, :]), chunked(sc[0:4, 1, :]), per(mrow[:, 0, :]), add)
            tt(chunked(sc[96:100, 0, :]), chunked(sc[0:4, 0, :]), per(mrow[:, 1, :]), add).then_inc(s.rows_c, 1)
            for h in range(M_H):
                w = lambda t: cols[0:M_D, V_CW + 4 * t + h:V_CW + 4 * t + h + 1]
                chain(ts(cu[:, h, :], mu[:, h, 0:S], w(0), None, mul))
                for t in range(1, M_CONV):
                    ins = stt(cu[:, h, :], mu[:, h, t:t + S], w(t), cu[:, h, :], mul, add)
                    if t < M_CONV - 1:
                        chain(ins)
                ins.then_inc(s.conv_done, 1)
            v.wait_ge(s.rowcols, 1)
            v.tensor_copy(sc[:, 2, :], bank(4, 2))
            v.tensor_copy(car.rearrange("p h t -> p (h t)"), ps[:, 3072:3072 + M_H * TB])
            stage(v, "mlstm_rows")
            rc = sc[:, 2, :].rearrange("p (t n) -> p t n", n=P)
            for t in range(TB):
                v.wait_ge(s.ktok_done, t + 1)
                o = 2048 + 512 * (t % 2)
                tt(mk[:, t], ps[:, o:o + M_W].rearrange("p (h d) -> p h d", h=M_H),
                   rc[:, t, 96:100].unsqueeze(2).to_broadcast([P, M_H, M_D]), mul).then_inc(s.ktok_copied, 1)
            stage(v, "mlstm_qk")
            for t in range(TB):
                v.wait_ge(s.ms_done, t + 1)
                if t >= 2:
                    v.wait_ge(s.mo_done, t - 1)
                row = sc[:, 3 * (t % 2), 0:512].rearrange("p (h n) -> p h n", h=M_H)
                sl = lambda b: ps[:, 512 * b:512 * b + 512].rearrange("p (h n) -> p h n", h=M_H)
                tt(row, sl(2 + t % 2), tri[:, :].unsqueeze(1).to_broadcast([P, M_H, P]), add).then_inc(s.md_done, 1)
                v.wait_ge(s.mexp_done, t + 1)
                tt(row, sl(t % 2), row, mul).then_inc(s.ms_weighted, 1)
                v.wait_ge(s.mo_done, t + 1)
                for h in range(M_H):
                    stt(ct[:, h, :], ct[:, h, :], car[0:M_D, h, t:t + 1], ps[0:M_D, 3072 + 97 * h:3169 + 97 * h], mul, add)
                v.wait_ge(s.mintra, t + 1)
                for h in range(M_H):
                    last = stt(mv[:, t, h, :], ps[:, 2048 + 97 * h:2145 + 97 * h], rc[:, t, 32 + h:33 + h],
                               intra[:, h, :], mul, add)
                last.then_inc(s.mstate, 1)
            stage(v, "mlstm_scanned")
            hn = mv.rearrange("p t h d -> p (t h) d")
            m0, m1, m2, m3 = (mst[:, i] for i in range(4))
            f0, f1, f2, f3 = (m.rearrange("p t h -> p (t h)") for m in (m0, m1, m2, m3))
            wide = lambda m: m.unsqueeze(2).to_broadcast([P, TB * M_H, M_D])
            chain(stt(f0, hn[:, :, M_D], -1.0, hn[:, :, M_D], mul, mx))
            chain(tt(m0, m0, rc[:, :, 64:68], mx))
            chain(v.reciprocal(f1, f0))
            chain(tt(hn[:, :, 0:M_D], hn[:, :, 0:M_D], wide(f1), mul))
            sqs = ht[:, 4:7, :].rearrange("p a b -> p (a b)").rearrange("p (a d) -> p a d", d=M_D)
            chain(tt(sqs, hn[:, :, 0:M_D], hn[:, :, 0:M_D], mul))
            v.tensor_reduce(f2, sqs, AX.X, add).then_inc(s.ms_sum, 1)
            v.wait_ge(s.ms_root, 1)
            chain(v.reciprocal(f1, f3))
            tt(hn[:, :, 0:M_D], hn[:, :, 0:M_D], wide(f1), mul).then_inc(s.ht_ready, 1)
            for n in range(2 * M_H):
                h, half = n // 2, n % 2
                c_ = slice(512 * half, 512 * half + 512)
                v.wait_ge(s.ht_done, n + 1)
                if n == 0:
                    v.wait_ge(s.ms_root, 1)
                tmp = sc[0:M_D, 3, c_]
                stt(tmp, ps[0:M_D, 512 * (n % 2):512 * (n % 2) + 512], cols[0:M_D, V_NG + h:V_NG + h + 1],
                    cu[:, h, c_], mul, add).then_inc(s.ht_copied, 1)
                v.wait_ge(s.ht_copied, n + 1)
                tt(mz[:, h, c_], tmp, mz[:, h, c_], mul)
            stage(v, "mlstm_out")
            stage(v, "y_1")
            root(1)
            for k in range(KC):
                chain(stt(ht[:, k, :], ht[:, k, :], misc[:, 48 + k:49 + k], sc[:, 3, :], mul, mul))
                tt(xt[:, k, :], xt[:, k, :], ht[:, k, :], add)
            stage(v, "x_1")
            root(2)
            scaled(xt, V_MIX, ht)
            stage(v, "normed_2")
            stage(v, "mixer_in")
            for kv in range(2):
                v.wait_ge(s.cmp_h1, kv + 1)
                v.tensor_copy(hbias[:, kv:kv + 1], ps[:, 512:513]).then_inc(s.cmp_bias, 1)
                for g in range(2):
                    v.wait_ge(s.cmp_h2, 2 * kv + g + 1)
                    src = ps[:, 2048 + 512 * g:2048 + 512 * g + 64]
                    if kv == 0:
                        ins = v.tensor_copy(kcmp[64 * g:64 * g + 64, 0:N_CMP], src[0:64, 0:N_CMP])
                    else:
                        ins = v.tensor_copy(vcmp[:, g, :], src[0:N_CMP, :])
                    ins.then_inc(s.cmp_copied, 1)
            v.memset(psum_p, 0.0)
            v.reciprocal(pw_rc, pw_rc)
            stage(v, "compressed")
            soft_attention(nsa_units, N_FIRST)
            stage(v, "mixer_attended")
            for n in range(8):
                c_, half = n // 2, n % 2
                v.wait_ge(s.turn_done, len(TURNS) + n + 1)
                v.tensor_copy(ht[:, c_, 512 * half:512 * half + 512], bank(n % 2)).then_inc(s.turn_copied, 1)
            stage(v, "mixer_turned")

            def add_product(j0, bias):
                for k in range(KC):
                    j = j0 + k
                    v.wait_ge(s.g_out, j + 1)
                    src = bank(2 * (j % 2), 2)
                    if bias is None:
                        ins = tt(xt[:, k, :], src, xt[:, k, :], add)
                    else:
                        ins = stt(xt[:, k, :], src, cols[:, bias + k:bias + k + 1], xt[:, k, :], add, add)
                    ins.then_inc(g_free[j % 2], 1)

            add_product(J_MIX, None)
            stage(v, "x_2")

            def ffn(l):
                with nc.vector.Fori(0, FC // 2) as i:
                    for m in range(2):
                        v.wait_ge(s.up_out, i * 2 + (N_F[l] + m + 1))
                        v.wait_ge(s.gate_free, i * 2 + (N_F[l] + m + 2))
                        row = act[:, bass.ds(i * 2 + m, 1), :]
                        tt(row, bank(2, 2), row, mul).then_inc(s.up_free, 1)
                stage(v, "ffn_act_%d" % (l + 1))
                with nc.vector.Fori(0, 2) as i:
                    for m in range(4):
                        v.wait_ge(s.down_out, i * 4 + (8 * l + m + 1))
                        row = xt[:, bass.ds(i * 4 + m, 1), :]
                        tt(row, bank(2 * m, 2), row, add).then_inc(s.down_free, 1)
                stage(v, ("x_3", "x_5")[l])

            root(3)
            scaled(xt, V_FFN, ht)
            stage(v, "normed_3")
            ffn(0)
            root(4)
            scaled(xt, V_MIX + 8, ht)
            stage(v, "normed_4")
            taps = lambda t, n: cols[:, V_WDW + 8 * t + n:V_WDW + 8 * t + n + 1]
            for n in range(KC):
                v.wait_ge(s.up_out, N_PW + n + 1)
                v.wait_ge(s.gate_free, N_PW + n + 2)
                stt(zp[:, n, CONV_W - 1:], bank(2, 2), cols[:, V_BPW1 + n:V_BPW1 + n + 1], sg, add, mul)\
                    .then_inc(s.up_free, 1)
                if n not in POOL_CONV:
                    v.wait_ge(s.up_free, N_PW + n + 2)
                    for t in range(CONV_W):
                        if t == 0:
                            ins = ts(zc[:, n, :], zp[:, n, 0:S], taps(0, n), cols[:, V_BDW + n:V_BDW + n + 1], mul, add)
                        else:
                            ins = stt(zc[:, n, :], zp[:, n, t:t + S], taps(t, n), zc[:, n, :], mul, add)
                        chain(ins)
            stage(v, "convolved")
            v.wait_ge(s.mean_copied, 1)
            for k in range(KC):
                last = tt(zc[:, k, :], zc[:, k, :], sc[:, 2, :], sub)
            last.then_inc(s.xc_done, 1)
            v.wait_ge(s.xc_done, 1)
            root(5)
            for k in range(KC):
                tt(zc[:, k, :], zc[:, k, :], sc[:, 3, :], mul).then_inc(s.h_mul, 1)
            stage(v, "conv_normed")
            add_product(J_PW2, V_BPW2)
            stage(v, "x_4")
            root(6)
            scaled(xt, V_FFN + 8, ht)
            stage(v, "normed_5")
            ffn(1)
            root(7)
            scaled(xt, V_FINAL, ht)
            stage(v, "normed_6")

        @block.gpsimd
        def _(g):
            chained = [0]

            def chain(ins):
                chained[0] += 1
                ins.then_inc(s.pool_chain, 1)
                g.wait_ge(s.pool_chain, chained[0])

            def select(o, pattern, op, fill, base, mult):
                return g.affine_select(out=o, in_=o, pattern=pattern, compare_op=op, fill=fill, base=base,
                                       channel_multiplier=mult)

            g.memset(sc[:, 0, 384:512], 0.0).then_inc(s.const_ok, 1)
            g.memset(ones[:, :], 1.0)
            chain(g.memset(ident[:, :], 0.0))
            select(ident[:, :], [[-1, P]], ALU.not_equal, 1.0, 0, 1).then_inc(s.const_ok, 1)
            dist = sc[:, 1, 0:256]
            chain(g.iota(dist, [[-1, 256]], base=P, channel_multiplier=1, allow_small_or_imprecise_dtypes=True))
            for h in range(A_H):
                o = swa_bias[:, 256 * h:256 * h + 256]
                chain(g.tensor_scalar(o, dist, -a_slope(h), 0.0, ALU.mult, ALU.add))
                chain(select(o, [[-1, 256]], ALU.is_ge, NEG, P, 1))
                chain(select(o, [[1, 256]], ALU.is_gt, NEG, 0, -1))
            chain(g.memset(tri[:, :], 0.0))
            chain(select(tri[:, :], [[1, P]], ALU.is_ge, NEG, 0, -1))
            stage(g, "loaded")
            stage(g, "normed_1")
            stage(g, "attention_in")
            for i, un in enumerate(stick_units):
                n = N_SWA + i

                def strict(sem_):
                    d = sc[:, n % 2, un.w - P:un.w]
                    select(d, [[-1, P]], ALU.is_gt, 0.0, 0, 1).then_inc(sem_, 1)
                g.wait_ge(s.z_sp, i + 1)
                strict(s.z_spm)
                if i >= 1:
                    stick_weights(g, i - 1)
            stick_weights(g, len(stick_units) - 1)
            stage(g, "attended")
            stage(g, "turned")
            g.memset(selr, 0.0)
            chain(g.memset(ct, 0.0))
            for h in range(M_H):
                chain(select(selr[:, h, :], [[0, P]], ALU.not_equal, 1.0, -h, 1))
            chain(g.memset(mu[:, :, 0:3], 0.0))
            chain(g.memset(mv[:, :, :, M_D], 1.0))
            stage(g, "mlstm_in")
            chain(g.iota(causal[:, :], [[1, S]], base=P - S, channel_multiplier=-1, allow_small_or_imprecise_dtypes=True))
            chain(select(causal[:, :], [[-1, S]], ALU.is_ge, NEG, S - P, 1))
            chain(g.iota(band[:, :], [[1, 640]], base=-512, channel_multiplier=-1, allow_small_or_imprecise_dtypes=True))
            chain(select(band[:, :], [[-1, 640]], ALU.is_ge, NEG, 512, 1))
            chain(select(band[:, :], [[1, 640]], ALU.is_gt, NEG, 0, -1))
            stage(g, "mlstm_rows")
            stage(g, "mlstm_qk")
            stage(g, "mlstm_scanned")
            stage(g, "mlstm_out")
            stage(g, "y_1")
            stage(g, "x_1")
            flat = cdist.rearrange("p a b -> p (a b)")
            chain(g.iota(flat, [[-P, TB], [16, N_CMP]], base=31, channel_multiplier=-1, allow_small_or_imprecise_dtypes=True))
            chain(select(cdist, [[P, TB], [-16, N_CMP]], ALU.is_ge, NEG, -31, 1))
            chain(g.memset(force, 0.0))
            for hb in range(2):
                o = force[64 * hb:64 * hb + 64]
                chain(select(o, [[2, TB], [-1, 16]], ALU.not_equal, 1e4, hb, 0))
                chain(select(o, [[2, TB], [-1, 16]], ALU.not_equal, 1e4, hb - 1, 0))
                chain(select(o, [[0, TB], [1, 16]], ALU.not_equal, 1e4, 0, 0))
                chain(select(o, [[2, TB], [-1, 16]], ALU.is_ge, NEG, hb, 0))
            chain(g.iota(pw_rc, [[1, 16]], base=1, channel_multiplier=0, allow_small_or_imprecise_dtypes=True))
            chain(g.memset(u[:, :, 0:16], 0.0))
            stage(g, "normed_2")
            stage(g, "mixer_in")
            stage(g, "compressed")
            ta = ht[:, 0:2, :].rearrange("p a b -> p (a b)")
            tb = ht[:, 2:4, :].rearrange("p a b -> p (a b)")
            chain(g.memset(ta[:, 0:16], 0.0))
            chain(g.memset(tb[:, 0:16], 0.0))
            for gi_ in range(4):
                w = 2 ** (gi_ + 1)
                src, step = u[:, gi_, :], 1
                for k in range(gi_ + 1):
                    dst = (ta, tb)[k % 2]
                    chain(g.tensor_tensor(dst[:, 16:16 + S], src[:, 16:16 + S], src[:, 16 - step:16 - step + S], ALU.add))
                    src, step = dst, 2 * step
                rcw = pw_rc[:, 0:w]
                tw = misc[:, 192:192 + w]
                chain(g.tensor_scalar(tw, rcw, float(w), 1.0, ALU.mult, ALU.max))
                chain(g.tensor_tensor(src[:, 16:16 + w], src[:, 16:16 + w], tw, ALU.mult))
                chain(g.tensor_scalar(src[:, 16:16 + S], src[:, 16:16 + S], 1.0 / w, 1.0, ALU.mult, ALU.mult))
                chain(g.tensor_tensor(u[:, gi_, 16:16 + S], src[:, 16:16 + S], u[:, gi_, 16:16 + S], ALU.subtract))
            g.nop().then_inc(s.pool_d, 1)
            stage(g, "mixer_attended")
            stage(g, "mixer_turned")
            stage(g, "x_2")
            stage(g, "normed_3")
            stage(g, "ffn_act_1")
            stage(g, "x_3")
            chain(g.memset(zp[:, :, 0:CONV_W - 1], 0.0))
            stage(g, "normed_4")
            for n in POOL_CONV:
                g.wait_ge(s.up_free, N_PW + n + 2)
                taps = lambda t: cols[:, V_WDW + 8 * t + n:V_WDW + 8 * t + n + 1]
                chain(g.tensor_scalar(zc[:, n, :], zp[:, n, 0:S], taps(0), cols[:, V_BDW + n:V_BDW + n + 1],
                                      ALU.mult, ALU.add))
                for t in range(1, CONV_W):
                    chain(g.tensor_scalar(ptmp, zp[:, n, t:t + S], taps(t), 1.0, ALU.mult, ALU.mult))
                    chain(g.tensor_tensor(zc[:, n, :], zc[:, n, :], ptmp, ALU.add))
            stage(g, "convolved")
            for name in STAGES[STAGES.index("convolved") + 1:]:
                stage(g, name)


_INS = ["x", "c", "w_mod", "b_mod", "g_pre", "g_post", "w_in", "m_conv_w", "m_conv_b", "m_wq", "m_wk", "m_b_i", "m_b_f",
        "m_norm_g", "m_skip", "a_sinks", "w_out", "mix_norm_2", "ffn_norm_2", "nsa_w_in_2", "cmp_pos_k_2",
        "cmp_pos_v_2", "cmp_k_w1_2", "cmp_k_w2_2", "cmp_v_w1_2", "cmp_v_w2_2", "pool_w_2", "pool_scale_2",
        "mix_w_out_2", "conv_w_pw1_2", "conv_b_pw1_2", "conv_w_dw_2", "conv_b_dw_2", "conv_ln_g_2", "conv_ln_b_2",
        "conv_w_pw2_2", "conv_b_pw2_2", "ffn_w_gate_2", "ffn_w_up_2", "ffn_w_down_2", "final_norm_2"]
_OUTS = [((1, S, D), "float32")]


def kernel(**inputs):
    import numpy as _np
    import concourse.bacc as _bacc
    from concourse import mybir as _mybir
    from concourse.bass_utils import run_bass_kernel_spmd as _run

    nc = _bacc.Bacc("TRN2", target_bir_lowering=False, num_devices=1)
    arrays, args = {}, []
    for name in _INS:
        a = _np.ascontiguousarray(inputs[name])
        arrays[f"in_{name}_dram"] = a
        args.append(nc.dram_tensor(f"in_{name}_dram", a.shape, _mybir.dt.from_np(a.dtype), kind="ExternalInput").ap())
    for i, (shape, dtype) in enumerate(_OUTS):
        dt = _mybir.dt.from_np(_np.dtype(dtype))
        args.append(nc.dram_tensor(f"out_{i}_dram", shape, dt, kind="ExternalOutput").ap())
    build(nc, *args)
    r = _run(nc, [arrays], core_ids=[0])
    return r.results[0]["out_0_dram"]
```

```python
import concourse.bass as bass
from concourse import mybir
from contextlib import ExitStack

F32 = mybir.dt.float32
F32R = mybir.dt.float32r
ALU = mybir.AluOpType
ACT = mybir.ActivationFunctionType
AX = mybir.AxisListType

P = 128
S = 1024
D = 1024
KC = D // P
TB = S // P
EPS = 1e-6
LN_EPS = 1e-5
NEG = -1e30
BIGF = 3e38

M_H, M_D, M_CONV = 4, 96, 4
M_W = M_H * M_D
A_H, A_D, A_W, A_KVW = 6, 64, 384, 128
S_H, S_D, S_W = 4, 64, 256
C_MU, C_MVG, C_MZ = 0, M_W, 2 * M_W + 2 * M_H
C_AQ = C_MZ + M_W
C_AK = C_AQ + A_W
C_AZ = C_AK + 2 * A_KVW
C_SQ = C_AZ + A_W
C_SK, C_SV, C_SZ = C_SQ + S_W, C_SQ + 2 * S_W, C_SQ + 3 * S_W
VGW = M_W + 2 * M_H

N_H, N_G, N_D = 8, 2, 64
N_CMP = 63
FF = 2816
FC = FF // P
CONV_W = 31
GC = 256
G_N = FF // GC
G_T = 3 * G_N
SLOT = KC * VGW

(V_C, V_BMOD, V_GPRE, V_GPOST, V_MIX, V_FFN, V_BPW1, V_BDW, V_LNG, V_LNB, V_BPW2) = (
    0, 8, 32, 40, 48, 64, 80, 96, 104, 112, 120)
V_WDW, V_FINAL = 128, 376
V_CW, V_CB, V_NG, V_SKIP, V_PS = 384, 400, 404, 408, 412
V_POS = 416
N_COLS = 480


class Signals:
    pass


class Unit:
    pass


def build(nc, x, c, w_mod, b_mod, g_pre, g_post, w_in, m_conv_w, m_conv_b, m_wq, m_wk, m_b_i, m_b_f,
          m_norm_g, m_skip, a_sinks, w_out, mix_norm_2, ffn_norm_2, nsa_w_in_2, cmp_pos_k_2,
          cmp_pos_v_2, cmp_k_w1_2, cmp_k_w2_2, cmp_v_w1_2, cmp_v_w2_2, pool_w_2, pool_scale_2,
          mix_w_out_2, conv_w_pw1_2, conv_b_pw1_2, conv_w_dw_2, conv_b_dw_2, conv_ln_g_2,
          conv_ln_b_2, conv_w_pw2_2, conv_b_pw2_2, ffn_w_gate_2, ffn_w_up_2, ffn_w_down_2,
          final_norm_2, out):
    with ExitStack() as ctx:
        def sb(name, shape):
            return ctx.enter_context(nc.sbuf_tensor(name, shape, F32))

        def sem(name):
            return ctx.enter_context(nc.semaphore(name))

        xt = sb("xt", [P, KC, S])
        ring = sb("ring", [P, 2, SLOT])
        sc = sb("sc", [P, 4, S])
        cols = sb("cols", [P, N_COLS])
        ident = sb("ident", [P, P])
        ones = sb("ones", [P, P])
        with ExitStack() as other:
            ht = other.enter_context(nc.sbuf_tensor("ht", [P, KC, S], F32))
            big = other.enter_context(nc.sbuf_tensor("big", [P, FC * S], F32))
            dists = other.enter_context(nc.sbuf_tensor("dists", [P, S + 640], F32))
            tri = other.enter_context(nc.sbuf_tensor("tri", [P, P], F32))
        h_part = [ctx.enter_context(nc.sbuf_tensor("h_" + part_, [P, KC, S], F32R)) for part_ in ("high", "low")]
        w_part = [ctx.enter_context(nc.sbuf_tensor("w_" + part_, [P, 2, KC * GC], F32R)) for part_ in ("high", "low")]
        act_part = [ctx.enter_context(nc.sbuf_tensor("act_" + part_, [P, 2, 2, S], F32R)) for part_ in ("high", "low")]
        PASSES = ((0, 0), (1, 0), (0, 1))
        swa_bias = dists[:, 0:256 * A_H]
        causal = dists[:, 0:S]
        band = dists[:, S:S + 640]
        stat = sb("stat", [P, 16, 4])
        misc = sb("misc", [P, 256])
        ps = ctx.enter_context(nc.psum_tensor("ps", [P, 4096], F32))

        def bank(b, n=1):
            return ps[:, 512 * b:512 * (b + n)]

        def part(a, shape=None, parts=P):
            n = 1
            for s_ in shape:
                n *= s_
            v = big[0:parts, a:a + n]
            if len(shape) == 2:
                return v.rearrange("p (a b) -> p a b", a=shape[0])
            if len(shape) == 3:
                return v.rearrange("p (a b c) -> p a b c", a=shape[0], b=shape[1])
            return v

        az = part(0, (3, S))
        sz = part(3072, (2, S))
        aq = part(5120, (3, S))
        ak = part(8192, (S,))
        av = part(9216, (TB, P))
        sq = part(10240, (2, S))
        sk = part(12288, (2, S))
        sv = part(14336, (TB, S_W))
        ao = part(16384, (TB, A_W))
        so = part(19456, (TB, S_W))
        cu = part(5120, (M_H, S), M_D)
        mz = part(9216, (M_H, S), M_D)
        mu = part(13312, (M_H, S + 3), M_D)
        mq = part(13312, (M_H, S), M_D)
        mv = part(17420, (TB, M_H, M_D + 1))
        gi = part(20524, (TB, 8))
        ct = part(20588, (M_H, M_D + 1), M_D)
        intra = part(20976, (M_H, M_D + 1))
        selr = part(21364, (M_H, P), 4)
        car = part(21876, (M_H, TB))
        mrow = part(21908, (3, TB), 4)
        mst = part(21932, (4, TB, M_H))
        mkt = ht[0:M_D, 0:4, :]
        mk = ht[:, 4:7, :].rearrange("p a b -> p (a b)").rearrange("p (t h d) -> p t h d", t=TB, h=M_H)
        nq = part(0, (4, S))
        kc_t = part(4096, (S,))
        vc_t = part(5120, (S,))
        ks = part(6144, (S,))
        kw = part(7168, (S,))
        vs = part(8192, (TB, P))
        vw = part(9216, (TB, P))
        u = part(10240, (4, S + 16))
        no = part(14400, (TB, 512))
        tg = part(18496, (2, S))
        ng = part(20544, (TB, 24))
        kcmp = part(20736, (N_CMP + 1,))
        vcmp = part(20800, (N_G, N_D), N_CMP)
        hid = part(20928, (2, N_CMP + 1))
        hbias = part(21056, (2,))
        cdist = part(21060, (TB, N_CMP))
        force = part(21568, (TB, 16))
        imp = part(21696, (16 * 6,))
        psum_p = part(21792, (2, 68))
        w2s = misc[:, 64:192].rearrange("p (w d) -> p w d", w=2)
        pw_rc = part(22064, (16,))
        zp = part(0, (KC, S + CONV_W - 1))
        zc = part(8432, (KC, S))
        sg = part(16624, (S,))
        ptmp = part(17648, (S,))

        s = Signals()
        s.w_used = sem("w_used")
        s.par_in = sem("par_in")
        s.x_in = sem("x_in")
        s.small_in = sem("small_in")
        s.const_ok = sem("const_ok")
        s.stage_end = sem("stage_end")
        s.tr_done = sem("tr_done")
        s.tr_free = sem("tr_free")
        s.cols_ok = sem("cols_ok")
        s.c_act = sem("c_act")
        s.mod_done = sem("mod_done")
        s.sq_ready = sem("sq_ready")
        s.sq_used = sem("sq_used")
        s.rs_ready = sem("rs_ready")
        s.sum_done = sem("sum_done")
        s.h_mul = sem("h_mul")
        s.h_hi = sem("h_hi")
        s.h_ok = sem("h_ok")
        s.x_add = sem("x_add")
        s.w_hi = sem("w_hi")
        s.w_split = sem("w_split")
        s.act_hi = sem("act_hi")
        s.act_ready = sem("act_ready")
        s.pad_ok = sem("pad_ok")
        s.zc_ok = sem("zc_ok")
        s.zc_ok_pool = sem("zc_ok_pool")
        s.g_out = sem("g_out")
        s.dve_chain = sem("dve_chain")
        s.act_chain = sem("act_chain")
        s.pool_chain = sem("pool_chain")
        s.gate_out = sem("gate_out")
        s.gate_free = sem("gate_free")
        s.up_out = sem("up_out")
        s.up_free = sem("up_free")
        s.down_out = sem("down_out")
        s.down_free = sem("down_free")
        s.s_done = sem("s_done")
        s.l_done = sem("l_done")
        s.e_done = sem("e_done")
        s.pt_done = sem("pt_done")
        s.pt_copied = sem("pt_copied")
        s.pv_done = sem("pv_done")
        s.o_done = sem("o_done")
        s.z_ln = sem("z_ln")
        s.z_sp = sem("z_sp")
        s.z_spm = sem("z_spm")
        s.x_exp = sem("x_exp")
        s.turn_done = sem("turn_done")
        s.turn_copied = sem("turn_copied")
        s.gates_up = sem("gates_up")
        s.rows_a = sem("rows_a")
        s.rows_b = sem("rows_b")
        s.rows_c = sem("rows_c")
        s.rows_d = sem("rows_d")
        s.rowcols = sem("rowcols")
        s.conv_done = sem("conv_done")
        s.qk_done = sem("qk_done")
        s.qk_copied = sem("qk_copied")
        s.ktok_done = sem("ktok_done")
        s.ktok_copied = sem("ktok_copied")
        s.ms_done = sem("ms_done")
        s.md_done = sem("md_done")
        s.mexp_done = sem("mexp_done")
        s.ms_weighted = sem("ms_weighted")
        s.mo_done = sem("mo_done")
        s.mintra = sem("mintra")
        s.mstate = sem("mstate")
        s.ms_sum = sem("ms_sum")
        s.ms_root = sem("ms_root")
        s.ht_ready = sem("ht_ready")
        s.ht_done = sem("ht_done")
        s.ht_copied = sem("ht_copied")
        s.cmp_h1 = sem("cmp_h1")
        s.cmp_bias = sem("cmp_bias")
        s.cmp_hid = sem("cmp_hid")
        s.cmp_h2 = sem("cmp_h2")
        s.cmp_copied = sem("cmp_copied")
        s.pool_d = sem("pool_d")
        s.pool_mm = sem("pool_mm")
        s.pool_copied = sem("pool_copied")
        s.mean_done = sem("mean_done")
        s.mean_copied = sem("mean_copied")
        s.xc_done = sem("xc_done")
        s.ft_done = sem("ft_done")
        s.out_ready = sem("out_ready")
        w_ready = [sem("w_ready0"), sem("w_ready1")]
        g_free = [sem("g_free0"), sem("g_free1")]
        out_done = [sem("out_done0"), sem("out_done1")]

        tiles = [1] * 8
        T_IN = len(tiles)
        tiles += [6, 1, 1, 1, 1, 1, 1, 1, 1, 1]
        T_QK = len(tiles)
        tiles += [2]
        T_OUT = len(tiles)
        tiles += [2] * 4
        T_NIN = len(tiles)
        tiles += [4, 4, 1, 1, 1, 1, 1]
        T_CMP = len(tiles)
        tiles += [2] * 4
        T_POOL = len(tiles)
        tiles += [1]
        T_MIX = len(tiles)
        tiles += [1] * 4
        T_F = []
        T_F.append(len(tiles)); tiles += [1] * G_T
        T_PW1 = len(tiles)
        tiles += [1] * 8
        T_PW2 = len(tiles)
        tiles += [1] * 4
        T_F.append(len(tiles)); tiles += [1] * G_T
        arrives = [16 * sum(tiles[t % 2:t + 1:2]) for t in range(len(tiles))]

        def freed(t):
            split_before = sum(max(0, min(G_T, t - 1 - t0)) for t0 in T_F)
            if any(t0 <= t - 2 < t0 + G_T for t0 in T_F):
                return s.w_split, split_before
            return s.w_used, t - 1 - split_before

        def slot(t, parts=P):
            return ring[0:parts, t % 2, :]

        def tile_of(t, k, n):
            return slot(t)[:, 0:k * n].rearrange("p (k n) -> p k n", k=k)

        win_v = w_in[0].rearrange("(k p) n -> p k n", p=P)
        nin_v = nsa_w_in_2[0].rearrange("(k p) n -> p k n", p=P)

        STAGES = ("loaded attention_in attended turned mlstm_in mlstm_rows mlstm_qk mlstm_scanned mlstm_out "
                  "y_1 x_1 mixer_in compressed mixer_attended mixer_turned x_2 x_3 convolved conv_normed x_4 x_5").split()
        def stage(eng, name):
            eng.drain().then_inc(s.stage_end, 1)
            eng.wait_ge(s.stage_end, 4 * (STAGES.index(name) + 1))

        J_IN = 0
        J_IN2 = J_IN + 3 + 1 + 1 + 3 + 2 + 2 + 2 + 2
        J_OUT = J_IN2 + 4 + 4 + 4
        J_NIN = J_OUT + 8
        J_MIX = J_NIN + 4 + 2 + 2 + 2 + 3 + 2
        J_PW2 = J_MIX + 8

        def a_slope(h):
            return 2.0 ** (-8.0 * (h + 1) / A_H)

        def n_slope(h):
            return 2.0 ** (-(h + 1))

        def unit(kind, i, h, q, k, w, v, out_, dist=None, slope=1.0, sink=None, gate=None, g=0, first=True):
            un = Unit()
            un.kind, un.i, un.h, un.q, un.k, un.w, un.v, un.out = kind, i, h, q, k, w, v, out_
            un.dist, un.slope, un.sink, un.gate, un.g, un.first = dist, slope, sink, gate, g, first
            return un

        def rows_of(half):
            return slice(64 * half, 64 * half + 64)

        swa_units, stick_units, nsa_units = [], [], []
        for i in range(TB):
            for h in range(A_H):
                half, c_ = h // 3, h % 3
                b0 = max(0, i - 1)
                w = P * (i + 1 - b0)
                swa_units.append(unit(
                    "swa", i, h, aq[rows_of(half), c_, P * i:P * i + P], ak[rows_of(half), P * b0:P * b0 + w], w,
                    lambda b, b0=b0, half=half: av[:, b0 + b, 64 * half:64 * half + 64],
                    ao[:, i, 64 * h:64 * h + 64], swa_bias[:, 256 * h + 256 - w:256 * h + 256], 1.0, sink=True))
            for h in range(S_H):
                half, c_ = h % 2, h // 2
                w = P * (i + 1)
                stick_units.append(unit(
                    "stick", i, h, sq[rows_of(half), c_, P * i:P * i + P], sk[rows_of(half), c_, 0:w], w,
                    lambda b, h=h: sv[:, b, 64 * h:64 * h + 64], so[:, i, 64 * h:64 * h + 64]))
            for kind in ("cmp", "win", "sel"):
                for h in range(N_H):
                    g, c_ = h // 4, h % 4
                    cols_ = slice(64 * g, 64 * g + 64)
                    q = nq[rows_of(g), c_, P * i:P * i + P]
                    branch = ("cmp", "sel", "win").index(kind)
                    args = dict(slope=n_slope(h), gate=ng[:, i, 3 * h + branch:3 * h + branch + 1], g=g,
                                first=kind == "cmp")
                    o = no[:, i, 64 * h:64 * h + 64]
                    if kind == "cmp":
                        un = unit(kind, i, h, q, kcmp[rows_of(g), 0:N_CMP], N_CMP,
                                  lambda b, g=g: vcmp[:, g, :], o, cdist[:, i, :], **args)
                    elif kind == "win":
                        b0 = max(0, i - 4)
                        w = P * (i + 1 - b0)
                        un = unit(kind, i, h, q, kw[rows_of(g), P * b0:P * b0 + w], w,
                                  lambda b, b0=b0, cols_=cols_: vw[:, b0 + b, cols_], o, band[:, 640 - w:640], **args)
                    else:
                        w = P * (i + 1)
                        un = unit(kind, i, h, q, ks[rows_of(g), 0:w], w,
                                  lambda b, cols_=cols_: vs[:, b, cols_], o, tg[:, g, 0:w], **args)
                    nsa_units.append(un)
        N_SWA = len(swa_units)
        N_FIRST = N_SWA + len(stick_units)
        TURNS = [(ao, c_, half) for c_ in range(3) for half in range(2)]
        TURNS += [(so, c_, half) for c_ in range(2) for half in range(2)]
        N_PAR = 23
        N_F, N_PW = (0, FC + KC), FC
        N_A = (0, FC)
        N_DOWN = (8, 8 + 8 * G_N)
        LAST = 1 + 3 * (G_N - 1) + 1
        POOL_CONV = (0, 3)
        H_MUL = {0: 0, 3: 8, 5: 16, 6: 24}
        H_OK = {0: 0, 2: 8, 3: 16, 4: 24, 5: 32, 6: 40, 7: 48}

        def stick_weights(g, i):
            un, n = stick_units[i], N_SWA + i
            g.wait_ge(s.x_exp, i + 1)
            g.affine_select(out=sc[:, n % 2, un.w - P:un.w], in_=sc[:, n % 2, un.w - P:un.w], pattern=[[-1, P]],
                            compare_op=ALU.is_gt, fill=0.0, base=0, channel_multiplier=1).then_inc(s.e_done, 1)

        block = ctx.enter_context(nc.Block())

        @block.sync
        def _(sp):
            def load(dst, src, arrived):
                sp.dma_start(dst, src).then_inc(arrived, 16)

            def rows(v, n, w=P):
                return v.rearrange("(a b) -> a b", b=w)
            pr = sc[:, 0:1, :].rearrange("p a b -> p (a b)")
            r0, r1, r2, r3, r4 = (pr[:, P * i:P * i + P] for i in range(5))
            load(r0[V_C:V_C + 8, :], c[0].rearrange("(a b) -> a b", b=P), s.par_in)
            load(r0[V_BMOD:V_BMOD + 24, :], b_mod[0].rearrange("(a b) -> a b", b=P), s.par_in)
            load(r0[V_GPRE:V_GPRE + 8, :], g_pre[0].rearrange("(a b) -> a b", b=P), s.par_in)
            load(r0[V_GPOST:V_GPOST + 8, :], g_post[0].rearrange("(a b) -> a b", b=P), s.par_in)
            load(r0[V_MIX:V_MIX + 16, :], mix_norm_2.rearrange("l (a b) -> (l a) b", b=P), s.par_in)
            load(r0[V_FFN:V_FFN + 16, :], ffn_norm_2.rearrange("l (a b) -> (l a) b", b=P), s.par_in)
            load(r0[V_BPW1:V_BPW1 + 16, :], conv_b_pw1_2[0].rearrange("(a b) -> a b", b=P), s.par_in)
            load(r0[V_BDW:V_BDW + 8, :], conv_b_dw_2[0].rearrange("(a b) -> a b", b=P), s.par_in)
            load(r0[V_LNG:V_LNG + 8, :], conv_ln_g_2[0].rearrange("(a b) -> a b", b=P), s.par_in)
            load(r0[V_LNB:V_LNB + 8, :], conv_ln_b_2[0].rearrange("(a b) -> a b", b=P), s.par_in)
            load(r0[V_BPW2:V_BPW2 + 8, :], conv_b_pw2_2[0].rearrange("(a b) -> a b", b=P), s.par_in)
            wdw = conv_w_dw_2[0].rearrange("t (a b) -> (t a) b", b=P)
            load(r1, wdw[0:P, :], s.par_in)
            load(r2[0:120, :], wdw[P:248, :], s.par_in)
            load(r2[120:128, :], final_norm_2.rearrange("(a b) -> a b", b=P), s.par_in)
            sp.wait_ge(s.const_ok, 1)
            load(r3[0:16, 0:96], m_conv_w[0].rearrange("t (a b) -> (t a) b", b=96), s.par_in)
            load(r3[16:20, 0:96], m_conv_b[0].rearrange("(a b) -> a b", b=96), s.par_in)
            load(r3[20:24, 0:96], m_norm_g[0].rearrange("(a b) -> a b", b=96), s.par_in)
            load(r3[24:28, 0:96], m_skip[0].rearrange("(a b) -> a b", b=96), s.par_in)
            load(r3[28:32, :], pool_scale_2[0].rearrange("(a b) -> a b", b=P), s.par_in)
            for i, pos in enumerate((cmp_pos_k_2, cmp_pos_v_2)):
                for half in range(2):
                    load(r4[32 * i:32 * i + 32, 64 * half:64 * half + 64], pos[0], s.par_in)
            load(misc[0:4, 0:1], m_b_i[0].rearrange("(h o) -> h o", o=1), s.small_in)
            load(misc[0:4, 1:2], m_b_f[0].rearrange("(h o) -> h o", o=1), s.small_in)
            load(misc[:, 2:8], a_sinks[0:1, :].to_broadcast([P, A_H]), s.small_in)
            load(w2s[:, 0, :], cmp_k_w2_2[0], s.small_in)
            load(w2s[:, 1, :], cmp_v_w2_2[0], s.small_in)
            for half in range(2):
                load(big[:, 4096 * half:4096 * half + 4096].rearrange("p (t d) -> p t d", d=D),
                     x[0].rearrange("(t p) d -> p t d", p=P)[:, 4 * half:4 * half + 4, :], s.x_in)

            def tile(t, *pairs):
                if t >= 2:
                    sp.wait_ge(*freed(t))
                for dst, src in pairs:
                    load(dst, src, w_ready[t % 2])

            for k in range(8):
                tile(k, (slot(k)[:, 0:3 * D], w_mod[0][k * P:(k + 1) * P, :]))
            t = T_IN
            aqt = tile_of(t, KC, A_W).rearrange("p k (r two d) -> p k r two d", two=2, d=A_D)
            if t >= 2:
                sp.wait_ge(s.w_used, t - 1)
            aqs = win_v[:, :, C_AQ:C_AQ + A_W].rearrange("p k (two r d) -> p k r two d", two=2, d=A_D)
            for two in range(2):
                for r_ in range(3):
                    load(aqt[:, :, r_, two, :], aqs[:, :, r_, two, :], w_ready[t % 2])
            for i, (c0, n) in enumerate([(C_AK, 256), (C_AZ, A_W), (C_SQ, S_W), (C_SK, S_W), (C_SV, S_W),
                                         (C_SZ, S_W), (C_MU, M_W), (C_MVG, VGW), (C_MZ, M_W)]):
                t = T_IN + 1 + i
                tile(t, (tile_of(t, KC, n), win_v[:, :, c0:c0 + n]))
            t = T_QK
            qk = slot(t, M_D)[:, 0:768].rearrange("p (w h e) -> p w h e", w=2, h=M_H)
            tile(t, (qk[:, 0], m_wq[0].rearrange("h d e -> d h e")), (qk[:, 1], m_wk[0].rearrange("h d e -> d h e")))
            for i in range(4):
                t = T_OUT + i
                tile(t, (slot(t, M_D)[:, 0:1024].rearrange("p (k n) -> p k n", k=4),
                         w_out[0][0:M_W, 256 * i:256 * i + 256].rearrange("(k p) n -> p k n", p=M_D)),
                     (slot(t)[:, 1024:2304].rearrange("p (k n) -> p k n", k=5),
                      w_out[0][M_W:D, 256 * i:256 * i + 256].rearrange("(k p) n -> p k n", p=P)))
            for i in range(2):
                t = T_NIN + i
                qt = tile_of(t, KC, 256).rearrange("p k (r two d) -> p k r two d", two=2, d=N_D)
                sp.wait_ge(s.w_used, t - 1)
                for two in range(2):
                    for r_ in range(2):
                        c0 = 256 * two + 128 * i + 64 * r_
                        load(qt[:, :, r_, two, :], nin_v[:, :, c0:c0 + 64], w_ready[t % 2])
            for i, (c0, n) in enumerate([(512, 256), (768, 256), (1024, 256), (1280, 280), (1560, 256)]):
                t = T_NIN + 2 + i
                tile(t, (tile_of(t, KC, n), nin_v[:, :, c0:c0 + n]))
            for i in range(4):
                t = T_CMP + i
                src = (cmp_k_w1_2, cmp_v_w1_2)[i // 2][0][1024 * (i % 2):1024 * (i % 2) + 1024, :].rearrange(
                    "(i d) n -> d i n", d=N_D)
                dst = slot(t)[:, 0:2048].rearrange("p (i n) -> p i n", n=P)
                tile(t, (dst[0:64], src), (dst[64:128], src))
            t = T_POOL
            tile(t, (slot(t)[:, 0:512].rearrange("p (g e) -> p g e", g=4), pool_w_2[0].rearrange("g c e -> c g e")))
            mo_v = mix_w_out_2[0].rearrange("(k p) n -> p k n", p=P)
            for i in range(4):
                t = T_MIX + i
                tile(t, (tile_of(t, KC, 256), mo_v[:, :, 256 * i:256 * i + 256]))

            def ffn_tiles(l):
                gv = ffn_w_gate_2[l].rearrange("(k p) n -> p k n", p=P)
                uv = ffn_w_up_2[l].rearrange("(k p) n -> p k n", p=P)
                dv = ffn_w_down_2[l].rearrange("(k p) n -> p k n", p=P)
                t0 = T_F[l]
                tile(t0, (tile_of(t0, KC, GC), gv[:, :, 0:GC]))
                tile(t0 + 1, (tile_of(t0 + 1, KC, GC), uv[:, :, 0:GC]))
                with nc.sync.Fori(0, (G_N - 1) // 2) as i:
                    for r in range(2):
                        for j in range(3):
                            t = t0 + 2 + 3 * r + j
                            sp.wait_ge(s.w_split, i * 6 + (G_T * l + t - 1 - t0))
                            dst = tile_of(t, KC, GC) if j < 2 else tile_of(t, 2, D)
                            src = ((gv, uv)[j][:, :, bass.ds(i * (2 * GC) + GC * (r + 1), GC)] if j < 2
                                   else dv[:, bass.ds(i * 4 + 2 * r, 2), :])
                            load(dst, src, w_ready[t % 2])
                t = t0 + LAST
                tile(t, (tile_of(t, 2, D), dv[:, FC - 2:FC, :]))

            ffn_tiles(0)
            p1_v = conv_w_pw1_2[0].rearrange("(k p) n -> p k n", p=P)
            p2_v = conv_w_pw2_2[0].rearrange("(k p) n -> p k n", p=P)
            for i in range(4):
                for j in range(2):
                    t = T_PW1 + 2 * i + j
                    c0 = (D if j == 0 else 0) + 256 * i
                    tile(t, (tile_of(t, KC, 256), p1_v[:, :, c0:c0 + 256]))
            for i in range(4):
                t = T_PW2 + i
                tile(t, (tile_of(t, KC, 256), p2_v[:, :, 256 * i:256 * i + 256]))
            ffn_tiles(1)
            with nc.sync.Fori(0, TB // 2) as i:
                for j in range(2):
                    sp.wait_ge(s.out_ready, i * 2 + (j + 1))
                    sp.dma_start(out[0].rearrange("(t p) d -> p t d", p=P)[:, bass.ds(i * 2 + j, 1), :],
                                 sc[:, j:j + 1, :]).then_inc(out_done[j], 16)
            for j in range(2):
                sp.wait_ge(out_done[j], 16 * TB // 2)
        @block.tensor
        def _(pe):
            mm = pe.matmul

            def need(t):
                pe.wait_ge(w_ready[t % 2], arrives[t])

            def group(j):
                if j >= 2:
                    pe.wait_ge(g_free[j % 2], j // 2)
                return bank(2 * (j % 2), 2)

            def feature_chunk(j, w, kk, src, m, norm=None):
                o = group(j)
                for half in range(2):
                    for k in range(kk):
                        if norm is not None and half == 0:
                            pe.wait_ge(s.h_ok, H_OK[norm] + k + 1)
                        last = mm(o[0:m, 512 * half:512 * half + 512], w(k), src(k)[:, 512 * half:512 * half + 512],
                                  start=k == 0, stop=k == kk - 1)
                last.then_inc(s.g_out, 1)

            def used():
                pe.drain().then_inc(s.w_used, 1)

            pe.wait_ge(s.const_ok, 2)
            pe.wait_ge(s.par_in, 16 * N_PAR)
            for i, (n, o) in enumerate(((128, 0), (128, 128), (128, 256), (32, V_CW), (64, V_POS))):
                last = pe.transpose(ps[:, o:o + n], sc[0:n, 0, P * i:P * i + P], ident[0:n, 0:n])
            last.then_inc(s.tr_done, 1)
            pe.wait_ge(s.x_in, 32)
            for k in range(KC):
                b = 2 + 2 * (k % 2)
                if k >= 2:
                    pe.wait_ge(s.tr_free, k - 1)
                for t in range(TB):
                    last = pe.transpose(ps[:, 512 * b + P * t:512 * b + P * t + P],
                                        big[:, D * t + P * k:D * t + P * k + P], ident[:, :])
                last.then_inc(s.tr_done, 1)

            def norm_sum(n):
                pe.wait_ge(s.sq_used, 8 * n + 8)
                for half in range(2):
                    last = mm(bank(6 + half), ones[:, :], sc[:, 2, 512 * half:512 * half + 512], start=True, stop=True)
                last.then_inc(s.sum_done, 1)

            norm_sum(0)
            pe.wait_ge(s.c_act, 1)
            for k in range(KC):
                need(k)
                for n in range(24):
                    last = mm(ps[:, 512 + n:513 + n], slot(k)[:, P * n:P * n + P], misc[:, 8 + k:9 + k],
                              start=k == 0 and n == 0, stop=k == KC - 1, skip_group_check=True)
                last.then_inc(s.w_used, 1)
            pe.drain().then_inc(s.mod_done, 1)

            stage(pe, "loaded")
            hs = lambda k: ht[:, k, :]
            j = [J_IN]

            def wide(t, n, c0, m, count, norm=None):
                w = tile_of(t, KC, n)
                for i in range(count):
                    feature_chunk(j[0], lambda k: w[:, k, c0 + m * i:c0 + m * i + m], KC, hs, m,
                                  norm if i == 0 else None)
                    j[0] += 1

            def tokens(t, n, c0, m, per, stride):
                w = tile_of(t, KC, n)
                for i in range(TB // per):
                    o = group(j[0])
                    for b in range(per):
                        for k in range(KC):
                            last = mm(o[:, stride * b:stride * b + m], ht[:, k, P * (per * i + b):P * (per * i + b) + P],
                                      w[:, k, c0:c0 + m], start=k == 0, stop=k == KC - 1)
                    last.then_inc(s.g_out, 1)
                    j[0] += 1

            need(T_IN); wide(T_IN, A_W, 0, P, 3, norm=0); used()
            need(T_IN + 1); wide(T_IN + 1, 256, 0, P, 1); tokens(T_IN + 1, 256, P, P, 8, P); used()
            need(T_IN + 2); wide(T_IN + 2, A_W, 0, P, 3); used()
            need(T_IN + 3); wide(T_IN + 3, S_W, 0, P, 2); used()
            need(T_IN + 4); wide(T_IN + 4, S_W, 0, P, 2); used()
            need(T_IN + 5); tokens(T_IN + 5, S_W, 0, S_W, 4, S_W); used()
            need(T_IN + 6); wide(T_IN + 6, S_W, 0, P, 2); used()
            stage(pe, "attention_in")

            def attention(units, n0, lag):
                N = len(units)
                for i in range(N + lag + 1):
                    if i < N:
                        un, n = units[i], n0 + i
                        if i >= 2:
                            pe.wait_ge(s.l_done, n - 1)
                        for a in range(0, un.w, 512):
                            e = min(512, un.w - a)
                            last = mm(ps[:, 1024 * (n % 2) + a:1024 * (n % 2) + a + e], un.q, un.k[:, a:a + e],
                                      start=True, stop=True)
                        last.then_inc(s.s_done, 1)
                    if 0 <= i - lag < N:
                        un, n = units[i - lag], n0 + i - lag
                        pe.wait_ge(s.e_done, n + 1)
                        if n >= 1:
                            pe.wait_ge(s.pt_copied, n)
                        for a in range(0, un.w, P):
                            e = min(P, un.w - a)
                            last = pe.transpose(ps[0:e, 2048 + a:2048 + a + P], sc[:, n % 2, a:a + e], ident[:, :])
                        last.then_inc(s.pt_done, 1)
                    if i - lag - 1 >= 0:
                        un, n = units[i - lag - 1], n0 + i - lag - 1
                        pe.wait_ge(s.pt_copied, n + 1)
                        if n >= 2:
                            pe.wait_ge(s.o_done, n - 1)
                        blocks = (un.w + P - 1) // P
                        for b in range(blocks):
                            e = min(P, un.w - P * b)
                            last = mm(ps[:, 3072 + 512 * (n % 2):3136 + 512 * (n % 2)],
                                      sc[0:e, 2 + n % 2, P * b:P * b + P], un.v(b),
                                      start=b == 0, stop=b == blocks - 1)
                        last.then_inc(s.pv_done, 1)

            attention(swa_units, 0, 1)
            attention(stick_units, N_SWA, 2)
            stage(pe, "attended")
            for n, (src, c_, half) in enumerate(TURNS):
                if n >= 2:
                    pe.wait_ge(s.turn_copied, n - 1)
                for b in range(4):
                    last = pe.transpose(ps[:, 512 * (n % 2) + P * b:512 * (n % 2) + P * b + P],
                                        src[:, 4 * half + b, P * c_:P * c_ + P], ident[:, :])
                last.then_inc(s.turn_done, 1)
            stage(pe, "turned")
            assert j[0] == J_IN2
            need(T_IN + 7); wide(T_IN + 7, M_W, 0, M_D, 4); used()
            need(T_IN + 8); tokens(T_IN + 8, VGW, 0, VGW, 2, 512); used()
            need(T_IN + 9); wide(T_IN + 9, M_W, 0, M_D, 4); used()
            assert j[0] == J_OUT
            stage(pe, "mlstm_in")
            for g in range(2):
                for t in range(TB):
                    last = pe.transpose(ps[0:4, 1024 * g + P * t:1024 * g + P * t + P], gi[:, t, 4 * g:4 * g + 4],
                                        ident[:, :])
            last.then_inc(s.gates_up, 1)
            pe.wait_ge(s.rows_d, 1)
            for t in range(TB):
                pe.transpose(ps[:, 2048 + P * t:2048 + P * t + P], sc[:, 0, P * t:P * t + P], ident[:, :])
            for h in range(M_H):
                last = mm(ps[:, 3072 + TB * h:3072 + TB * h + TB], selr[:, h, :], mrow[:, 2, :], start=True, stop=True)
            last.then_inc(s.rowcols, 1)
            stage(pe, "mlstm_rows")
            need(T_QK)
            qk = slot(T_QK, M_D)[:, 0:768].rearrange("p (w h e) -> p w h e", w=2, h=M_H)
            for n in range(2 * M_H):
                w, h = n // M_H, n % M_H
                if n >= 2:
                    pe.wait_ge(s.qk_copied, n - 1)
                for half in range(2):
                    last = mm(ps[0:M_D, 1024 * (n % 2) + 512 * half:1024 * (n % 2) + 512 * half + 512],
                              qk[:, w, h, :], cu[:, h, 512 * half:512 * half + 512], start=True, stop=True)
                last.then_inc(s.qk_done, 1)
            for t in range(TB):
                if t >= 2:
                    pe.wait_ge(s.ktok_copied, t - 1)
                for h in range(M_H):
                    last = mm(ps[:, 2048 + 512 * (t % 2) + M_D * h:2048 + 512 * (t % 2) + M_D * h + M_D],
                              cu[:, h, P * t:P * t + P], qk[:, 1, h, :], start=True, stop=True)
                last.then_inc(s.ktok_done, 1)
            used()
            stage(pe, "mlstm_qk")
            for t in range(TB):
                if t >= 2:
                    pe.wait_ge(s.ms_weighted, t - 1)
                for h in range(M_H):
                    mm(ps[:, 512 * (t % 2) + P * h:512 * (t % 2) + P * h + P], mkt[:, h, P * t:P * t + P],
                       mq[:, h, P * t:P * t + P], start=True, stop=True)
                for h in range(M_H):
                    last = mm(ps[:, 1024 + 512 * (t % 2) + P * h:1024 + 512 * (t % 2) + P * h + P], selr[:, h, :],
                              sc[0:4, 1, P * t:P * t + P], start=True, stop=True)
                last.then_inc(s.ms_done, 1)
                if t >= 1:
                    pe.wait_ge(s.mstate, t)
                for h in range(M_H):
                    mm(ps[:, 2048 + 97 * h:2048 + 97 * h + 97], mq[:, h, P * t:P * t + P], ct[:, h, :],
                       start=True, stop=True)
                for h in range(M_H):
                    mm(ps[0:M_D, 3072 + 97 * h:3072 + 97 * h + 97], mk[:, t, h, :], mv[:, t, h, :],
                       start=True, stop=True)
                pe.wait_ge(s.ms_weighted, t + 1)
                for h in range(M_H):
                    last = mm(ps[:, 2560 + 97 * h:2560 + 97 * h + 97], sc[:, 3 * (t % 2), P * h:P * h + P],
                              mv[:, t, h, :], start=True, stop=True)
                last.then_inc(s.mo_done, 1)
            stage(pe, "mlstm_scanned")
            pe.wait_ge(s.ht_ready, 1)
            for n in range(2 * M_H):
                h, half = n // 2, n % 2
                if n >= 2:
                    pe.wait_ge(s.ht_copied, n - 1)
                for b in range(4):
                    last = pe.transpose(ps[0:M_D, 512 * (n % 2) + P * b:512 * (n % 2) + P * b + P],
                                        mv[:, 4 * half + b, h, 0:M_D], ident[:, :])
                last.then_inc(s.ht_done, 1)
            stage(pe, "mlstm_out")
            for i in range(4):
                t = T_OUT + i
                need(t)
                wa = slot(t, M_D)[:, 0:1024].rearrange("p (k n) -> p k n", k=4)
                wb = slot(t)[:, 1024:2304].rearrange("p (k n) -> p k n", k=5)
                for m in range(2):
                    feature_chunk(
                        J_OUT + 2 * i + m,
                        lambda k: wa[:, k, P * m:P * m + P] if k < 4 else wb[:, k - 4, P * m:P * m + P], 9,
                        lambda k: mz[:, k, :] if k < 4 else (az[:, k - 4, :] if k < 7 else sz[:, k - 7, :]), P)
                used()
            norm_sum(1)
            stage(pe, "y_1")
            norm_sum(2)
            stage(pe, "x_1")
            j[0] = J_NIN
            for i in range(2):
                need(T_NIN + i); wide(T_NIN + i, 256, 0, P, 2, norm=2 if i == 0 else None); used()
            t = T_NIN + 2
            need(t); wide(t, 256, 0, P, 2); used()
            need(t + 1); wide(t + 1, 256, 0, P, 1); tokens(t + 1, 256, P, P, 8, P); used()
            need(t + 2); wide(t + 2, 256, 0, P, 1); tokens(t + 2, 256, P, P, 8, P); used()
            need(t + 3); tokens(t + 3, 280, 0, 24, 8, 32); wide(t + 3, 280, 24, P, 2); used()
            need(t + 4); wide(t + 4, 256, 0, P, 2); used()
            assert j[0] == J_MIX
            stage(pe, "mixer_in")
            for kv in range(2):
                src = (kc_t, vc_t)[kv]
                t = T_CMP + 2 * kv
                need(t)
                need(t + 1)
                if kv:
                    pe.wait_ge(s.cmp_hid, 2)
                w1 = [slot(t + i)[:, 0:2048].rearrange("p (i n) -> p i n", n=P) for i in range(2)]
                for i in range(32):
                    last = mm(ps[:, 512:513], w1[i // 16][0:64, i % 16, :],
                              cols[0:64, V_POS + 32 * kv + i:V_POS + 32 * kv + i + 1], start=i == 0, stop=i == 31)
                for g in range(2):
                    rows = slice(64 * g, 64 * g + 64)
                    for i in range(32):
                        last = mm(ps[:, 1024 * g:1024 * g + N_CMP], w1[i // 16][rows, i % 16, :],
                                  src[rows, i:i + 16 * (N_CMP - 1) + 1:16], start=i == 0, stop=i == 31)
                last.then_inc(s.cmp_h1, 1)
                used()
                used()
                for g in range(2):
                    pe.wait_ge(s.cmp_hid, 2 * kv + g + 1)
                    if kv:
                        pe.wait_ge(s.cmp_copied, g + 1)
                    if kv == 0:
                        last = mm(ps[0:64, 2048 + 512 * g:2048 + 512 * g + N_CMP], w2s[:, 0, :], hid[:, g, 0:N_CMP],
                                  start=True, stop=True)
                    else:
                        last = mm(ps[0:N_CMP, 2048 + 512 * g:2048 + 512 * g + 64], hid[:, g, 0:N_CMP], w2s[:, 1, :],
                                  start=True, stop=True)
                    last.then_inc(s.cmp_h2, 1)
            stage(pe, "compressed")
            attention(nsa_units, N_FIRST, 1)
            stage(pe, "mixer_attended")
            for n in range(8):
                c_, half = n // 2, n % 2
                if n >= 2:
                    pe.wait_ge(s.turn_copied, len(TURNS) + n - 1)
                for b in range(4):
                    last = pe.transpose(ps[:, 512 * (n % 2) + P * b:512 * (n % 2) + P * b + P],
                                        no[:, 4 * half + b, P * c_:P * c_ + P], ident[:, :])
                last.then_inc(s.turn_done, 1)
            need(T_POOL)
            pe.wait_ge(s.pool_d, 1)
            wp = slot(T_POOL)[:, 0:512].rearrange("p (g e) -> p g e", g=4)
            for g in range(4):
                if g >= 2:
                    pe.wait_ge(s.pool_copied, g - 1)
                for half in range(2):
                    o = 2048 + 1024 * (g % 2) + 512 * half
                    last = mm(ps[:, o:o + 512], wp[:, g, :], u[:, g, 16 + 512 * half:16 + 512 * half + 512],
                              start=True, stop=True)
                last.then_inc(s.pool_mm, 1)
            used()
            stage(pe, "mixer_turned")

            def product(t0, j0, norm=None):
                for i in range(4):
                    t = t0 + i
                    need(t)
                    w = tile_of(t, KC, 256)
                    for m in range(2):
                        feature_chunk(j0 + 2 * i + m, lambda k: w[:, k, P * m:P * m + P], KC, hs, P,
                                      norm if i + m == 0 else None)
                    used()

            def two_kinds(t, m, kind, n, ready, norm=None):
                o_sem, f_sem = ((s.gate_out, s.gate_free), (s.up_out, s.up_free))[kind]
                if m == 0:
                    pe.wait_ge(w_ready[t % 2], ready)
                pe.wait_ge(f_sem, n + 1)
                w = tile_of(t, KC, 256)
                for half in range(2):
                    for k in range(KC):
                        if norm is not None and half == 0:
                            pe.wait_ge(s.h_ok, H_OK[norm] + k + 1)
                        last = mm(bank(2 * kind + half), w[:, k, P * m:P * m + P],
                                  ht[:, k, 512 * half:512 * half + 512], start=k == 0, stop=k == KC - 1)
                last.then_inc(o_sem, 1)
                if m == 1:
                    used()

            product(T_MIX, J_MIX)
            norm_sum(3)
            stage(pe, "x_2")

            def split_mm(o, part_, w, rows, start, stop):
                return mm(o, w, rows, start=start and part_ == 0, stop=stop and part_ == 2)

            def gates_and_ups(l, i, group_, norm=None):
                q = 3 * group_ - 1 if group_ else 0
                n = N_F[l] + 2 * group_
                for kind in range(2):
                    t = T_F[l] + q + kind
                    pe.wait_ge(s.w_split, i * 6 + (G_T * l + q + kind + 1))
                    hi, lo = (w_part[p_][:, t % 2, :].rearrange("p (k n) -> p k n", k=KC) for p_ in range(2))
                    if group_:
                        for m in range(2):
                            pe.wait_ge((s.gate_free, s.up_free)[kind], i * 4 + (n + m))
                            pe.wait_ge(s.down_free, i * 16 + (N_DOWN[l] + 8 * (group_ - 2) + 4 + 2 * kind + m + 1))
                    order = [(k, m, half) for m in range(2) for half in range(2) for k in range(KC)]
                    if norm is not None and kind == 0:
                        order = [(k, m, half) for k in range(KC) for m in range(2) for half in range(2)]
                    for k, m, half in order:
                        if norm is not None and kind == 0 and m + half == 0:
                            pe.wait_ge(s.h_ok, H_OK[norm] + k + 1)
                        for p_, (wp_, rp_) in enumerate(PASSES):
                            last = split_mm(bank(4 * kind + 2 * m + half), p_, (hi, lo)[wp_][:, k, P * m:P * m + P],
                                            h_part[rp_][:, k, 512 * half:512 * half + 512], k == 0, k == KC - 1)
                        if k == KC - 1 and half == 1:
                            last.then_inc((s.gate_out, s.up_out)[kind], 1)

            def downs(l, i, group_, after):
                q = 3 * group_ + 4 if group_ < G_N - 1 else LAST
                pe.wait_ge(s.w_split, i * 6 + (G_T * l + q + 1))
                pe.wait_ge(s.act_ready, i * 4 + (N_A[l] + 2 * group_ + 2))
                t = T_F[l] + q
                hi, lo = (w_part[p_][:, t % 2, :].rearrange("p (k n) -> p k n", k=2) for p_ in range(2))
                for c_ in range(KC):
                    if after and c_ < 4:
                        pe.wait_ge((s.gate_free, s.up_free)[c_ // 2], i * 4 + (N_F[l] + 2 * group_ + 2 + c_ % 2 + 2))
                    else:
                        pe.wait_ge(s.down_free, i * 16 + (N_DOWN[l] + 8 * group_ + c_ - 3))
                    for half in range(2):
                        for k in range(2):
                            for p_, (wp_, rp_) in enumerate(PASSES):
                                last = split_mm(bank(2 * (c_ % 4) + half), p_, (hi, lo)[wp_][:, k, P * c_:P * c_ + P],
                                                act_part[rp_][:, group_ % 2, k, 512 * half:512 * half + 512],
                                                k == 0, k == 1)
                    last.then_inc(s.down_out, 1)

            def ffn(l, norm):
                gates_and_ups(l, 0, 0, norm)
                with nc.tensor.Fori(0, (G_N - 1) // 2) as i:
                    for r in range(2):
                        gates_and_ups(l, i, 1 + r)
                        downs(l, i, r, True)
                downs(l, 0, G_N - 1, False)

            ffn(0, 3)
            norm_sum(4)
            stage(pe, "x_3")
            for i in range(4):
                for m in range(2):
                    for kind in range(2):
                        t = T_PW1 + 2 * i + kind
                        two_kinds(t, m, kind, N_PW + 2 * i + m, arrives[t], 4 if i + m + kind == 0 else None)
            for k in range(KC):
                if k in POOL_CONV:
                    pe.wait_ge(s.zc_ok_pool, POOL_CONV.index(k) + 1)
                else:
                    pe.wait_ge(s.zc_ok, k + 1 - sum(p_ < k for p_ in POOL_CONV))
                for half in range(2):
                    last = mm(bank(4 + half), ones[:, :], zc[:, k, 512 * half:512 * half + 512],
                              start=k == 0, stop=k == KC - 1)
            last.then_inc(s.mean_done, 1)
            stage(pe, "convolved")
            for k in range(KC):
                pe.wait_ge(s.sq_ready, 8 * 5 + k + 1)
                for half in range(2):
                    last = mm(bank(6 + half), ones[:, :], sc[:, k % 2, 512 * half:512 * half + 512],
                              start=k == 0, stop=k == KC - 1)
                last.then_inc(s.sq_used, 1)
            stage(pe, "conv_normed")
            product(T_PW2, J_PW2, norm=5)
            norm_sum(6)
            stage(pe, "x_4")
            ffn(1, 6)
            norm_sum(7)
            stage(pe, "x_5")
            pe.wait_ge(s.h_ok, H_OK[7] + 8)
            for t in range(TB):
                if t >= 2:
                    pe.wait_ge(s.out_ready, t - 1)
                for k in range(KC):
                    last = pe.transpose(ps[:, 1024 * (t % 2) + P * k:1024 * (t % 2) + P * k + P],
                                        ht[:, k, P * t:P * t + P], ident[:, :])
                last.then_inc(s.ft_done, 1)

        @block.scalar
        def _(a):
            f = a.activation
            chained = [0]

            def chain(ins):
                chained[0] += 1
                ins.then_inc(s.act_chain, 1)
                a.wait_ge(s.act_chain, chained[0])

            a.wait_ge(s.cols_ok, 1)
            f(misc[:, 8:16], cols[:, V_C:V_C + 8], ACT.Silu).then_inc(s.c_act, 1)

            def square(n, k, src):
                if 8 * n + k >= 2:
                    a.wait_ge(s.sq_used, 8 * n + k - 1)
                f(sc[:, k % 2, :], src[:, k, :], ACT.Square).then_inc(s.sq_ready, 1)

            def root(n, eps=EPS):
                if n == 5:
                    a.wait_ge(s.sq_used, 8 * n + 8)
                else:
                    a.wait_ge(s.sum_done, n + 1 - (n > 5))
                f(sc[:, 3, :], bank(6, 2), ACT.Sqrt, bias=eps, scale=1.0 / D).then_inc(s.rs_ready, 1)

            for k in range(KC):
                a.wait_ge(s.tr_free, k + 1)
                if k == 0:
                    a.wait_ge(s.tr_done, 1)
                square(0, k, xt)
            root(0)
            stage(a, "loaded")
            for k in range(KC):
                a.wait_ge(s.h_mul, k + 1)
                f(ht[:, k, :], ht[:, k, :], ACT.Identity, bias=misc[:, 16 + k:17 + k]).then_inc(s.h_ok, 1)

            def copy_out(j, jobs):
                for o, m, per, stride, width, func, scale in jobs:
                    a.wait_ge(s.g_out, j + 1)
                    src = bank(2 * (j % 2), 2)[0:m, :]
                    if per:
                        src = src[:, 0:per * stride].rearrange("p (b n) -> p b n", b=per)[:, :, width[0]:width[1]]
                    if len(o[0].shape) == 4:
                        src = src.rearrange("p b (h d) -> p b h d", h=M_H)
                    if len(o) == 1:
                        f(o[0], src, func, scale=scale).then_inc(g_free[j % 2], 1)
                    else:
                        f(o[0], src, func, scale=scale)
                        s2 = bank(2 * (j % 2), 2)[:, 0:per * stride].rearrange("p (b n) -> p b n", b=per)
                        f(o[1], s2[:, :, width[1]:width[1] + 8], func).then_inc(g_free[j % 2], 1)
                    j += 1
                return j

            w8 = A_D ** -0.5
            cp = lambda o, fn=ACT.Copy, sc_=1.0, m=P: ([o], m, 0, 0, None, fn, sc_)
            jobs = [cp(aq[:, i, :], sc_=w8) for i in range(3)] + [cp(ak), ([av], P, 8, P, (0, P), ACT.Copy, 1.0)]
            jobs += [cp(az[:, i, :], ACT.Silu) for i in range(3)]
            jobs += [cp(sq[:, i, :], sc_=w8) for i in range(2)] + [cp(sk[:, i, :]) for i in range(2)]
            jobs += [([sv[:, 4 * i:4 * i + 4, :]], P, 4, S_W, (0, S_W), ACT.Copy, 1.0) for i in range(2)]
            jobs += [cp(sz[:, i, :], ACT.Silu) for i in range(2)]
            assert copy_out(J_IN, jobs) == J_IN2
            stage(a, "attention_in")

            def copy_pt(n, un):
                a.wait_ge(s.pt_done, n + 1)
                if n >= 2:
                    a.wait_ge(s.pv_done, n - 1)
                e = min(P, un.w)
                blocks = (un.w + P - 1) // P
                f(sc[0:e, 2 + n % 2, 0:P * blocks], ps[0:e, 2048:2048 + P * blocks], ACT.Copy).then_inc(s.pt_copied, 1)

            def soft_attention(units, n0):
                N = len(units)
                for i in range(N + 1):
                    if i < N:
                        un, n = units[i], n0 + i
                        a.wait_ge(s.l_done, n + 1)
                        r = stat[:, n % 16, :]
                        if un.sink is not None:
                            f(r[:, 3:4], misc[:, 2 + un.h:3 + un.h], ACT.Exp, bias=r[:, 0:1])
                        f(sc[:, n % 2, 0:un.w], sc[:, n % 2, 0:un.w], ACT.Exp, bias=r[:, 0:1], scale=-1.0,
                          accum_out=r[:, 1:2]).then_inc(s.e_done, 1)
                    if i >= 1:
                        copy_pt(n0 + i - 1, units[i - 1])

            def stick_attention(units, n0):
                N = len(units)
                for i in range(N + 2):
                    if i < N:
                        un, n = units[i], n0 + i
                        a.wait_ge(s.s_done, n + 1)
                        a.wait_ge(s.pt_done, n - 1)
                        row = sc[:, n % 2, 0:un.w]
                        chain(f(row, ps[:, 1024 * (n % 2):1024 * (n % 2) + un.w], ACT.Abs))
                        chain(f(row, row, ACT.Exp, scale=-1.0))
                        f(row, row, ACT.Ln, bias=1.0).then_inc(s.z_ln, 1)
                    if 0 <= i - 1 < N:
                        un, n = units[i - 1], n0 + i - 1
                        a.wait_ge(s.l_done, n + 1)
                        row = sc[:, n % 2, 0:un.w]
                        f(row, row, ACT.Exp).then_inc(s.x_exp, 1)
                    if i - 2 >= 0:
                        copy_pt(n0 + i - 2, units[i - 2])

            soft_attention(swa_units, 0)
            stick_attention(stick_units, N_SWA)
            stage(a, "attended")
            stage(a, "turned")
            jobs = [cp(mu[:, h, 3:S + 3], m=M_D) for h in range(M_H)]
            jobs += [([mv[:, 2 * i:2 * i + 2, :, 0:M_D], gi[:, 2 * i:2 * i + 2, :]], P, 2, 512, (0, M_W), ACT.Copy, 1.0)
                     for i in range(4)]
            jobs += [cp(mz[:, h, :], ACT.Silu, m=M_D) for h in range(M_H)]
            assert copy_out(J_IN2, jobs) == J_OUT
            stage(a, "mlstm_in")
            hr = lambda i: ht[0:4, i, :]
            a.wait_ge(s.rows_a, 1)
            chain(f(hr(2), hr(1), ACT.Abs))
            chain(f(hr(2), hr(2), ACT.Exp, scale=-1.0))
            f(hr(2), hr(2), ACT.Ln, bias=1.0).then_inc(s.rows_b, 1)
            a.wait_ge(s.rows_c, 1)
            f(sc[32:36, 0, :], sc[32:36, 0, :], ACT.Exp)
            f(sc[64:68, 0, :], hr(6), ACT.Exp, scale=-1.0)
            f(sc[96:100, 0, :], sc[96:100, 0, :], ACT.Exp)
            f(mrow[:, 2, :], mrow[:, 2, :], ACT.Exp).then_inc(s.rows_d, 1)
            for h in range(M_H):
                a.wait_ge(s.conv_done, h + 1)
                f(cu[:, h, :], cu[:, h, :], ACT.Silu, bias=cols[0:M_D, V_CB + h:V_CB + h + 1])
            stage(a, "mlstm_rows")
            for n in range(2 * M_H):
                a.wait_ge(s.qk_done, n + 1)
                dst = mq[:, n, :] if n < M_H else mkt[:, n - M_H, :]
                f(dst, ps[0:M_D, 1024 * (n % 2):1024 * (n % 2) + 1024], ACT.Copy,
                  scale=M_D ** -0.5 if n < M_H else 1.0).then_inc(s.qk_copied, 1)
            stage(a, "mlstm_qk")
            for t in range(TB):
                a.wait_ge(s.md_done, t + 1)
                for h in range(M_H):
                    row = sc[:, 3 * (t % 2), P * h:P * h + P]
                    last = f(row, row, ACT.Exp, bias=sc[:, 2, P * t + h:P * t + h + 1])
                last.then_inc(s.mexp_done, 1)
                a.wait_ge(s.mo_done, t + 1)
                if t >= 1:
                    a.wait_ge(s.mstate, t)
                f(intra, ps[:, 2560:2560 + 388], ACT.Copy).then_inc(s.mintra, 1)
            stage(a, "mlstm_scanned")
            for h in range(M_H):
                f(cu[:, h, :], cu[:, h, :], ACT.Copy, scale=cols[0:M_D, V_SKIP + h:V_SKIP + h + 1])
            a.wait_ge(s.ms_sum, 1)
            f(mst[:, 3], mst[:, 2], ACT.Sqrt, bias=EPS, scale=1.0 / M_D).then_inc(s.ms_root, 1)
            stage(a, "mlstm_out")
            for k in range(KC):
                j = J_OUT + k
                copy_out(j, [cp(ht[:, k, :])])
                a.wait_ge(g_free[j % 2], j // 2 + 1)
                square(1, k, ht)
            root(1)
            stage(a, "y_1")
            for k in range(KC):
                a.wait_ge(s.x_add, k + 1)
                square(2, k, xt)
            root(2)
            stage(a, "x_1")
            jobs = []
            for i in range(4):
                jobs.append(([nq[:, i, :]], P, 0, 0, None, ACT.Copy, None))
            jobs += [cp(kc_t), cp(vc_t), cp(ks), ([vs], P, 8, P, (0, P), ACT.Copy, 1.0)]
            jobs += [cp(kw), ([vw], P, 8, P, (0, P), ACT.Copy, 1.0), ([ng], P, 8, 32, (0, 24), ACT.Sigmoid, 1.0)]
            jobs += [cp(u[:, i, 16:S + 16]) for i in range(4)]
            for i in range(4):
                j = J_NIN + i
                a.wait_ge(s.g_out, j + 1)
                src = bank(2 * (j % 2), 2)
                f(nq[0:64, i, :], src[0:64, :], ACT.Copy, scale=N_D ** -0.5 / n_slope(i))
                f(nq[64:128, i, :], src[64:128, :], ACT.Copy, scale=N_D ** -0.5 / n_slope(i + 4)).then_inc(g_free[j % 2], 1)
            assert copy_out(J_NIN + 4, jobs[4:]) == J_MIX
            stage(a, "mixer_in")
            for kv in range(2):
                a.wait_ge(s.cmp_bias, kv + 1)
                if kv:
                    a.wait_ge(s.cmp_h2, 2)
                for g in range(2):
                    f(hid[:, g, 0:N_CMP], ps[:, 1024 * g:1024 * g + N_CMP], ACT.Gelu_apprx_tanh,
                      bias=hbias[:, kv:kv + 1]).then_inc(s.cmp_hid, 1)
            stage(a, "compressed")
            soft_attention(nsa_units, N_FIRST)
            stage(a, "mixer_attended")
            for g in range(4):
                a.wait_ge(s.pool_mm, g + 1)
                f(ht[:, 4 + g, :], ps[:, 2048 + 1024 * (g % 2):3072 + 1024 * (g % 2)], ACT.Copy,
                  scale=cols[:, V_PS + g:V_PS + g + 1]).then_inc(s.pool_copied, 1)
            stage(a, "mixer_turned")

            def product_squares(n, j0):
                for k in range(KC):
                    j = j0 + k
                    a.wait_ge(g_free[j % 2], j // 2 + 1)
                    square(n, k, xt)
                root(n)

            product_squares(3, J_MIX)
            stage(a, "x_2")

            def gates(l, i, group_):
                for m in range(2):
                    n = N_F[l] + 2 * group_ + m
                    a.wait_ge(s.gate_out, i * 4 + (n + 1))
                    if group_:
                        a.wait_ge(s.act_ready, i * 4 + (N_A[l] + 2 * group_ + m - 1))
                    f(sc[:, m, :], bank(2 * m, 2), ACT.Silu).then_inc(s.gate_free, 1)

            def ffn(l, norm):
                for k in range(KC):
                    a.wait_ge(s.h_mul, H_MUL[norm] + k + 1)
                    f(h_part[0][:, k, :], sc[:, k % 2, :], ACT.Copy).then_inc(s.h_hi, 1)
                gates(l, 0, 0)
                with nc.scalar.Fori(0, (G_N - 1) // 2) as i:
                    for r in range(2):
                        gates(l, i, 1 + r)
                for k in range(KC):
                    a.wait_ge(s.down_free, N_DOWN[l] + 8 * (G_N - 1) + k + 1)
                    square(norm + 1, k, xt)
                root(norm + 1)

            a.nop().then_inc(s.gate_free, 1)
            ffn(0, 3)
            stage(a, "x_3")
            for n in range(KC):
                a.wait_ge(s.gate_out, N_PW + n + 1)
                a.wait_ge(s.up_free, N_PW + n + 1)
                f(sg, bank(0, 2), ACT.Sigmoid, bias=cols[:, V_BPW1 + 8 + n:V_BPW1 + 9 + n]).then_inc(s.gate_free, 1)
            a.wait_ge(s.mean_done, 1)
            f(sc[:, 2, :], bank(4, 2), ACT.Copy, scale=1.0 / D).then_inc(s.mean_copied, 1)
            stage(a, "convolved")
            for k in range(KC):
                a.wait_ge(s.xc_done, k + 1)
                square(5, k, zc)
            root(5, LN_EPS)
            for k in range(KC):
                a.wait_ge(s.h_mul, H_MUL[5] + k + 1)
                f(ht[:, k, :], zc[:, k, :], ACT.Silu, bias=cols[:, V_LNB + k:V_LNB + k + 1],
                  scale=cols[:, V_LNG + k:V_LNG + k + 1]).then_inc(s.h_ok, 1)
            stage(a, "conv_normed")
            product_squares(6, J_PW2)
            stage(a, "x_4")
            ffn(1, 6)
            stage(a, "x_5")
            for t in range(TB):
                a.wait_ge(s.ft_done, t + 1)
                if t >= 2:
                    a.wait_ge(out_done[t % 2], 16 * (t // 2))
                f(sc[:, t % 2, :], bank(2 * (t % 2), 2), ACT.Copy).then_inc(s.out_ready, 1)

        @block.vector
        def _(v):
            tt, ts, stt = v.tensor_tensor, v.tensor_scalar, v.scalar_tensor_tensor
            mul, add, sub, mx = ALU.mult, ALU.add, ALU.subtract, ALU.max
            chained = [0]

            def chain(ins):
                chained[0] += 1
                ins.then_inc(s.dve_chain, 1)
                v.wait_ge(s.dve_chain, chained[0])

            v.nop().then_inc(s.up_free, 1)
            for _ in range(KC):
                v.nop().then_inc(s.down_free, 1)

            def sum_square(n, k):
                v.wait_ge(s.sq_ready, 8 * n + k + 1)
                if k == 0:
                    v.tensor_copy(sc[:, 2, :], sc[:, 0, :]).then_inc(s.sq_used, 1)
                else:
                    v.wait_ge(s.sq_used, 8 * n + k)
                    tt(sc[:, 2, :], sc[:, 2, :], sc[:, k % 2, :], add).then_inc(s.sq_used, 1)

            def added_and_squared(n, put):
                for k in range(KC + 1):
                    if k < KC:
                        put(k)
                    if k >= 1:
                        sum_square(n, k - 1)
            v.wait_ge(s.tr_done, 1)
            v.tensor_copy(cols[:, :], ps[:, 0:N_COLS]).then_inc(s.cols_ok, 1)

            def turned(k):
                v.wait_ge(s.tr_done, k + 2)
                v.tensor_copy(xt[:, k, :], bank(2 + 2 * (k % 2), 2)).then_inc(s.tr_free, 1)

            added_and_squared(0, turned)
            v.wait_ge(s.cols_ok, 1)
            v.wait_ge(s.small_in, 80)
            v.tensor_scalar(misc[:, 56:62], misc[:, 2:8], -1.0, None, mul)
            v.wait_ge(s.mod_done, 1)
            chain(tt(misc[:, 16:40], ps[:, 512:536], cols[:, V_BMOD:V_BMOD + 24], add))
            stt(misc[:, 40:48], misc[:, 24:32], 1.0, cols[:, V_GPRE:V_GPRE + 8], add, mul)
            tt(misc[:, 48:56], misc[:, 32:40], cols[:, V_GPOST:V_GPOST + 8], mul)

            def root(n):
                v.wait_ge(s.rs_ready, n + 1)
                chain(v.reciprocal(sc[:, 3, :], sc[:, 3, :]))

            def scaled(src, g0, dst, gains=cols, made=s.h_ok):
                for k in range(KC):
                    stt(dst[:, k, :], src[:, k, :], gains[:, g0 + k:g0 + k + 1], sc[:, 3, :], mul, mul).then_inc(made, 1)

            root(0)
            stage(v, "loaded")
            scaled(xt, 40, ht, misc, s.h_mul)
            stage(v, "attention_in")

            def outputs(n, un):
                r = stat[:, n % 16, :]
                src = ps[:, 3072 + 512 * (n % 2):3136 + 512 * (n % 2)]
                v.wait_ge(s.pv_done, n + 1)
                if un.kind == "stick":
                    v.tensor_copy(un.out, src).then_inc(s.o_done, 1)
                    return
                if un.first:
                    ts(un.out, src, r[:, 2:3], None, mul).then_inc(s.o_done, 1)
                else:
                    v.wait_ge(s.o_done, n)
                    stt(un.out, src, r[:, 2:3], un.out, mul, add).then_inc(s.o_done, 1)

            def sums(n, un):
                r = stat[:, n % 16, :]
                v.wait_ge(s.e_done, n + 1)
                if un.sink is not None:
                    chain(tt(r[:, 1:2], r[:, 1:2], r[:, 3:4], add))
                if un.kind == "cmp" and un.i == 0:
                    chain(ts(r[:, 1:2], r[:, 1:2], 1e-30, None, mx))
                chain(v.reciprocal(r[:, 2:3], r[:, 1:2]))
                if un.kind == "cmp":
                    prob = psum_p[:, un.g, 4:4 + N_CMP]
                    if un.h % 4 == 0:
                        chain(ts(prob, sc[:, n % 2, 0:N_CMP], r[:, 2:3], None, mul))
                    else:
                        chain(stt(prob, sc[:, n % 2, 0:N_CMP], r[:, 2:3], prob, mul, add))
                if un.gate is not None:
                    chain(tt(r[:, 2:3], r[:, 2:3], un.gate, mul))

            def selection(un):
                pp = psum_p[:, un.g, :]
                i0, i1, top, rep = (imp[:, 16 * a_:16 * a_ + 16] for a_ in range(4))
                chain(v.tensor_reduce(i0, pp[:, 4:68].rearrange("p (j n) -> p j n", n=4)[:, :, 0:3], AX.X, add))
                chain(tt(i1, pp[:, 7:68:4], pp[:, 3:64:4], add))
                chain(stt(i0, i1, 0.5, i0, mul, add))
                chain(tt(i0, i0, force[:, un.i, :], add))
                chain(v.max(top[:, 0:8], i0))
                chain(v.match_replace(rep, top[:, 0:8], i0, -BIGF))
                chain(ts(rep, rep, -2e38, NEG, ALU.is_gt, mul))
                nb = 2 * (un.i + 1)
                chain(tt(tg[:, un.g, 0:un.w].rearrange("p (b n) -> p b n", b=nb),
                         causal[:, P * (7 - un.i):P * (7 - un.i) + un.w].rearrange("p (b n) -> p b n", b=nb),
                         rep[:, 0:nb].unsqueeze(2).to_broadcast([P, nb, 64]), add))

            def soft_attention(units, n0):
                N = len(units)
                for i in range(N + 2):
                    if i < N:
                        un, n = units[i], n0 + i
                        if un.kind == "sel" and un.h % 4 == 0:
                            selection(un)
                        v.wait_ge(s.s_done, n + 1)
                        if i >= 2:
                            v.wait_ge(s.pt_done, n - 1)
                        r = stat[:, n % 16, :]
                        first = misc[:, 56 + un.h:57 + un.h] if un.sink is not None else (
                            1e20 if un.kind == "cmp" else BIGF)
                        v.tensor_tensor_reduce(sc[:, n % 2, 0:un.w], un.dist, ps[:, 1024 * (n % 2):1024 * (n % 2) + un.w],
                                               -un.slope, first, add, ALU.min, r[:, 0:1]).then_inc(s.l_done, 1)
                    if 0 <= i - 1 < N:
                        sums(n0 + i - 1, units[i - 1])
                    if i >= 2:
                        outputs(n0 + i - 2, units[i - 2])

            def stick_attention(units, n0):
                N = len(units)
                for i in range(N + 3):
                    if i < N:
                        un, n = units[i], n0 + i
                        v.wait_ge(s.z_ln, n - n0 + 1)
                        row = sc[:, n % 2, 0:un.w]
                        stt(row, ps[:, 1024 * (n % 2):1024 * (n % 2) + un.w], 0.0, row, mx, add).then_inc(s.z_sp, 1)
                    if 0 <= i - 1 < N:
                        un, n = units[i - 1], n0 + i - 1
                        v.wait_ge(s.z_spm, n - n0 + 1)
                        row = sc[:, n % 2, 0:un.w]
                        back = row[:, ::-1]
                        chain(v.tensor_tensor_scan(back, ones[:, 0:1].to_broadcast([P, un.w]), back, 0.0, mul, add))
                        tt(row, ps[:, 1024 * (n % 2):1024 * (n % 2) + un.w], row, sub).then_inc(s.l_done, 1)
                    if i - 3 >= 0:
                        outputs(n0 + i - 3, units[i - 3])

            soft_attention(swa_units, 0)
            stick_attention(stick_units, N_SWA)
            stage(v, "attended")
            for n, (src, c_, half) in enumerate(TURNS):
                v.wait_ge(s.turn_done, n + 1)
                dst = (az if n < 6 else sz)[:, c_, 512 * half:512 * half + 512]
                tt(dst, bank(n % 2), dst, mul).then_inc(s.turn_copied, 1)
            stage(v, "turned")
            stage(v, "mlstm_in")
            hr = lambda i: ht[0:4, i, :]
            chunked = lambda ap: ap.rearrange("p (t n) -> p t n", n=P)
            per = lambda ap: ap.unsqueeze(2).to_broadcast([4, TB, P])
            v.wait_ge(s.gates_up, 1)
            ts(hr(0), ps[0:4, 0:1024], misc[0:4, 0:1], None, add)
            ts(hr(1), ps[0:4, 1024:2048], misc[0:4, 1:2], None, add).then_inc(s.rows_a, 1)
            v.memset(hr(4), 1.0)
            chain(v.memset(sc[:, 0, :], 0.0))
            chain(v.memset(hr(4)[:, 0:S:P], 0.0))
            v.wait_ge(s.rows_b, 1)
            chain(stt(hr(3), hr(1), 0.0, hr(2), ALU.min, sub))
            v.tensor_tensor_scan(hr(5), hr(4), hr(3), 0.0, mul, add)
            chain(v.tensor_tensor_scan(hr(6), hr(3), hr(0), 0.0, add, mx))
            chain(tt(sc[0:4, 0, :], hr(0), hr(5), sub))
            tt(sc[0:4, 1, :], hr(5), hr(6), sub)
            v.memset(mrow[:, 0, 0:1], 0.0)
            v.tensor_copy(mrow[:, 0, 1:TB], hr(6)[:, P - 1:S - P:P])
            chain(tt(mrow[:, 1, :], hr(5)[:, P - 1:S:P], hr(6)[:, P - 1:S:P], sub))
            chain(tt(mrow[:, 2, :], mrow[:, 1, :], mrow[:, 0, :], add))
            tt(chunked(sc[32:36, 0, :]), chunked(sc[0:4, 1, :]), per(mrow[:, 0, :]), add)
            tt(chunked(sc[96:100, 0, :]), chunked(sc[0:4, 0, :]), per(mrow[:, 1, :]), add).then_inc(s.rows_c, 1)
            for h in range(M_H):
                w = lambda t: cols[0:M_D, V_CW + 4 * t + h:V_CW + 4 * t + h + 1]
                chain(ts(cu[:, h, :], mu[:, h, 0:S], w(0), None, mul))
                for t in range(1, M_CONV):
                    ins = stt(cu[:, h, :], mu[:, h, t:t + S], w(t), cu[:, h, :], mul, add)
                    if t < M_CONV - 1:
                        chain(ins)
                ins.then_inc(s.conv_done, 1)
            v.wait_ge(s.rowcols, 1)
            v.tensor_copy(sc[:, 2, :], bank(4, 2))
            v.tensor_copy(car.rearrange("p h t -> p (h t)"), ps[:, 3072:3072 + M_H * TB])
            stage(v, "mlstm_rows")
            rc = sc[:, 2, :].rearrange("p (t n) -> p t n", n=P)
            for t in range(TB):
                v.wait_ge(s.ktok_done, t + 1)
                o = 2048 + 512 * (t % 2)
                tt(mk[:, t], ps[:, o:o + M_W].rearrange("p (h d) -> p h d", h=M_H),
                   rc[:, t, 96:100].unsqueeze(2).to_broadcast([P, M_H, M_D]), mul).then_inc(s.ktok_copied, 1)
            stage(v, "mlstm_qk")
            for t in range(TB):
                v.wait_ge(s.ms_done, t + 1)
                if t >= 2:
                    v.wait_ge(s.mo_done, t - 1)
                row = sc[:, 3 * (t % 2), 0:512].rearrange("p (h n) -> p h n", h=M_H)
                sl = lambda b: ps[:, 512 * b:512 * b + 512].rearrange("p (h n) -> p h n", h=M_H)
                tt(row, sl(2 + t % 2), tri[:, :].unsqueeze(1).to_broadcast([P, M_H, P]), add).then_inc(s.md_done, 1)
                v.wait_ge(s.mexp_done, t + 1)
                tt(row, sl(t % 2), row, mul).then_inc(s.ms_weighted, 1)
                v.wait_ge(s.mo_done, t + 1)
                for h in range(M_H):
                    stt(ct[:, h, :], ct[:, h, :], car[0:M_D, h, t:t + 1], ps[0:M_D, 3072 + 97 * h:3169 + 97 * h], mul, add)
                v.wait_ge(s.mintra, t + 1)
                for h in range(M_H):
                    last = stt(mv[:, t, h, :], ps[:, 2048 + 97 * h:2145 + 97 * h], rc[:, t, 32 + h:33 + h],
                               intra[:, h, :], mul, add)
                last.then_inc(s.mstate, 1)
            stage(v, "mlstm_scanned")
            hn = mv.rearrange("p t h d -> p (t h) d")
            m0, m1, m2, m3 = (mst[:, i] for i in range(4))
            f0, f1, f2, f3 = (m.rearrange("p t h -> p (t h)") for m in (m0, m1, m2, m3))
            wide = lambda m: m.unsqueeze(2).to_broadcast([P, TB * M_H, M_D])
            chain(stt(f0, hn[:, :, M_D], -1.0, hn[:, :, M_D], mul, mx))
            chain(tt(m0, m0, rc[:, :, 64:68], mx))
            chain(v.reciprocal(f1, f0))
            chain(tt(hn[:, :, 0:M_D], hn[:, :, 0:M_D], wide(f1), mul))
            sqs = ht[:, 4:7, :].rearrange("p a b -> p (a b)").rearrange("p (a d) -> p a d", d=M_D)
            chain(tt(sqs, hn[:, :, 0:M_D], hn[:, :, 0:M_D], mul))
            v.tensor_reduce(f2, sqs, AX.X, add).then_inc(s.ms_sum, 1)
            v.wait_ge(s.ms_root, 1)
            chain(v.reciprocal(f1, f3))
            tt(hn[:, :, 0:M_D], hn[:, :, 0:M_D], wide(f1), mul).then_inc(s.ht_ready, 1)
            for n in range(2 * M_H):
                h, half = n // 2, n % 2
                c_ = slice(512 * half, 512 * half + 512)
                v.wait_ge(s.ht_done, n + 1)
                if n == 0:
                    v.wait_ge(s.ms_root, 1)
                tmp = sc[0:M_D, 3, c_]
                stt(tmp, ps[0:M_D, 512 * (n % 2):512 * (n % 2) + 512], cols[0:M_D, V_NG + h:V_NG + h + 1],
                    cu[:, h, c_], mul, add).then_inc(s.ht_copied, 1)
                v.wait_ge(s.ht_copied, n + 1)
                tt(mz[:, h, c_], tmp, mz[:, h, c_], mul)
            stage(v, "mlstm_out")
            for k in range(KC):
                sum_square(1, k)
            root(1)
            stage(v, "y_1")

            def first_added(k):
                chain(stt(ht[:, k, :], ht[:, k, :], misc[:, 48 + k:49 + k], sc[:, 3, :], mul, mul))
                tt(xt[:, k, :], xt[:, k, :], ht[:, k, :], add).then_inc(s.x_add, 1)

            added_and_squared(2, first_added)
            root(2)
            stage(v, "x_1")
            scaled(xt, V_MIX, ht)
            stage(v, "mixer_in")
            for kv in range(2):
                v.wait_ge(s.cmp_h1, kv + 1)
                v.tensor_copy(hbias[:, kv:kv + 1], ps[:, 512:513]).then_inc(s.cmp_bias, 1)
                for g in range(2):
                    v.wait_ge(s.cmp_h2, 2 * kv + g + 1)
                    src = ps[:, 2048 + 512 * g:2048 + 512 * g + 64]
                    if kv == 0:
                        ins = v.tensor_copy(kcmp[64 * g:64 * g + 64, 0:N_CMP], src[0:64, 0:N_CMP])
                    else:
                        ins = v.tensor_copy(vcmp[:, g, :], src[0:N_CMP, :])
                    ins.then_inc(s.cmp_copied, 1)
            v.memset(psum_p, 0.0)
            v.reciprocal(pw_rc, pw_rc)
            stage(v, "compressed")
            soft_attention(nsa_units, N_FIRST)
            stage(v, "mixer_attended")
            for n in range(8):
                c_, half = n // 2, n % 2
                v.wait_ge(s.turn_done, len(TURNS) + n + 1)
                v.tensor_copy(ht[:, c_, 512 * half:512 * half + 512], bank(n % 2)).then_inc(s.turn_copied, 1)
            stage(v, "mixer_turned")

            def add_product(j0, bias, norm):
                def put(k):
                    j = j0 + k
                    v.wait_ge(s.g_out, j + 1)
                    src = bank(2 * (j % 2), 2)
                    if bias is None:
                        ins = tt(xt[:, k, :], src, xt[:, k, :], add)
                    else:
                        ins = stt(xt[:, k, :], src, cols[:, bias + k:bias + k + 1], xt[:, k, :], add, add)
                    ins.then_inc(g_free[j % 2], 1)
                added_and_squared(norm, put)
                root(norm)

            add_product(J_MIX, None, 3)
            stage(v, "x_2")

            def split_tile(l, i, q):
                t = T_F[l] + q
                v.wait_ge(w_ready[t % 2], i * 48 + arrives[t])
                raw = slot(t)[:, 0:KC * GC]
                v.tensor_copy(w_part[0][:, t % 2, :], raw).then_inc(s.w_hi, 1)
                v.wait_ge(s.w_hi, i * 6 + (G_T * l + q + 1))
                tt(w_part[1][:, t % 2, :], raw, w_part[0][:, t % 2, :].bitcast(F32), sub).then_inc(s.w_split, 1)

            def hidden(l, i, group_):
                for m in range(2):
                    n, c_ = N_F[l] + 2 * group_ + m, N_A[l] + 2 * group_ + m
                    v.wait_ge(s.up_out, i * 4 + (n + 1))
                    v.wait_ge(s.gate_free, i * 4 + (n + 2))
                    row = sc[:, 2 + m, :]
                    hi, lo = (act_part[p_][:, group_ % 2, m, :] for p_ in range(2))
                    tt(row, bank(4 + 2 * m, 2), sc[:, m, :], mul).then_inc(s.up_free, 1)
                    v.wait_ge(s.up_free, i * 4 + (n + 2))
                    v.tensor_copy(hi, row).then_inc(s.act_hi, 1)
                    v.wait_ge(s.act_hi, i * 4 + (c_ + 1))
                    tt(lo, row, hi.bitcast(F32), sub).then_inc(s.act_ready, 1)

            def add_down(l, i, group_, k):
                v.wait_ge(s.down_out, i * 16 + (N_DOWN[l] - 8 + 8 * group_ + k + 1))
                v.wait_ge(s.down_free, i * 16 + (N_DOWN[l] + 8 * (group_ - 1) + k + 1))
                tt(xt[:, k, :], bank(2 * (k % 4), 2), xt[:, k, :], add).then_inc(s.down_free, 1)

            def middle(l, i, group_, add_before=True):
                q = 3 * group_ - 1
                split_tile(l, i, q)
                if add_before:
                    for k in range(KC):
                        add_down(l, i, group_ - 2, k)
                split_tile(l, i, q + 1)
                v.wait_ge(s.gate_out, i * 4 + (N_F[l] + 2 * group_ + 2))
                split_tile(l, i, q + 2)
                hidden(l, i, group_)

            def ffn(l, norm, gain):
                t0 = T_F[l]
                split_tile(l, 0, 0)
                for k in range(KC + 1):
                    if k < KC:
                        if k >= 2:
                            v.wait_ge(s.h_ok, H_OK[norm] + k - 1)
                        stt(sc[:, k % 2, :], xt[:, k, :], cols[:, gain + k:gain + k + 1], sc[:, 3, :], mul, mul)\
                            .then_inc(s.h_mul, 1)
                    if k >= 1:
                        v.wait_ge(s.h_hi, 8 * l + k)
                        tt(h_part[1][:, k - 1, :], sc[:, (k - 1) % 2, :], h_part[0][:, k - 1, :].bitcast(F32), sub)\
                            .then_inc(s.h_ok, 1)
                split_tile(l, 0, 1)
                hidden(l, 0, 0)
                middle(l, 0, 1, add_before=False)
                middle(l, 0, 2)
                with nc.vector.Fori(0, (G_N - 3) // 2) as i:
                    for r in range(2):
                        middle(l, i, 3 + r)
                split_tile(l, 0, LAST)
                for k in range(KC):
                    add_down(l, 0, G_N - 2, k)
                added_and_squared(norm + 1, lambda k: add_down(l, 0, G_N - 1, k))
                root(norm + 1)

            ffn(0, 3, V_FFN)
            stage(v, "x_3")
            scaled(xt, V_MIX + 8, ht)
            taps = lambda t, n: cols[:, V_WDW + 8 * t + n:V_WDW + 8 * t + n + 1]
            v.wait_ge(s.pad_ok, 1)
            for n in range(KC):
                v.wait_ge(s.up_out, N_PW + n + 1)
                v.wait_ge(s.gate_free, N_PW + n + 2)
                stt(zp[:, n, CONV_W - 1:], bank(2, 2), cols[:, V_BPW1 + n:V_BPW1 + n + 1], sg, add, mul)\
                    .then_inc(s.up_free, 1)
                if n not in POOL_CONV:
                    v.wait_ge(s.up_free, N_PW + n + 2)
                    for t in range(CONV_W):
                        if t == 0:
                            ins = ts(zc[:, n, :], zp[:, n, 0:S], taps(0, n), cols[:, V_BDW + n:V_BDW + n + 1], mul, add)
                        else:
                            ins = stt(zc[:, n, :], zp[:, n, t:t + S], taps(t, n), zc[:, n, :], mul, add)
                        if t < CONV_W - 1:
                            chain(ins)
                    ins.then_inc(s.zc_ok, 1)
            stage(v, "convolved")
            v.wait_ge(s.mean_copied, 1)
            for k in range(KC):
                tt(zc[:, k, :], zc[:, k, :], sc[:, 2, :], sub).then_inc(s.xc_done, 1)
            root(5)
            for k in range(KC):
                tt(zc[:, k, :], zc[:, k, :], sc[:, 3, :], mul).then_inc(s.h_mul, 1)
            stage(v, "conv_normed")
            add_product(J_PW2, V_BPW2, 6)
            stage(v, "x_4")
            ffn(1, 6, V_FFN + 8)
            stage(v, "x_5")
            scaled(xt, V_FINAL, ht)

        @block.gpsimd
        def _(g):
            chained = [0]

            def chain(ins):
                chained[0] += 1
                ins.then_inc(s.pool_chain, 1)
                g.wait_ge(s.pool_chain, chained[0])

            def select(o, pattern, op, fill, base, mult):
                return g.affine_select(out=o, in_=o, pattern=pattern, compare_op=op, fill=fill, base=base,
                                       channel_multiplier=mult)

            g.memset(sc[:, 0, 384:512], 0.0).then_inc(s.const_ok, 1)
            g.memset(ones[:, :], 1.0)
            chain(g.memset(ident[:, :], 0.0))
            select(ident[:, :], [[-1, P]], ALU.not_equal, 1.0, 0, 1).then_inc(s.const_ok, 1)
            dist = ht[:, 0, 0:256]
            chain(g.iota(dist, [[-1, 256]], base=P, channel_multiplier=1, allow_small_or_imprecise_dtypes=True))
            for h in range(A_H):
                o = swa_bias[:, 256 * h:256 * h + 256]
                chain(g.tensor_scalar(o, dist, -a_slope(h), 0.0, ALU.mult, ALU.add))
                chain(select(o, [[-1, 256]], ALU.is_ge, NEG, P, 1))
                chain(select(o, [[1, 256]], ALU.is_gt, NEG, 0, -1))
            chain(g.memset(tri[:, :], 0.0))
            chain(select(tri[:, :], [[1, P]], ALU.is_ge, NEG, 0, -1))
            stage(g, "loaded")
            stage(g, "attention_in")
            for i, un in enumerate(stick_units):
                n = N_SWA + i

                def strict(sem_):
                    d = sc[:, n % 2, un.w - P:un.w]
                    select(d, [[-1, P]], ALU.is_gt, 0.0, 0, 1).then_inc(sem_, 1)
                g.wait_ge(s.z_sp, i + 1)
                strict(s.z_spm)
                if i >= 1:
                    stick_weights(g, i - 1)
            stick_weights(g, len(stick_units) - 1)
            stage(g, "attended")
            stage(g, "turned")
            g.memset(selr, 0.0)
            chain(g.memset(ct, 0.0))
            for h in range(M_H):
                chain(select(selr[:, h, :], [[0, P]], ALU.not_equal, 1.0, -h, 1))
            chain(g.memset(mu[:, :, 0:3], 0.0))
            chain(g.memset(mv[:, :, :, M_D], 1.0))
            stage(g, "mlstm_in")
            chain(g.iota(causal[:, :], [[1, S]], base=P - S, channel_multiplier=-1, allow_small_or_imprecise_dtypes=True))
            chain(select(causal[:, :], [[-1, S]], ALU.is_ge, NEG, S - P, 1))
            chain(g.iota(band[:, :], [[1, 640]], base=-512, channel_multiplier=-1, allow_small_or_imprecise_dtypes=True))
            chain(select(band[:, :], [[-1, 640]], ALU.is_ge, NEG, 512, 1))
            chain(select(band[:, :], [[1, 640]], ALU.is_gt, NEG, 0, -1))
            stage(g, "mlstm_rows")
            stage(g, "mlstm_qk")
            stage(g, "mlstm_scanned")
            stage(g, "mlstm_out")
            stage(g, "y_1")
            stage(g, "x_1")
            flat = cdist.rearrange("p a b -> p (a b)")
            chain(g.iota(flat, [[-P, TB], [16, N_CMP]], base=31, channel_multiplier=-1, allow_small_or_imprecise_dtypes=True))
            chain(select(cdist, [[P, TB], [-16, N_CMP]], ALU.is_ge, NEG, -31, 1))
            chain(g.memset(force, 0.0))
            for hb in range(2):
                o = force[64 * hb:64 * hb + 64]
                chain(select(o, [[2, TB], [-1, 16]], ALU.not_equal, 1e4, hb, 0))
                chain(select(o, [[2, TB], [-1, 16]], ALU.not_equal, 1e4, hb - 1, 0))
                chain(select(o, [[0, TB], [1, 16]], ALU.not_equal, 1e4, 0, 0))
                chain(select(o, [[2, TB], [-1, 16]], ALU.is_ge, NEG, hb, 0))
            chain(g.iota(pw_rc, [[1, 16]], base=1, channel_multiplier=0, allow_small_or_imprecise_dtypes=True))
            chain(g.memset(u[:, :, 0:16], 0.0))
            stage(g, "mixer_in")
            stage(g, "compressed")
            ta = ht[:, 0:2, :].rearrange("p a b -> p (a b)")
            tb = ht[:, 2:4, :].rearrange("p a b -> p (a b)")
            chain(g.memset(ta[:, 0:16], 0.0))
            chain(g.memset(tb[:, 0:16], 0.0))
            for gi_ in range(4):
                w = 2 ** (gi_ + 1)
                src, step = u[:, gi_, :], 1
                for k in range(gi_ + 1):
                    dst = (ta, tb)[k % 2]
                    chain(g.tensor_tensor(dst[:, 16:16 + S], src[:, 16:16 + S], src[:, 16 - step:16 - step + S], ALU.add))
                    src, step = dst, 2 * step
                rcw = pw_rc[:, 0:w]
                tw = misc[:, 192:192 + w]
                chain(g.tensor_scalar(tw, rcw, float(w), 1.0, ALU.mult, ALU.max))
                chain(g.tensor_tensor(src[:, 16:16 + w], src[:, 16:16 + w], tw, ALU.mult))
                chain(g.tensor_scalar(src[:, 16:16 + S], src[:, 16:16 + S], 1.0 / w, 1.0, ALU.mult, ALU.mult))
                chain(g.tensor_tensor(u[:, gi_, 16:16 + S], src[:, 16:16 + S], u[:, gi_, 16:16 + S], ALU.subtract))
            g.nop().then_inc(s.pool_d, 1)
            stage(g, "mixer_attended")
            stage(g, "mixer_turned")
            stage(g, "x_2")
            stage(g, "x_3")
            g.memset(zp[:, :, 0:CONV_W - 1], 0.0).then_inc(s.pad_ok, 1)
            g.wait_ge(s.pad_ok, 1)
            for n in POOL_CONV:
                g.wait_ge(s.up_free, N_PW + n + 2)
                taps = lambda t: cols[:, V_WDW + 8 * t + n:V_WDW + 8 * t + n + 1]
                chain(g.tensor_scalar(zc[:, n, :], zp[:, n, 0:S], taps(0), cols[:, V_BDW + n:V_BDW + n + 1],
                                      ALU.mult, ALU.add))
                for t in range(1, CONV_W):
                    chain(g.tensor_scalar(ptmp, zp[:, n, t:t + S], taps(t), 1.0, ALU.mult, ALU.mult))
                    chain(g.tensor_tensor(zc[:, n, :], zc[:, n, :], ptmp, ALU.add))
                g.nop().then_inc(s.zc_ok_pool, 1)
            stage(g, "convolved")
            for name in STAGES[STAGES.index("convolved") + 1:]:
                stage(g, name)


_INS = ["x", "c", "w_mod", "b_mod", "g_pre", "g_post", "w_in", "m_conv_w", "m_conv_b", "m_wq", "m_wk", "m_b_i", "m_b_f",
        "m_norm_g", "m_skip", "a_sinks", "w_out", "mix_norm_2", "ffn_norm_2", "nsa_w_in_2", "cmp_pos_k_2",
        "cmp_pos_v_2", "cmp_k_w1_2", "cmp_k_w2_2", "cmp_v_w1_2", "cmp_v_w2_2", "pool_w_2", "pool_scale_2",
        "mix_w_out_2", "conv_w_pw1_2", "conv_b_pw1_2", "conv_w_dw_2", "conv_b_dw_2", "conv_ln_g_2", "conv_ln_b_2",
        "conv_w_pw2_2", "conv_b_pw2_2", "ffn_w_gate_2", "ffn_w_up_2", "ffn_w_down_2", "final_norm_2"]
_OUTS = [((1, S, D), "float32")]


def kernel(**inputs):
    import numpy as _np
    import concourse.bacc as _bacc
    from concourse import mybir as _mybir
    from concourse.bass_utils import run_bass_kernel_spmd as _run

    nc = _bacc.Bacc("TRN2", target_bir_lowering=False, num_devices=1)
    arrays, args = {}, []
    for name in _INS:
        a = _np.ascontiguousarray(inputs[name])
        arrays[f"in_{name}_dram"] = a
        args.append(nc.dram_tensor(f"in_{name}_dram", a.shape, _mybir.dt.from_np(a.dtype), kind="ExternalInput").ap())
    for i, (shape, dtype) in enumerate(_OUTS):
        dt = _mybir.dt.from_np(_np.dtype(dtype))
        args.append(nc.dram_tensor(f"out_{i}_dram", shape, dt, kind="ExternalOutput").ap())
    build(nc, *args)
    r = _run(nc, [arrays], core_ids=[0])
    return r.results[0]["out_0_dram"]
```

```python
import concourse.bass as bass
from concourse import mybir
from contextlib import ExitStack

F32 = mybir.dt.float32
F32R = mybir.dt.float32r
ALU = mybir.AluOpType
ACT = mybir.ActivationFunctionType
AX = mybir.AxisListType

P = 128
S = 1024
D = 1024
KC = D // P
TB = S // P
EPS = 1e-6
LN_EPS = 1e-5
NEG = -1e30
BIGF = 3e38

M_H, M_D, M_CONV = 4, 96, 4
M_W = M_H * M_D
A_H, A_D, A_W, A_KVW = 6, 64, 384, 128
S_H, S_D, S_W = 4, 64, 256
C_MU, C_MVG, C_MZ = 0, M_W, 2 * M_W + 2 * M_H
C_AQ = C_MZ + M_W
C_AK = C_AQ + A_W
C_AZ = C_AK + 2 * A_KVW
C_SQ = C_AZ + A_W
C_SK, C_SV, C_SZ = C_SQ + S_W, C_SQ + 2 * S_W, C_SQ + 3 * S_W
VGW = M_W + 2 * M_H

N_H, N_G, N_D = 8, 2, 64
N_CMP = 63
FF = 2816
FC = FF // P
CONV_W = 31
GC = 256
G_N = FF // GC
G_T = 3 * G_N
SLOT = KC * VGW

(V_C, V_BMOD, V_GPRE, V_GPOST, V_MIX, V_FFN, V_BPW1, V_BDW, V_LNG, V_LNB, V_BPW2) = (
    0, 8, 32, 40, 48, 64, 80, 96, 104, 112, 120)
V_WDW, V_FINAL = 128, 376
V_CW, V_CB, V_NG, V_SKIP, V_PS = 384, 400, 404, 408, 412
V_POS = 416
N_COLS = 448


class Signals:
    pass


class Unit:
    pass


def build(nc, x, c, w_mod, b_mod, g_pre, g_post, w_in, m_conv_w, m_conv_b, m_wq, m_wk, m_b_i, m_b_f,
          m_norm_g, m_skip, a_sinks, w_out, mix_norm_2, ffn_norm_2, nsa_w_in_2, cmp_pos_k_2,
          cmp_pos_v_2, cmp_k_w1_2, cmp_k_w2_2, cmp_v_w1_2, cmp_v_w2_2, pool_w_2, pool_scale_2,
          mix_w_out_2, conv_w_pw1_2, conv_b_pw1_2, conv_w_dw_2, conv_b_dw_2, conv_ln_g_2,
          conv_ln_b_2, conv_w_pw2_2, conv_b_pw2_2, ffn_w_gate_2, ffn_w_up_2, ffn_w_down_2,
          final_norm_2, out):
    with ExitStack() as ctx:
        def sb(name, shape):
            return ctx.enter_context(nc.sbuf_tensor(name, shape, F32))

        def sem(name):
            return ctx.enter_context(nc.semaphore(name))

        xt = sb("xt", [P, KC, S])
        ring = sb("ring", [P, 2, SLOT])
        sc = sb("sc", [P, 4, S])
        cols = sb("cols", [P, N_COLS])
        ident = sb("ident", [P, P])
        ones = sb("ones", [P, P])
        with ExitStack() as other:
            ht = other.enter_context(nc.sbuf_tensor("ht", [P, KC, S], F32))
            big = other.enter_context(nc.sbuf_tensor("big", [P, FC * S], F32))
            dists = other.enter_context(nc.sbuf_tensor("dists", [P, S + 640], F32))
            tri = other.enter_context(nc.sbuf_tensor("tri", [P, P], F32))
        h_part = [ctx.enter_context(nc.sbuf_tensor("h_" + part_, [P, KC, S], F32R)) for part_ in ("high", "low")]
        w_part = [ctx.enter_context(nc.sbuf_tensor("w_" + part_, [P, 2, KC * GC], F32R)) for part_ in ("high", "low")]
        act_part = [ctx.enter_context(nc.sbuf_tensor("act_" + part_, [P, 2, 2, S], F32R)) for part_ in ("high", "low")]
        PASSES = ((0, 0), (1, 0), (0, 1))
        swa_bias = dists[:, 0:256 * A_H]
        causal = dists[:, 0:S]
        band = dists[:, S:S + 640]
        stat = sb("stat", [P, 16, 4])
        misc = sb("misc", [P, 256])
        ps = ctx.enter_context(nc.psum_tensor("ps", [P, 4096], F32))

        def bank(b, n=1):
            return ps[:, 512 * b:512 * (b + n)]

        def part(a, shape=None, parts=P):
            n = 1
            for s_ in shape:
                n *= s_
            v = big[0:parts, a:a + n]
            if len(shape) == 2:
                return v.rearrange("p (a b) -> p a b", a=shape[0])
            if len(shape) == 3:
                return v.rearrange("p (a b c) -> p a b c", a=shape[0], b=shape[1])
            return v

        mod_sum = part(KC * D, (3 * D,))
        az = part(0, (3, S))
        sz = part(3072, (2, S))
        aq = part(5120, (3, S))
        ak = part(8192, (S,))
        av = part(9216, (TB, P))
        sq = part(10240, (2, S))
        sk = part(12288, (2, S))
        sv = part(14336, (TB, S_W))
        first_rows = part(16384, (4, S))
        keep = part(20480, (2, S))
        cu = part(5120, (M_H, S), M_D)
        mz = part(9216, (M_H, S), M_D)
        mu = part(13312, (M_H, S + 3), M_D)
        mq = part(13312, (M_H, S), M_D)
        mv = part(17420, (TB, M_H, M_D + 1))
        gi = part(20524, (TB, 8))
        ct = part(20588, (M_H, M_D + 1), M_D)
        intra = part(20976, (M_H, M_D + 1))
        selr = part(21364, (M_H, P), 4)
        car = part(21876, (M_H, TB))
        mrow = part(21908, (3, TB), 4)
        mst = part(21932, (4, TB, M_H))
        second_rows = ht[:, 4:8, :]
        left = sc[:, 0:2, :]
        mkt = ht[0:M_D, 0:4, :]
        mk = ht[:, 4:7, :].rearrange("p a b -> p (a b)").rearrange("p (t h d) -> p t h d", t=TB, h=M_H)
        nq = part(0, (4, S))
        ks = part(6144, (S,))
        kw = part(7168, (S,))
        vs = part(8192, (TB, P))
        vw = part(9216, (TB, P))
        u = part(10240, (4, S + 16))
        no = part(14400, (4, S))
        pairs_k = part(14400, (2, S))
        pairs_v = part(16448, (2, S))
        tg = part(18496, (2, S))
        ng = part(20544, (TB, 24))
        kcmp = part(20736, (N_CMP + 1,))
        vcmp = part(20800, (N_G, N_D), N_CMP)
        hid = part(20928, (2, N_CMP + 1))
        hbias = part(21056, (2,))
        cdist = part(21060, (TB, N_CMP))
        force = part(21568, (TB, 16))
        imp = part(21696, (16 * 6,))
        psum_p = part(21792, (2, 68))
        w2s = misc[:, 64:192].rearrange("p (w d) -> p w d", w=2)
        pw_rc = part(22064, (16,))
        zp = part(0, (KC, S + CONV_W - 1))
        zc = part(8432, (KC, S))
        tap_diag = sc[:, :, :].rearrange("p a b -> p (a b)")[:, 0:CONV_W * P].rearrange("p (t n) -> p t n", t=CONV_W)
        sg = part(16624, (S,))
        ptmp = part(17648, (S,))

        s = Signals()
        s.w_used = sem("w_used")
        s.par_in = sem("par_in")
        s.x_in = sem("x_in")
        s.small_in = sem("small_in")
        s.const_ok = sem("const_ok")
        s.stage_end = sem("stage_end")
        s.tr_done = sem("tr_done")
        s.tr_free = sem("tr_free")
        s.cols_ok = sem("cols_ok")
        s.c_act = sem("c_act")
        s.mod_done = sem("mod_done")
        s.sq_ready = sem("sq_ready")
        s.sq_used = sem("sq_used")
        s.rs_ready = sem("rs_ready")
        s.sum_done = sem("sum_done")
        s.h_mul = sem("h_mul")
        s.h_hi = sem("h_hi")
        s.h_ok = sem("h_ok")
        s.x_add = sem("x_add")
        s.w_hi = sem("w_hi")
        s.w_split = sem("w_split")
        s.act_hi = sem("act_hi")
        s.act_ready = sem("act_ready")
        s.pad_ok = sem("pad_ok")
        s.diag_ok = sem("diag_ok")
        s.conv_out = sem("conv_out")
        s.zc_ok_pe = sem("zc_ok_pe")
        s.zc_ok = sem("zc_ok")
        s.zc_ok_pool = sem("zc_ok_pool")
        s.g_out = sem("g_out")
        s.dve_chain = sem("dve_chain")
        s.act_chain = sem("act_chain")
        s.pool_chain = sem("pool_chain")
        s.gate_out = sem("gate_out")
        s.gate_free = sem("gate_free")
        s.up_out = sem("up_out")
        s.up_free = sem("up_free")
        s.down_out = sem("down_out")
        s.down_free = sem("down_free")
        s.s_done = sem("s_done")
        s.l_done = sem("l_done")
        s.e_done = sem("e_done")
        s.pt_done = sem("pt_done")
        s.pt_copied = sem("pt_copied")
        s.pv_done = sem("pv_done")
        s.exp_done = sem("exp_done")
        s.o_free = sem("o_free")
        s.z_masked = sem("z_masked")
        s.gates_up = sem("gates_up")
        s.rows_a = sem("rows_a")
        s.rows_b = sem("rows_b")
        s.rows_c = sem("rows_c")
        s.rows_d = sem("rows_d")
        s.rowcols = sem("rowcols")
        s.mu_pad = sem("mu_pad")
        s.conv_done = sem("conv_done")
        s.qk_done = sem("qk_done")
        s.qk_copied = sem("qk_copied")
        s.ktok_done = sem("ktok_done")
        s.ktok_copied = sem("ktok_copied")
        s.ms_done = sem("ms_done")
        s.md_done = sem("md_done")
        s.mexp_done = sem("mexp_done")
        s.ms_weighted = sem("ms_weighted")
        s.mo_done = sem("mo_done")
        s.mintra = sem("mintra")
        s.mstate = sem("mstate")
        s.ms_sum = sem("ms_sum")
        s.ms_root = sem("ms_root")
        s.ht_ready = sem("ht_ready")
        s.ht_done = sem("ht_done")
        s.ht_copied = sem("ht_copied")
        s.pw_made = sem("pw_made")
        s.cmp_h1 = sem("cmp_h1")
        s.cmp_bias = sem("cmp_bias")
        s.cmp_hid = sem("cmp_hid")
        s.cmp_h2 = sem("cmp_h2")
        s.cmp_copied = sem("cmp_copied")
        s.pool_d = sem("pool_d")
        s.pool_mm = sem("pool_mm")
        s.pool_copied = sem("pool_copied")
        s.mean_done = sem("mean_done")
        s.mean_copied = sem("mean_copied")
        s.xc_done = sem("xc_done")
        s.ft_done = sem("ft_done")
        s.out_ready = sem("out_ready")
        w_ready = [sem("w_ready0"), sem("w_ready1")]
        g_free = [sem("g_free0"), sem("g_free1")]
        out_done = [sem("out_done0"), sem("out_done1")]

        tiles = [1] * 8
        T_IN = len(tiles)
        tiles += [6, 2, 1, 1, 2, 1, 1, 1, 1]
        T_QK = len(tiles)
        tiles += [2]
        T_OUT = len(tiles)
        tiles += [2] * 4
        T_NIN = len(tiles)
        NIN_TILES = "kv_c w1 q q w1 k v u u".split()
        tiles += [{"kv_c": 1, "w1": 1, "q": 4, "k": 2, "v": 2, "u": 1}[kind] for kind in NIN_TILES]
        T_POOL = len(tiles)
        tiles += [1]
        T_MIX = len(tiles)
        tiles += [1] * 4
        T_F = []
        T_F.append(len(tiles)); tiles += [1] * G_T
        T_PW1 = len(tiles)
        tiles += [1] * 8
        T_PW2 = len(tiles)
        tiles += [1] * 4
        T_F.append(len(tiles)); tiles += [1] * G_T
        arrives = [16 * sum(tiles[t % 2:t + 1:2]) for t in range(len(tiles))]

        def freed(t):
            split_before = sum(max(0, min(G_T, t - 1 - t0)) for t0 in T_F)
            if any(t0 <= t - 2 < t0 + G_T for t0 in T_F):
                return s.w_split, split_before
            return s.w_used, t - 1 - split_before

        def slot(t, parts=P):
            return ring[0:parts, t % 2, :]

        def tile_of(t, k, n):
            return slot(t)[:, 0:k * n].rearrange("p (k n) -> p k n", k=k)

        win_v = w_in[0].rearrange("(k p) n -> p k n", p=P)
        nin_v = nsa_w_in_2[0].rearrange("(k p) n -> p k n", p=P)

        STAGES = ("loaded attention_in attended mlstm_in mlstm_rows mlstm_qk mlstm_scanned mlstm_out "
                  "y_1 x_1 mixer_in mixer_attended mixer_turned x_2 x_3 convolved conv_normed x_4 x_5").split()
        def stage(eng, name):
            eng.drain().then_inc(s.stage_end, 1)
            eng.wait_ge(s.stage_end, 4 * (STAGES.index(name) + 1))

        J_IN = 0
        J_IN2 = J_IN + 3 + 3 + 3 + 2 + 4 + 2
        J_OUT = J_IN2 + 4 + 4 + 4
        J_NIN = J_OUT + 8
        J_MIX = J_NIN + 2 + 4 + 2 + 4 + 4
        J_PW2 = J_MIX + 8

        def a_slope(h):
            return 2.0 ** (-8.0 * (h + 1) / A_H)

        def n_slope(h):
            return 2.0 ** (-(h + 1))

        def unit(kind, i, h, q, k, w, v, dist=None, slope=1.0, gate=None, g=0, first=True, last=True):
            un = Unit()
            un.kind, un.i, un.h, un.q, un.k, un.w, un.v = kind, i, h, q, k, w, v
            un.dist, un.slope, un.gate, un.g = dist, slope, gate, g
            un.block = ("swa", "stick").index(kind) * TB + i if kind in ("swa", "stick") else 2 * TB + i
            un.first, un.last = first, last
            return un

        def rows_of(half):
            return slice(64 * half, 64 * half + 64)

        swa_units, stick_units, nsa_units = [], [], []
        for i in range(TB):
            for h in range(A_H):
                half, c_ = h // 3, h % 3
                b0 = max(0, i - 1)
                w = P * (i + 1 - b0)
                swa_units.append(unit(
                    "swa", i, h, aq[rows_of(half), c_, P * i:P * i + P], ak[rows_of(half), P * b0:P * b0 + w], w,
                    lambda b, b0=b0, half=half: av[:, b0 + b, 64 * half:64 * half + 64],
                    swa_bias[:, 256 * h + 256 - w:256 * h + 256], 1.0))
            for h in range(S_H):
                half, c_ = h % 2, h // 2
                w = P * (i + 1)
                stick_units.append(unit(
                    "stick", i, h, sq[rows_of(half), c_, P * i:P * i + P], sk[rows_of(half), c_, 0:w], w,
                    lambda b, h=h: sv[:, b, 64 * h:64 * h + 64]))
            for kind in ("cmp", "win", "sel"):
                for h in range(N_H):
                    g, c_ = h // 4, h % 4
                    cols_ = slice(64 * g, 64 * g + 64)
                    q = nq[rows_of(g), c_, P * i:P * i + P]
                    branch = ("cmp", "sel", "win").index(kind)
                    args = dict(slope=n_slope(h), gate=ng[:, i, 3 * h + branch:3 * h + branch + 1], g=g,
                                first=kind == "cmp", last=kind == "sel")
                    if kind == "cmp":
                        un = unit(kind, i, h, q, kcmp[rows_of(g), 0:N_CMP], N_CMP,
                                  lambda b, g=g: vcmp[:, g, :], cdist[:, i, :], **args)
                    elif kind == "win":
                        b0 = max(0, i - 4)
                        w = P * (i + 1 - b0)
                        un = unit(kind, i, h, q, kw[rows_of(g), P * b0:P * b0 + w], w,
                                  lambda b, b0=b0, cols_=cols_: vw[:, b0 + b, cols_], band[:, 640 - w:640], **args)
                    else:
                        w = P * (i + 1)
                        un = unit(kind, i, h, q, ks[rows_of(g), 0:w], w,
                                  lambda b, cols_=cols_: vs[:, b, cols_], tg[:, g, 0:w], **args)
                    nsa_units.append(un)
        N_SWA = len(swa_units)
        N_FIRST = N_SWA + len(stick_units)
        LAG, LAG_STICK = 2, 3
        N_PAR = 21
        N_F, N_PW = (0, FC + KC), FC
        N_A = (0, FC)
        N_DOWN = (8, 8 + 8 * G_N)
        LAST = 1 + 3 * (G_N - 1) + 1
        POOL_CONV, PE_CONV = (0, 3), 5
        VECTOR_CONV = [n for n in range(KC) if n not in POOL_CONV and n != PE_CONV]
        H_MUL = {0: 0, 3: 8, 5: 16, 6: 24}
        H_OK = {0: 0, 2: 8, 3: 16, 4: 24, 5: 32, 6: 40, 7: 48}

        def weights_row(n):
            return (first_rows if n < N_FIRST else second_rows)[:, n % 4, :]

        def block_end(units, i):
            return i == len(units) - 1 or units[i + 1].i != units[i].i

        block = ctx.enter_context(nc.Block())

        @block.sync
        def _(sp):
            def load(dst, src, arrived):
                sp.dma_start(dst, src).then_inc(arrived, 16)

            for half in range(2):
                load(big[:, 4096 * half:4096 * half + 4096].rearrange("p (t d) -> p t d", d=D),
                     x[0].rearrange("(t p) d -> p t d", p=P)[:, 4 * half:4 * half + 4, :], s.x_in)
            def rows(v, n, w=P):
                return v.rearrange("(a b) -> a b", b=w)
            pr = sc[:, 0:1, :].rearrange("p a b -> p (a b)")
            r0, r1, r2, r3, r4 = (pr[:, P * i:P * i + P] for i in range(5))
            load(r0[V_C:V_C + 8, :], c[0].rearrange("(a b) -> a b", b=P), s.par_in)
            load(r0[V_BMOD:V_BMOD + 24, :], b_mod[0].rearrange("(a b) -> a b", b=P), s.par_in)
            load(r0[V_GPRE:V_GPRE + 8, :], g_pre[0].rearrange("(a b) -> a b", b=P), s.par_in)
            load(r0[V_GPOST:V_GPOST + 8, :], g_post[0].rearrange("(a b) -> a b", b=P), s.par_in)
            load(r0[V_MIX:V_MIX + 16, :], mix_norm_2.rearrange("l (a b) -> (l a) b", b=P), s.par_in)
            load(r0[V_FFN:V_FFN + 16, :], ffn_norm_2.rearrange("l (a b) -> (l a) b", b=P), s.par_in)
            load(r0[V_BPW1:V_BPW1 + 16, :], conv_b_pw1_2[0].rearrange("(a b) -> a b", b=P), s.par_in)
            load(r0[V_BDW:V_BDW + 8, :], conv_b_dw_2[0].rearrange("(a b) -> a b", b=P), s.par_in)
            load(r0[V_LNG:V_LNG + 8, :], conv_ln_g_2[0].rearrange("(a b) -> a b", b=P), s.par_in)
            load(r0[V_LNB:V_LNB + 8, :], conv_ln_b_2[0].rearrange("(a b) -> a b", b=P), s.par_in)
            load(r0[V_BPW2:V_BPW2 + 8, :], conv_b_pw2_2[0].rearrange("(a b) -> a b", b=P), s.par_in)
            wdw = conv_w_dw_2[0].rearrange("t (a b) -> (t a) b", b=P)
            load(r1, wdw[0:P, :], s.par_in)
            load(r2[0:120, :], wdw[P:248, :], s.par_in)
            load(r2[120:128, :], final_norm_2.rearrange("(a b) -> a b", b=P), s.par_in)
            sp.wait_ge(s.const_ok, 1)
            load(r3[0:16, 0:96], m_conv_w[0].rearrange("t (a b) -> (t a) b", b=96), s.par_in)
            load(r3[16:20, 0:96], m_conv_b[0].rearrange("(a b) -> a b", b=96), s.par_in)
            load(r3[20:24, 0:96], m_norm_g[0].rearrange("(a b) -> a b", b=96), s.par_in)
            load(r3[24:28, 0:96], m_skip[0].rearrange("(a b) -> a b", b=96), s.par_in)
            load(r3[28:32, :], pool_scale_2[0].rearrange("(a b) -> a b", b=P), s.par_in)
            for i, pos in enumerate((cmp_pos_k_2, cmp_pos_v_2)):
                load(r4[16 * i:16 * i + 16, :], pos[0].rearrange("(i two) d -> i (two d)", two=2), s.par_in)
            load(misc[0:4, 0:1], m_b_i[0].rearrange("(h o) -> h o", o=1), s.small_in)
            load(misc[0:4, 1:2], m_b_f[0].rearrange("(h o) -> h o", o=1), s.small_in)
            load(misc[:, 2:8], a_sinks[0:1, :].to_broadcast([P, A_H]), s.small_in)
            load(w2s[:, 0, :], cmp_k_w2_2[0], s.small_in)
            load(w2s[:, 1, :], cmp_v_w2_2[0], s.small_in)
            def tile(t, *pairs):
                if t >= 2:
                    sp.wait_ge(*freed(t))
                for dst, src in pairs:
                    load(dst, src, w_ready[t % 2])

            def joined(t, src, pieces):
                w, at, pairs = tile_of(t, KC, sum(n for _, n in pieces)), 0, []
                for c0, n in pieces:
                    pairs.append((w[:, :, at:at + n], src[:, :, c0:c0 + n]))
                    at += n
                tile(t, *pairs)

            for k in range(8):
                tile(k, (slot(k)[:, 0:3 * D], w_mod[0][k * P:(k + 1) * P, :]))
            t = T_IN
            aqt = tile_of(t, KC, A_W).rearrange("p k (r two d) -> p k r two d", two=2, d=A_D)
            if t >= 2:
                sp.wait_ge(s.w_used, t - 1)
            aqs = win_v[:, :, C_AQ:C_AQ + A_W].rearrange("p k (two r d) -> p k r two d", two=2, d=A_D)
            for two in range(2):
                for r_ in range(3):
                    load(aqt[:, :, r_, two, :], aqs[:, :, r_, two, :], w_ready[t % 2])
            for i, pieces in enumerate([((C_AK, A_KVW), (C_SK, S_W)), ((C_AZ, A_W),), ((C_SQ, S_W),),
                                        ((C_AK + A_KVW, A_KVW), (C_SV, S_W)), ((C_SZ, S_W),), ((C_MU, M_W),),
                                        ((C_MVG, VGW),), ((C_MZ, M_W),)]):
                joined(T_IN + 1 + i, win_v, pieces)
            t = T_QK
            qk = slot(t, M_D)[:, 0:768].rearrange("p (w h e) -> p w h e", w=2, h=M_H)
            tile(t, (qk[:, 0], m_wq[0].rearrange("h d e -> d h e")), (qk[:, 1], m_wk[0].rearrange("h d e -> d h e")))
            for i in range(4):
                t = T_OUT + i
                tile(t, (slot(t, M_D)[:, 0:1024].rearrange("p (k n) -> p k n", k=4),
                         w_out[0][0:M_W, 256 * i:256 * i + 256].rearrange("(k p) n -> p k n", p=M_D)),
                     (slot(t)[:, 1024:2304].rearrange("p (k n) -> p k n", k=5),
                      w_out[0][M_W:D, 256 * i:256 * i + 256].rearrange("(k p) n -> p k n", p=P)))
            done = {"w1": 0, "q": 0, "u": 0}
            for at, kind in enumerate(NIN_TILES):
                t = T_NIN + at
                i = done.get(kind, 0)
                if kind == "kv_c":
                    joined(t, nin_v, ((512, 256),))
                elif kind == "k":
                    joined(t, nin_v, ((768, 128), (1024, 128)))
                elif kind == "v":
                    joined(t, nin_v, ((896, 128), (1152, 152)))
                elif kind == "u":
                    joined(t, nin_v, ((1304 + 256 * i, 256),))
                elif kind == "q":
                    qt = tile_of(t, KC, 256).rearrange("p k (r two d) -> p k r two d", two=2, d=N_D)
                    tile(t, *[(qt[:, :, r_, two, :], nin_v[:, :, c0:c0 + 64]) for two in range(2) for r_ in range(2)
                              for c0 in (256 * two + 128 * i + 64 * r_,)])
                else:
                    tile(t, (tile_of(t, 16, P), (cmp_k_w1_2, cmp_v_w1_2)[i][0].rearrange("(i q) n -> q i n", q=P)))
                if kind in done:
                    done[kind] += 1
            t = T_POOL
            tile(t, (slot(t)[:, 0:512].rearrange("p (g e) -> p g e", g=4), pool_w_2[0].rearrange("g c e -> c g e")))
            mo_v = mix_w_out_2[0].rearrange("(k p) n -> p k n", p=P)
            for i in range(4):
                t = T_MIX + i
                tile(t, (tile_of(t, KC, 256), mo_v[:, :, 256 * i:256 * i + 256]))

            def ffn_tiles(l):
                gv = ffn_w_gate_2[l].rearrange("(k p) n -> p k n", p=P)
                uv = ffn_w_up_2[l].rearrange("(k p) n -> p k n", p=P)
                dv = ffn_w_down_2[l].rearrange("(k p) n -> p k n", p=P)
                t0 = T_F[l]
                tile(t0, (tile_of(t0, KC, GC), gv[:, :, 0:GC]))
                tile(t0 + 1, (tile_of(t0 + 1, KC, GC), uv[:, :, 0:GC]))
                with nc.sync.Fori(0, (G_N - 1) // 2) as i:
                    for r in range(2):
                        for j in range(3):
                            t = t0 + 2 + 3 * r + j
                            sp.wait_ge(s.w_split, i * 6 + (G_T * l + t - 1 - t0))
                            dst = tile_of(t, KC, GC) if j < 2 else tile_of(t, 2, D)
                            src = ((gv, uv)[j][:, :, bass.ds(i * (2 * GC) + GC * (r + 1), GC)] if j < 2
                                   else dv[:, bass.ds(i * 4 + 2 * r, 2), :])
                            load(dst, src, w_ready[t % 2])
                t = t0 + LAST
                tile(t, (tile_of(t, 2, D), dv[:, FC - 2:FC, :]))

            ffn_tiles(0)
            p1_v = conv_w_pw1_2[0].rearrange("(k p) n -> p k n", p=P)
            p2_v = conv_w_pw2_2[0].rearrange("(k p) n -> p k n", p=P)
            for i in range(4):
                for j in range(2):
                    t = T_PW1 + 2 * i + j
                    c0 = (D if j == 0 else 0) + 256 * i
                    tile(t, (tile_of(t, KC, 256), p1_v[:, :, c0:c0 + 256]))
            for i in range(4):
                t = T_PW2 + i
                tile(t, (tile_of(t, KC, 256), p2_v[:, :, 256 * i:256 * i + 256]))
            ffn_tiles(1)
            with nc.sync.Fori(0, TB // 2) as i:
                for j in range(2):
                    sp.wait_ge(s.out_ready, i * 2 + (j + 1))
                    sp.dma_start(out[0].rearrange("(t p) d -> p t d", p=P)[:, bass.ds(i * 2 + j, 1), :],
                                 sc[:, j:j + 1, :]).then_inc(out_done[j], 16)
            for j in range(2):
                sp.wait_ge(out_done[j], 16 * TB // 2)
        @block.tensor
        def _(pe):
            mm = pe.matmul

            def need(t):
                pe.wait_ge(w_ready[t % 2], arrives[t])

            def group(j):
                if j >= 2:
                    pe.wait_ge(g_free[j % 2], j // 2)
                return bank(2 * (j % 2), 2)

            def feature_chunk(j, w, kk, src, m, norm=None):
                o = group(j)
                for half in range(2):
                    for k in range(kk):
                        if norm is not None and half == 0:
                            pe.wait_ge(s.h_ok, H_OK[norm] + k + 1)
                        last = mm(o[0:m, 512 * half:512 * half + 512], w(k), src(k)[:, 512 * half:512 * half + 512],
                                  start=k == 0, stop=k == kk - 1)
                last.then_inc(s.g_out, 1)

            def used():
                pe.drain().then_inc(s.w_used, 1)

            pe.wait_ge(s.const_ok, 2)
            pe.wait_ge(s.par_in, 16 * N_PAR)
            for i, (n, o) in enumerate(((128, 0), (128, 128), (128, 256), (32, V_CW), (32, V_POS))):
                last = pe.transpose(ps[:, o:o + n], sc[0:n, 0, P * i:P * i + P], ident[0:n, 0:n])
            last.then_inc(s.tr_done, 1)
            pe.wait_ge(s.x_in, 32)
            for k in range(KC):
                b = 2 + 2 * (k % 2)
                if k >= 2:
                    pe.wait_ge(s.tr_free, k - 1)
                for t in range(TB):
                    last = pe.transpose(ps[:, 512 * b + P * t:512 * b + P * t + P],
                                        big[:, D * t + P * k:D * t + P * k + P], ident[:, :])
                last.then_inc(s.tr_done, 1)

            def norm_sum(n):
                pe.wait_ge(s.sq_used, 8 * n + 8)
                for half in range(2):
                    last = mm(bank(6 + half), ones[:, :], sc[:, 2, 512 * half:512 * half + 512], start=True, stop=True)
                last.then_inc(s.sum_done, 1)

            norm_sum(0)
            pe.wait_ge(s.w_used, KC)
            for n in range(24):
                last = mm(ps[:, 512 + n:513 + n], mod_sum[:, P * n:P * n + P], ones[:, 0:1], start=True, stop=True)
            last.then_inc(s.mod_done, 1)

            stage(pe, "loaded")
            hs = lambda k: ht[:, k, :]
            j = [J_IN]

            def wide(t, n, c0, m, count, norm=None):
                w = tile_of(t, KC, n)
                for i in range(count):
                    feature_chunk(j[0], lambda k: w[:, k, c0 + m * i:c0 + m * i + m], KC, hs, m,
                                  norm if i == 0 else None)
                    j[0] += 1

            def tokens(t, n, c0, m, per, stride):
                w = tile_of(t, KC, n)
                for i in range(TB // per):
                    o = group(j[0])
                    for b in range(per):
                        for k in range(KC):
                            last = mm(o[:, stride * b:stride * b + m], ht[:, k, P * (per * i + b):P * (per * i + b) + P],
                                      w[:, k, c0:c0 + m], start=k == 0, stop=k == KC - 1)
                    last.then_inc(s.g_out, 1)
                    j[0] += 1

            need(T_IN); wide(T_IN, A_W, 0, P, 3, norm=0); used()
            need(T_IN + 1); wide(T_IN + 1, A_W, 0, P, 3); used()
            need(T_IN + 2); wide(T_IN + 2, A_W, 0, P, 3); used()
            need(T_IN + 3); wide(T_IN + 3, S_W, 0, P, 2); used()
            need(T_IN + 4); tokens(T_IN + 4, A_W, 0, A_W, 2, 512); used()
            need(T_IN + 5); wide(T_IN + 5, S_W, 0, P, 2); used()
            stage(pe, "attention_in")

            def attention(units, n0, lag):
                N = len(units)
                for i in range(N + lag + 1):
                    if i < N:
                        un, n = units[i], n0 + i
                        if i >= 2:
                            pe.wait_ge(s.l_done, n - 1)
                        for a in range(0, un.w, 512):
                            e = min(512, un.w - a)
                            last = mm(ps[:, 1024 * (n % 2) + a:1024 * (n % 2) + a + e], un.q, un.k[:, a:a + e],
                                      start=True, stop=True)
                        last.then_inc(s.s_done, 1)
                    if 0 <= i - lag < N:
                        un, n = units[i - lag], n0 + i - lag
                        pe.wait_ge(s.e_done, n + 1)
                        if n >= 1:
                            pe.wait_ge(s.pt_copied, n)
                        row = weights_row(n)
                        for a in range(0, un.w, P):
                            e = min(P, un.w - a)
                            last = pe.transpose(ps[0:e, 2048 + a:2048 + a + P], row[:, a:a + e], ident[:, :])
                        last.then_inc(s.pt_done, 1)
                    if i - lag - 1 >= 0:
                        un, n = units[i - lag - 1], n0 + i - lag - 1
                        pe.wait_ge(s.pt_copied, n + 1)
                        if un.block >= 2 and un.h == 0 and un.first:
                            pe.wait_ge(s.o_free, un.block - 1)
                        half, c_ = un.h % 2, un.h // 2
                        o = bank(6 + un.block % 2)[64 * half:64 * half + 64, P * c_:P * c_ + P]
                        blocks = (un.w + P - 1) // P
                        for b in range(blocks):
                            e = min(P, un.w - P * b)
                            last = mm(o, un.v(b), sc[0:e, 2 + n % 2, P * b:P * b + P],
                                      start=un.first and un.h < 2 and b == 0, stop=un.last and b == blocks - 1,
                                      skip_group_check=True)
                        last.then_inc(s.pv_done, 1)

            attention(swa_units, 0, LAG)
            attention(stick_units, N_SWA, LAG_STICK)
            stage(pe, "attended")
            assert j[0] == J_IN2
            need(T_IN + 6); wide(T_IN + 6, M_W, 0, M_D, 4); used()
            need(T_IN + 7); tokens(T_IN + 7, VGW, 0, VGW, 2, 512); used()
            need(T_IN + 8); wide(T_IN + 8, M_W, 0, M_D, 4); used()
            assert j[0] == J_OUT
            stage(pe, "mlstm_in")
            for g in range(2):
                for t in range(TB):
                    last = pe.transpose(ps[0:4, 1024 * g + P * t:1024 * g + P * t + P], gi[:, t, 4 * g:4 * g + 4],
                                        ident[:, :])
            last.then_inc(s.gates_up, 1)
            pe.wait_ge(s.rows_d, 1)
            for t in range(TB):
                pe.transpose(ps[:, 2048 + P * t:2048 + P * t + P], sc[:, 0, P * t:P * t + P], ident[:, :])
            for h in range(M_H):
                last = mm(ps[:, 3072 + TB * h:3072 + TB * h + TB], selr[:, h, :], mrow[:, 2, :], start=True, stop=True)
            last.then_inc(s.rowcols, 1)
            stage(pe, "mlstm_rows")
            need(T_QK)
            qk = slot(T_QK, M_D)[:, 0:768].rearrange("p (w h e) -> p w h e", w=2, h=M_H)
            for n in range(2 * M_H):
                w, h = n // M_H, n % M_H
                if n >= 2:
                    pe.wait_ge(s.qk_copied, n - 1)
                for half in range(2):
                    last = mm(ps[0:M_D, 1024 * (n % 2) + 512 * half:1024 * (n % 2) + 512 * half + 512],
                              qk[:, w, h, :], cu[:, h, 512 * half:512 * half + 512], start=True, stop=True)
                last.then_inc(s.qk_done, 1)
            for t in range(TB):
                if t >= 2:
                    pe.wait_ge(s.ktok_copied, t - 1)
                for h in range(M_H):
                    last = mm(ps[:, 2048 + 512 * (t % 2) + M_D * h:2048 + 512 * (t % 2) + M_D * h + M_D],
                              cu[:, h, P * t:P * t + P], qk[:, 1, h, :], start=True, stop=True)
                last.then_inc(s.ktok_done, 1)
            used()
            stage(pe, "mlstm_qk")
            for t in range(TB):
                if t >= 2:
                    pe.wait_ge(s.ms_weighted, t - 1)
                for h in range(M_H):
                    mm(ps[:, 512 * (t % 2) + P * h:512 * (t % 2) + P * h + P], mkt[:, h, P * t:P * t + P],
                       mq[:, h, P * t:P * t + P], start=True, stop=True)
                for h in range(M_H):
                    last = mm(ps[:, 1024 + 512 * (t % 2) + P * h:1024 + 512 * (t % 2) + P * h + P], selr[:, h, :],
                              sc[0:4, 1, P * t:P * t + P], start=True, stop=True)
                last.then_inc(s.ms_done, 1)
                if t >= 1:
                    pe.wait_ge(s.mstate, t)
                for h in range(M_H):
                    mm(ps[:, 2048 + 97 * h:2048 + 97 * h + 97], mq[:, h, P * t:P * t + P], ct[:, h, :],
                       start=True, stop=True)
                for h in range(M_H):
                    mm(ps[0:M_D, 3072 + 97 * h:3072 + 97 * h + 97], mk[:, t, h, :], mv[:, t, h, :],
                       start=True, stop=True)
                pe.wait_ge(s.ms_weighted, t + 1)
                for h in range(M_H):
                    last = mm(ps[:, 2560 + 97 * h:2560 + 97 * h + 97], sc[:, 3 * (t % 2), P * h:P * h + P],
                              mv[:, t, h, :], start=True, stop=True)
                last.then_inc(s.mo_done, 1)
            stage(pe, "mlstm_scanned")
            pe.wait_ge(s.ht_ready, 1)
            for n in range(2 * M_H):
                h, half = n // 2, n % 2
                if n >= 2:
                    pe.wait_ge(s.ht_copied, n - 1)
                for b in range(4):
                    last = pe.transpose(ps[0:M_D, 512 * (n % 2) + P * b:512 * (n % 2) + P * b + P],
                                        mv[:, 4 * half + b, h, 0:M_D], ident[:, :])
                last.then_inc(s.ht_done, 1)
            stage(pe, "mlstm_out")
            for i in range(4):
                t = T_OUT + i
                need(t)
                wa = slot(t, M_D)[:, 0:1024].rearrange("p (k n) -> p k n", k=4)
                wb = slot(t)[:, 1024:2304].rearrange("p (k n) -> p k n", k=5)
                for m in range(2):
                    feature_chunk(
                        J_OUT + 2 * i + m,
                        lambda k: wa[:, k, P * m:P * m + P] if k < 4 else wb[:, k - 4, P * m:P * m + P], 9,
                        lambda k: mz[:, k, :] if k < 4 else (az[:, k - 4, :] if k < 7 else sz[:, k - 7, :]), P)
                used()
            norm_sum(1)
            stage(pe, "y_1")
            norm_sum(2)
            stage(pe, "x_1")
            j[0] = J_NIN

            def compress(t, kv):
                src = (pairs_k, pairs_v)[kv]
                w1 = tile_of(t, 16, P)
                if kv:
                    pe.wait_ge(s.cmp_hid, 2)
                    pe.wait_ge(s.cmp_copied, 2)
                pe.wait_ge(g_free[(J_NIN + kv) % 2], (J_NIN + kv) // 2 + 1)
                for n in range(16):
                    mm(ps[:, 3072:3073], w1[:, n, :], cols[:, V_POS + 16 * kv + n:V_POS + 16 * kv + n + 1],
                       start=n == 0, stop=n == 15)
                for g in range(2):
                    for n in range(16):
                        last = mm(ps[:, 2048 + 512 * g:2048 + 512 * g + N_CMP], w1[:, n, :],
                                  src[:, g, 2 * n:2 * n + 16 * (N_CMP - 1) + 1:16], start=n == 0, stop=n == 15)
                last.then_inc(s.cmp_h1, 1)

            def compressed_tokens(kv):
                for g in range(2):
                    pe.wait_ge(s.cmp_hid, 2 * kv + g + 1)
                    if kv:
                        pe.wait_ge(s.cmp_copied, g + 1)
                    o = (3584, 3136)[g]
                    if kv == 0:
                        last = mm(ps[0:64, o:o + N_CMP], w2s[:, 0, :], hid[:, g, 0:N_CMP], start=True, stop=True)
                    else:
                        last = mm(ps[0:N_CMP, o:o + 64], hid[:, g, 0:N_CMP], w2s[:, 1, :], start=True, stop=True)
                    last.then_inc(s.cmp_h2, 1)

            sums_made = 0
            for at, kind in enumerate(NIN_TILES):
                t = T_NIN + at
                need(t)
                if kind == "w1":
                    compress(t, sums_made)
                    sums_made += 1
                elif kind == "v":
                    tokens(t, 280, 0, 280, 2, 512)
                else:
                    wide(t, 256, 0, P, 2, norm=2 if at == 0 else None)
                used()
                if at in (2, 5):
                    compressed_tokens(at // 5)
            assert j[0] == J_MIX
            stage(pe, "mixer_in")
            attention(nsa_units, N_FIRST, LAG)
            stage(pe, "mixer_attended")
            need(T_POOL)
            pe.wait_ge(s.pool_d, 1)
            wp = slot(T_POOL)[:, 0:512].rearrange("p (g e) -> p g e", g=4)
            for g in range(4):
                if g >= 2:
                    pe.wait_ge(s.pool_copied, g - 1)
                for half in range(2):
                    o = 2048 + 1024 * (g % 2) + 512 * half
                    last = mm(ps[:, o:o + 512], wp[:, g, :], u[:, g, 16 + 512 * half:16 + 512 * half + 512],
                              start=True, stop=True)
                last.then_inc(s.pool_mm, 1)
            used()
            stage(pe, "mixer_turned")

            def product(t0, j0, norm=None, src=hs):
                for i in range(4):
                    t = t0 + i
                    need(t)
                    w = tile_of(t, KC, 256)
                    for m in range(2):
                        feature_chunk(j0 + 2 * i + m, lambda k: w[:, k, P * m:P * m + P], KC, src, P,
                                      norm if i + m == 0 else None)
                    used()

            def two_kinds(t, m, kind, n, ready, norm=None):
                o_sem, f_sem = ((s.gate_out, s.gate_free), (s.up_out, s.up_free))[kind]
                if m == 0:
                    pe.wait_ge(w_ready[t % 2], ready)
                pe.wait_ge(f_sem, n + 1)
                w = tile_of(t, KC, 256)
                for half in range(2):
                    for k in range(KC):
                        if norm is not None and half == 0:
                            pe.wait_ge(s.h_ok, H_OK[norm] + k + 1)
                        last = mm(bank(2 * kind + half), w[:, k, P * m:P * m + P],
                                  ht[:, k, 512 * half:512 * half + 512], start=k == 0, stop=k == KC - 1)
                last.then_inc(o_sem, 1)
                if m == 1:
                    used()

            product(T_MIX, J_MIX, src=lambda k: no[:, k, :] if k < 4 else ht[:, k, :])
            norm_sum(3)
            stage(pe, "x_2")

            def split_mm(o, part_, w, rows, start, stop):
                return mm(o, w, rows, start=start and part_ == 0, stop=stop and part_ == 2)

            def gates_and_ups(l, i, group_, norm=None):
                q = 3 * group_ - 1 if group_ else 0
                n = N_F[l] + 2 * group_
                for kind in range(2):
                    t = T_F[l] + q + kind
                    pe.wait_ge(s.w_split, i * 6 + (G_T * l + q + kind + 1))
                    hi, lo = (w_part[p_][:, t % 2, :].rearrange("p (k n) -> p k n", k=KC) for p_ in range(2))
                    if group_:
                        for m in range(2):
                            pe.wait_ge((s.gate_free, s.up_free)[kind], i * 4 + (n + m))
                            pe.wait_ge(s.down_free, i * 16 + (N_DOWN[l] + 8 * (group_ - 2) + 4 + 2 * kind + m + 1))
                    order = [(k, m, half) for m in range(2) for half in range(2) for k in range(KC)]
                    if norm is not None and kind == 0:
                        order = [(k, m, half) for k in range(KC) for m in range(2) for half in range(2)]
                    for k, m, half in order:
                        if norm is not None and kind == 0 and m + half == 0:
                            pe.wait_ge(s.h_ok, H_OK[norm] + k + 1)
                        for p_, (wp_, rp_) in enumerate(PASSES):
                            last = split_mm(bank(4 * kind + 2 * m + half), p_, (hi, lo)[wp_][:, k, P * m:P * m + P],
                                            h_part[rp_][:, k, 512 * half:512 * half + 512], k == 0, k == KC - 1)
                        if k == KC - 1 and half == 1:
                            last.then_inc((s.gate_out, s.up_out)[kind], 1)

            def downs(l, i, group_, after):
                q = 3 * group_ + 4 if group_ < G_N - 1 else LAST
                pe.wait_ge(s.w_split, i * 6 + (G_T * l + q + 1))
                pe.wait_ge(s.act_ready, i * 4 + (N_A[l] + 2 * group_ + 2))
                t = T_F[l] + q
                hi, lo = (w_part[p_][:, t % 2, :].rearrange("p (k n) -> p k n", k=2) for p_ in range(2))
                for c_ in range(KC):
                    if after and c_ < 4:
                        pe.wait_ge((s.gate_free, s.up_free)[c_ // 2], i * 4 + (N_F[l] + 2 * group_ + 2 + c_ % 2 + 2))
                    else:
                        pe.wait_ge(s.down_free, i * 16 + (N_DOWN[l] + 8 * group_ + c_ - 3))
                    for half in range(2):
                        for k in range(2):
                            for p_, (wp_, rp_) in enumerate(PASSES):
                                last = split_mm(bank(2 * (c_ % 4) + half), p_, (hi, lo)[wp_][:, k, P * c_:P * c_ + P],
                                                act_part[rp_][:, group_ % 2, k, 512 * half:512 * half + 512],
                                                k == 0, k == 1)
                    last.then_inc(s.down_out, 1)

            def ffn(l, norm):
                gates_and_ups(l, 0, 0, norm)
                with nc.tensor.Fori(0, (G_N - 1) // 2) as i:
                    for r in range(2):
                        gates_and_ups(l, i, 1 + r)
                        downs(l, i, r, True)
                downs(l, 0, G_N - 1, False)

            ffn(0, 3)
            norm_sum(4)
            stage(pe, "x_3")
            for i in range(4):
                for m in range(2):
                    for kind in range(2):
                        t = T_PW1 + 2 * i + kind
                        two_kinds(t, m, kind, N_PW + 2 * i + m, arrives[t], 4 if i + m + kind == 0 else None)
            pe.wait_ge(s.diag_ok, 1)
            pe.wait_ge(s.up_free, N_PW + PE_CONV + 2)
            for half in range(2):
                for t in range(CONV_W):
                    last = mm(bank(6 + half), tap_diag[:, t, :],
                              zp[:, PE_CONV, t + 512 * half:t + 512 * half + 512], start=t == 0, stop=t == CONV_W - 1)
            last.then_inc(s.conv_out, 1)
            for k in range(KC):
                if k in POOL_CONV:
                    pe.wait_ge(s.zc_ok_pool, POOL_CONV.index(k) + 1)
                elif k == PE_CONV:
                    pe.wait_ge(s.zc_ok_pe, 1)
                else:
                    pe.wait_ge(s.zc_ok, VECTOR_CONV.index(k) + 1)
                for half in range(2):
                    last = mm(bank(4 + half), ones[:, :], zc[:, k, 512 * half:512 * half + 512],
                              start=k == 0, stop=k == KC - 1)
            last.then_inc(s.mean_done, 1)
            stage(pe, "convolved")
            for k in range(KC):
                pe.wait_ge(s.sq_ready, 8 * 5 + k + 1)
                for half in range(2):
                    last = mm(bank(6 + half), ones[:, :], sc[:, k % 2, 512 * half:512 * half + 512],
                              start=k == 0, stop=k == KC - 1)
                last.then_inc(s.sq_used, 1)
            stage(pe, "conv_normed")
            product(T_PW2, J_PW2, norm=5)
            norm_sum(6)
            stage(pe, "x_4")
            ffn(1, 6)
            norm_sum(7)
            stage(pe, "x_5")
            pe.wait_ge(s.h_ok, H_OK[7] + 8)
            for t in range(TB):
                if t >= 2:
                    pe.wait_ge(s.out_ready, t - 1)
                for k in range(KC):
                    last = pe.transpose(ps[:, 1024 * (t % 2) + P * k:1024 * (t % 2) + P * k + P],
                                        ht[:, k, P * t:P * t + P], ident[:, :])
                last.then_inc(s.ft_done, 1)

        @block.scalar
        def _(a):
            f = a.activation
            chained = [0]

            def chain(ins):
                chained[0] += 1
                ins.then_inc(s.act_chain, 1)
                a.wait_ge(s.act_chain, chained[0])

            a.wait_ge(s.cols_ok, 1)
            f(misc[:, 8:16], cols[:, V_C:V_C + 8], ACT.Silu).then_inc(s.c_act, 1)

            def square(n, k, src):
                if 8 * n + k >= 2:
                    a.wait_ge(s.sq_used, 8 * n + k - 1)
                f(sc[:, k % 2, :], src[:, k, :], ACT.Square).then_inc(s.sq_ready, 1)

            def root(n, eps=EPS):
                if n == 5:
                    a.wait_ge(s.sq_used, 8 * n + 8)
                else:
                    a.wait_ge(s.sum_done, n + 1 - (n > 5))
                f(sc[:, 3, :], bank(6, 2), ACT.Sqrt, bias=eps, scale=1.0 / D).then_inc(s.rs_ready, 1)

            for k in range(KC):
                a.wait_ge(s.tr_free, k + 1)
                if k == 0:
                    a.wait_ge(s.tr_done, 1)
                square(0, k, xt)
            root(0)
            stage(a, "loaded")
            for k in range(KC):
                a.wait_ge(s.h_mul, k + 1)
                f(ht[:, k, :], ht[:, k, :], ACT.Identity, bias=misc[:, 16 + k:17 + k]).then_inc(s.h_ok, 1)

            def copy_out(j, jobs):
                for outs, m, per, stride, pieces, funcs, scale in jobs:
                    a.wait_ge(s.g_out, j + 1)
                    src = bank(2 * (j % 2), 2)[0:m, :]
                    for i, (o, func) in enumerate(zip(outs, funcs)):
                        piece = src
                        if per:
                            piece = src[:, 0:per * stride].rearrange("p (b n) -> p b n", b=per)
                            piece = piece[:, :, pieces[i][0]:pieces[i][1]]
                        if len(o.shape) == 4:
                            piece = piece.rearrange("p b (h d) -> p b h d", h=M_H)
                        last = f(o, piece, func, scale=scale)
                    last.then_inc(g_free[j % 2], 1)
                    j += 1
                return j

            w8 = A_D ** -0.5
            cp = lambda o, fn=ACT.Copy, sc_=1.0, m=P: ([o], m, 0, 0, None, [fn], sc_)
            jobs = [cp(aq[:, i, :], sc_=w8) for i in range(3)]
            jobs += [cp(ak)] + [cp(sk[:, i, :]) for i in range(2)]
            jobs += [cp(az[:, i, :], ACT.Silu) for i in range(3)]
            jobs += [cp(sq[:, i, :], sc_=w8) for i in range(2)]
            jobs += [([av[:, 2 * i:2 * i + 2, :], sv[:, 2 * i:2 * i + 2, :]], P, 2, 512, [(0, A_KVW), (A_KVW, A_W)],
                      [ACT.Copy] * 2, 1.0) for i in range(4)]
            jobs += [cp(sz[:, i, :], ACT.Silu) for i in range(2)]
            assert copy_out(J_IN, jobs) == J_IN2
            stage(a, "attention_in")

            def copy_pt(n, un):
                a.wait_ge(s.pt_done, n + 1)
                if n >= 2:
                    a.wait_ge(s.pv_done, n - 1)
                e = min(P, un.w)
                blocks = (un.w + P - 1) // P
                f(sc[0:e, 2 + n % 2, 0:P * blocks], ps[0:e, 2048:2048 + P * blocks], ACT.Copy).then_inc(s.pt_copied, 1)

            def soft_attention(units, n0):
                N = len(units)
                for i in range(N + LAG):
                    if i < N:
                        un, n = units[i], n0 + i
                        a.wait_ge(s.l_done, n + 1)
                        r = stat[:, n % 16, :]
                        row = weights_row(n)[:, 0:un.w]
                        if un.kind == "swa":
                            f(r[:, 3:4], misc[:, 2 + un.h:3 + un.h], ACT.Exp, bias=r[:, 0:1])
                        f(row, row, ACT.Exp, bias=r[:, 0:1], scale=-1.0, accum_out=r[:, 1:2]).then_inc(s.exp_done, 1)
                    if i >= LAG:
                        copy_pt(n0 + i - LAG, units[i - LAG])

            def stick_attention(units, n0):
                N = len(units)
                for i in range(N + LAG_STICK):
                    if i < N:
                        un, n = units[i], n0 + i
                        a.wait_ge(s.s_done, n + 1)
                        if i >= 2:
                            a.wait_ge(s.e_done, n - 1)
                        if i >= 4:
                            a.wait_ge(s.pt_done, n - 3)
                        z = ps[:, 1024 * (n % 2):1024 * (n % 2) + un.w]
                        f(keep[:, n % 2, 0:un.w], z, ACT.Sigmoid, scale=-1.0)
                        f(weights_row(n)[:, 0:un.w], z, ACT.Sigmoid).then_inc(s.l_done, 1)
                    if i >= LAG_STICK:
                        copy_pt(n0 + i - LAG_STICK, units[i - LAG_STICK])

            soft_attention(swa_units, 0)
            a.wait_ge(s.pt_done, N_SWA)
            stick_attention(stick_units, N_SWA)
            stage(a, "attended")
            jobs = [cp(mu[:, h, 3:S + 3], m=M_D) for h in range(M_H)]
            jobs += [([mv[:, 2 * i:2 * i + 2, :, 0:M_D], gi[:, 2 * i:2 * i + 2, :]], P, 2, 512,
                      [(0, M_W), (M_W, VGW)], [ACT.Copy] * 2, 1.0)
                     for i in range(4)]
            jobs += [cp(mz[:, h, :], ACT.Silu, m=M_D) for h in range(M_H)]
            assert copy_out(J_IN2, jobs) == J_OUT
            for h in range(M_H):
                a.wait_ge(s.conv_done, h + 1)
                f(cu[:, h, :], cu[:, h, :], ACT.Silu, bias=cols[0:M_D, V_CB + h:V_CB + h + 1])
            stage(a, "mlstm_in")
            hr = lambda i: ht[0:4, i, :]
            a.wait_ge(s.rows_a, 1)
            chain(f(hr(2), hr(1), ACT.Abs))
            chain(f(hr(2), hr(2), ACT.Exp, scale=-1.0))
            f(hr(2), hr(2), ACT.Ln, bias=1.0).then_inc(s.rows_b, 1)
            a.wait_ge(s.rows_c, 1)
            f(sc[32:36, 0, :], sc[32:36, 0, :], ACT.Exp)
            f(sc[64:68, 0, :], hr(6), ACT.Exp, scale=-1.0)
            f(sc[96:100, 0, :], sc[96:100, 0, :], ACT.Exp)
            f(mrow[:, 2, :], mrow[:, 2, :], ACT.Exp).then_inc(s.rows_d, 1)
            stage(a, "mlstm_rows")
            for n in range(2 * M_H):
                a.wait_ge(s.qk_done, n + 1)
                dst = mq[:, n, :] if n < M_H else mkt[:, n - M_H, :]
                f(dst, ps[0:M_D, 1024 * (n % 2):1024 * (n % 2) + 1024], ACT.Copy,
                  scale=M_D ** -0.5 if n < M_H else 1.0).then_inc(s.qk_copied, 1)
            stage(a, "mlstm_qk")
            for t in range(TB):
                a.wait_ge(s.md_done, t + 1)
                for h in range(M_H):
                    row = sc[:, 3 * (t % 2), P * h:P * h + P]
                    last = f(row, row, ACT.Exp, bias=sc[:, 2, P * t + h:P * t + h + 1])
                last.then_inc(s.mexp_done, 1)
                a.wait_ge(s.mo_done, t + 1)
                if t >= 1:
                    a.wait_ge(s.mstate, t)
                f(intra, ps[:, 2560:2560 + 388], ACT.Copy).then_inc(s.mintra, 1)
            stage(a, "mlstm_scanned")
            for h in range(M_H):
                f(cu[:, h, :], cu[:, h, :], ACT.Copy, scale=cols[0:M_D, V_SKIP + h:V_SKIP + h + 1])
            a.wait_ge(s.ms_sum, 1)
            f(mst[:, 3], mst[:, 2], ACT.Sqrt, bias=EPS, scale=1.0 / M_D).then_inc(s.ms_root, 1)
            stage(a, "mlstm_out")
            for k in range(KC):
                j = J_OUT + k
                copy_out(j, [cp(ht[:, k, :])])
                a.wait_ge(g_free[j % 2], j // 2 + 1)
                square(1, k, ht)
            root(1)
            stage(a, "y_1")
            for k in range(KC):
                a.wait_ge(s.x_add, k + 1)
                square(2, k, xt)
            root(2)
            stage(a, "x_1")

            def queries(j, i):
                a.wait_ge(s.g_out, j + 1)
                src = bank(2 * (j % 2), 2)
                f(nq[0:64, i, :], src[0:64, :], ACT.Copy, scale=N_D ** -0.5 / n_slope(i))
                f(nq[64:128, i, :], src[64:128, :], ACT.Copy, scale=N_D ** -0.5 / n_slope(i + 4)).then_inc(g_free[j % 2], 1)

            def hidden_values(kv):
                a.wait_ge(s.cmp_bias, kv + 1)
                if kv:
                    a.wait_ge(s.cmp_h2, 2)
                for g in range(2):
                    f(hid[:, g, 0:N_CMP], ps[:, 2048 + 512 * g:2048 + 512 * g + N_CMP], ACT.Gelu_apprx_tanh,
                      bias=hbias[:, kv:kv + 1]).then_inc(s.cmp_hid, 1)

            for kv, pairs in enumerate((pairs_k, pairs_v)):
                j = J_NIN + kv
                a.wait_ge(s.g_out, j + 1)
                src = bank(2 * (j % 2), 2)
                for g in range(2):
                    rows = slice(64 * g, 64 * g + 64)
                    f(pairs[0:64, g, :], src[rows, :], ACT.Copy)
                    last = f(pairs[64:128, g, 0:S - 1], src[rows, 1:S], ACT.Copy)
                last.then_inc(g_free[j % 2], 1)
            hidden_values(0)
            for i in range(4):
                queries(J_NIN + 2 + i, i)
            hidden_values(1)
            j = copy_out(J_NIN + 6, [cp(ks), cp(kw)])
            jobs = [([vs[:, 2 * i:2 * i + 2, :], vw[:, 2 * i:2 * i + 2, :], ng[:, 2 * i:2 * i + 2, :]], P, 2, 512,
                     [(0, 128), (128, 256), (256, 280)], [ACT.Copy, ACT.Copy, ACT.Sigmoid], 1.0) for i in range(4)]
            jobs += [cp(u[:, i, 16:S + 16]) for i in range(4)]
            assert copy_out(j, jobs) == J_MIX
            stage(a, "mixer_in")
            soft_attention(nsa_units, N_FIRST)
            stage(a, "mixer_attended")
            for g in range(4):
                a.wait_ge(s.pool_mm, g + 1)
                f(ht[:, 4 + g, :], ps[:, 2048 + 1024 * (g % 2):3072 + 1024 * (g % 2)], ACT.Copy,
                  scale=cols[:, V_PS + g:V_PS + g + 1]).then_inc(s.pool_copied, 1)
            stage(a, "mixer_turned")

            def product_squares(n, j0):
                for k in range(KC):
                    j = j0 + k
                    a.wait_ge(g_free[j % 2], j // 2 + 1)
                    square(n, k, xt)
                root(n)

            product_squares(3, J_MIX)
            stage(a, "x_2")

            def gates(l, i, group_):
                for m in range(2):
                    n = N_F[l] + 2 * group_ + m
                    a.wait_ge(s.gate_out, i * 4 + (n + 1))
                    if group_:
                        a.wait_ge(s.act_ready, i * 4 + (N_A[l] + 2 * group_ + m - 1))
                    f(sc[:, m, :], bank(2 * m, 2), ACT.Silu).then_inc(s.gate_free, 1)

            def ffn(l, norm):
                for k in range(KC):
                    a.wait_ge(s.h_mul, H_MUL[norm] + k + 1)
                    f(h_part[0][:, k, :], sc[:, k % 2, :], ACT.Copy).then_inc(s.h_hi, 1)
                gates(l, 0, 0)
                with nc.scalar.Fori(0, (G_N - 1) // 2) as i:
                    for r in range(2):
                        gates(l, i, 1 + r)
                for k in range(KC):
                    a.wait_ge(s.down_free, N_DOWN[l] + 8 * (G_N - 1) + k + 1)
                    square(norm + 1, k, xt)
                root(norm + 1)

            a.nop().then_inc(s.gate_free, 1)
            ffn(0, 3)
            stage(a, "x_3")
            for n in range(KC):
                a.wait_ge(s.gate_out, N_PW + n + 1)
                a.wait_ge(s.up_free, N_PW + n + 1)
                f(sg, bank(0, 2), ACT.Sigmoid, bias=cols[:, V_BPW1 + 8 + n:V_BPW1 + 9 + n]).then_inc(s.gate_free, 1)
                if n == 0:
                    a.wait_ge(s.h_ok, H_OK[4] + 8)
                    for t in range(CONV_W):
                        last = f(tap_diag[:, t, :], ident[:, :], ACT.Copy,
                                 scale=cols[:, V_WDW + 8 * t + PE_CONV:V_WDW + 8 * t + PE_CONV + 1])
                    last.then_inc(s.diag_ok, 1)
            a.wait_ge(s.conv_out, 1)
            f(zc[:, PE_CONV, :], bank(6, 2), ACT.Identity, bias=cols[:, V_BDW + PE_CONV:V_BDW + PE_CONV + 1])\
                .then_inc(s.zc_ok_pe, 1)
            a.wait_ge(s.mean_done, 1)
            f(sc[:, 2, :], bank(4, 2), ACT.Copy, scale=1.0 / D).then_inc(s.mean_copied, 1)
            stage(a, "convolved")
            for k in range(KC):
                a.wait_ge(s.xc_done, k + 1)
                square(5, k, zc)
            root(5, LN_EPS)
            for k in range(KC):
                a.wait_ge(s.h_mul, H_MUL[5] + k + 1)
                f(ht[:, k, :], zc[:, k, :], ACT.Silu, bias=cols[:, V_LNB + k:V_LNB + k + 1],
                  scale=cols[:, V_LNG + k:V_LNG + k + 1]).then_inc(s.h_ok, 1)
            stage(a, "conv_normed")
            product_squares(6, J_PW2)
            stage(a, "x_4")
            ffn(1, 6)
            stage(a, "x_5")
            for t in range(TB):
                a.wait_ge(s.ft_done, t + 1)
                if t >= 2:
                    a.wait_ge(out_done[t % 2], 16 * (t // 2))
                f(sc[:, t % 2, :], bank(2 * (t % 2), 2), ACT.Copy).then_inc(s.out_ready, 1)

        @block.vector
        def _(v):
            tt, ts, stt = v.tensor_tensor, v.tensor_scalar, v.scalar_tensor_tensor
            mul, add, sub, mx = ALU.mult, ALU.add, ALU.subtract, ALU.max
            chained = [0]

            def chain(ins):
                chained[0] += 1
                ins.then_inc(s.dve_chain, 1)
                v.wait_ge(s.dve_chain, chained[0])

            v.nop().then_inc(s.up_free, 1)
            for _ in range(KC):
                v.nop().then_inc(s.down_free, 1)

            def sum_square(n, k):
                v.wait_ge(s.sq_ready, 8 * n + k + 1)
                if k == 0:
                    v.tensor_copy(sc[:, 2, :], sc[:, 0, :]).then_inc(s.sq_used, 1)
                else:
                    v.wait_ge(s.sq_used, 8 * n + k)
                    tt(sc[:, 2, :], sc[:, 2, :], sc[:, k % 2, :], add).then_inc(s.sq_used, 1)

            def added_and_squared(n, put):
                for k in range(KC + 1):
                    if k < KC:
                        put(k)
                    if k >= 1:
                        sum_square(n, k - 1)
            v.wait_ge(s.tr_done, 1)
            v.tensor_copy(cols[:, :], ps[:, 0:N_COLS]).then_inc(s.cols_ok, 1)

            def turned(k):
                v.wait_ge(s.tr_done, k + 2)
                v.tensor_copy(xt[:, k, :], bank(2 + 2 * (k % 2), 2)).then_inc(s.tr_free, 1)

            added_and_squared(0, turned)
            v.wait_ge(s.cols_ok, 1)
            v.wait_ge(s.small_in, 80)
            v.wait_ge(s.c_act, 1)
            for k in range(KC):
                v.wait_ge(w_ready[k % 2], arrives[k])
                w = slot(k)[:, 0:3 * D]
                if k == 0:
                    ts(mod_sum, w, misc[:, 8:9], None, mul).then_inc(s.w_used, 1)
                else:
                    v.wait_ge(s.w_used, k)
                    stt(mod_sum, w, misc[:, 8 + k:9 + k], mod_sum, mul, add).then_inc(s.w_used, 1)
            v.tensor_scalar(misc[:, 56:62], misc[:, 2:8], -1.0, None, mul)
            v.wait_ge(s.mod_done, 1)
            chain(tt(misc[:, 16:40], ps[:, 512:536], cols[:, V_BMOD:V_BMOD + 24], add))
            stt(misc[:, 40:48], misc[:, 24:32], 1.0, cols[:, V_GPRE:V_GPRE + 8], add, mul)
            tt(misc[:, 48:56], misc[:, 32:40], cols[:, V_GPOST:V_GPOST + 8], mul)

            def root(n):
                v.wait_ge(s.rs_ready, n + 1)
                chain(v.reciprocal(sc[:, 3, :], sc[:, 3, :]))

            def scaled(src, g0, dst, gains=cols, made=s.h_ok):
                for k in range(KC):
                    stt(dst[:, k, :], src[:, k, :], gains[:, g0 + k:g0 + k + 1], sc[:, 3, :], mul, mul).then_inc(made, 1)

            root(0)
            stage(v, "loaded")
            scaled(xt, 40, ht, misc, s.h_mul)
            stage(v, "attention_in")

            def block_out(un, n):
                src = bank(6 + un.block % 2)
                t = slice(P * un.i, P * un.i + P)
                v.wait_ge(s.pv_done, n + 1)
                if un.kind == "sel":
                    ins = v.tensor_copy(no[:, :, t], src.rearrange("p (c t) -> p c t", c=4))
                else:
                    z = (az if un.kind == "swa" else sz)[:, :, t]
                    ins = tt(z, src[:, 0:P * z.shape[1]].rearrange("p (c t) -> p c t", t=P), z, mul)
                ins.then_inc(s.o_free, 1)

            def divided(n, un):
                r = stat[:, n % 16, :]
                row = weights_row(n)[:, 0:un.w]
                v.wait_ge(s.exp_done, n - (N_FIRST - N_SWA if n >= N_FIRST else 0) + 1)
                if un.kind == "swa":
                    chain(tt(r[:, 1:2], r[:, 1:2], r[:, 3:4], add))
                if un.kind == "cmp" and un.i == 0:
                    chain(ts(r[:, 1:2], r[:, 1:2], 1e-30, None, mx))
                chain(v.reciprocal(r[:, 2:3], r[:, 1:2]))
                if un.kind == "cmp":
                    prob = psum_p[:, un.g, 4:4 + N_CMP]
                    if un.h % 4 == 0:
                        chain(ts(prob, row, r[:, 2:3], None, mul))
                    else:
                        chain(stt(prob, row, r[:, 2:3], prob, mul, add))
                if un.gate is not None:
                    ts(row, row, r[:, 2:3], un.gate, mul, mul).then_inc(s.e_done, 1)
                else:
                    ts(row, row, r[:, 2:3], None, mul).then_inc(s.e_done, 1)

            def selection(un):
                pp = psum_p[:, un.g, :]
                i0, i1, top, rep = (imp[:, 16 * a_:16 * a_ + 16] for a_ in range(4))
                chain(v.tensor_reduce(i0, pp[:, 4:68].rearrange("p (j n) -> p j n", n=4)[:, :, 0:3], AX.X, add))
                chain(tt(i1, pp[:, 7:68:4], pp[:, 3:64:4], add))
                chain(stt(i0, i1, 0.5, i0, mul, add))
                chain(tt(i0, i0, force[:, un.i, :], add))
                chain(v.max(top[:, 0:8], i0))
                chain(v.match_replace(rep, top[:, 0:8], i0, -BIGF))
                chain(ts(rep, rep, -2e38, NEG, ALU.is_gt, mul))
                nb = 2 * (un.i + 1)
                chain(tt(tg[:, un.g, 0:un.w].rearrange("p (b n) -> p b n", b=nb),
                         causal[:, P * (7 - un.i):P * (7 - un.i) + un.w].rearrange("p (b n) -> p b n", b=nb),
                         rep[:, 0:nb].unsqueeze(2).to_broadcast([P, nb, 64]), add))

            def soft_attention(units, n0):
                N = len(units)
                for i in range(N + LAG + 2):
                    if i < N:
                        un, n = units[i], n0 + i
                        if un.kind == "sel" and un.h % 4 == 0:
                            selection(un)
                        v.wait_ge(s.s_done, n + 1)
                        if i >= 4:
                            v.wait_ge(s.pt_done, n - 3)
                        r = stat[:, n % 16, :]
                        first = misc[:, 56 + un.h:57 + un.h] if un.kind == "swa" else (
                            1e20 if un.kind == "cmp" else BIGF)
                        v.tensor_tensor_reduce(weights_row(n)[:, 0:un.w], un.dist,
                                               ps[:, 1024 * (n % 2):1024 * (n % 2) + un.w],
                                               -un.slope, first, add, ALU.min, r[:, 0:1]).then_inc(s.l_done, 1)
                    if 0 <= i - 1 < N:
                        divided(n0 + i - 1, units[i - 1])
                    e = i - LAG - 2
                    if e >= 0 and block_end(units, e):
                        block_out(units[e], n0 + e)

            def stick_attention(units, n0):
                N = len(units)
                for i in range(1, N + LAG_STICK + 2):
                    if i - 1 < N:
                        un, n = units[i - 1], n0 + i - 1
                        v.wait_ge(s.z_masked, i)
                        rest = left[:, n % 2, :]
                        back = rest[:, S - un.w:S - 1][:, ::-1]
                        chain(v.tensor_tensor_scan(back, keep[:, n % 2, 1:un.w][:, ::-1],
                                                   ones[:, 0:1].to_broadcast([P, un.w - 1]), 1.0, mul, mul))
                        row = weights_row(n)[:, 0:un.w]
                        tt(row, row, rest[:, S - un.w:S], mul).then_inc(s.e_done, 1)
                    e = i - LAG_STICK - 2
                    if e >= 0 and block_end(units, e):
                        block_out(units[e], n0 + e)

            soft_attention(swa_units, 0)
            chain(v.memset(left[:, :, S - 1:S], 1.0))
            stick_attention(stick_units, N_SWA)
            stage(v, "attended")
            v.wait_ge(s.mu_pad, 1)
            for h in range(M_H):
                jm = J_IN2 + h
                v.wait_ge(g_free[jm % 2], jm // 2 + 1)
                w = lambda t: cols[0:M_D, V_CW + 4 * t + h:V_CW + 4 * t + h + 1]
                chain(ts(cu[:, h, :], mu[:, h, 0:S], w(0), None, mul))
                for t in range(1, M_CONV):
                    ins = stt(cu[:, h, :], mu[:, h, t:t + S], w(t), cu[:, h, :], mul, add)
                    if t < M_CONV - 1:
                        chain(ins)
                ins.then_inc(s.conv_done, 1)
            stage(v, "mlstm_in")
            hr = lambda i: ht[0:4, i, :]
            chunked = lambda ap: ap.rearrange("p (t n) -> p t n", n=P)
            per = lambda ap: ap.unsqueeze(2).to_broadcast([4, TB, P])
            v.wait_ge(s.gates_up, 1)
            ts(hr(0), ps[0:4, 0:1024], misc[0:4, 0:1], None, add)
            ts(hr(1), ps[0:4, 1024:2048], misc[0:4, 1:2], None, add).then_inc(s.rows_a, 1)
            v.memset(hr(4), 1.0)
            chain(v.memset(sc[:, 0, :], 0.0))
            chain(v.memset(hr(4)[:, 0:S:P], 0.0))
            v.wait_ge(s.rows_b, 1)
            chain(stt(hr(3), hr(1), 0.0, hr(2), ALU.min, sub))
            v.tensor_tensor_scan(hr(5), hr(4), hr(3), 0.0, mul, add)
            chain(v.tensor_tensor_scan(hr(6), hr(3), hr(0), 0.0, add, mx))
            chain(tt(sc[0:4, 0, :], hr(0), hr(5), sub))
            tt(sc[0:4, 1, :], hr(5), hr(6), sub)
            v.memset(mrow[:, 0, 0:1], 0.0)
            v.tensor_copy(mrow[:, 0, 1:TB], hr(6)[:, P - 1:S - P:P])
            chain(tt(mrow[:, 1, :], hr(5)[:, P - 1:S:P], hr(6)[:, P - 1:S:P], sub))
            chain(tt(mrow[:, 2, :], mrow[:, 1, :], mrow[:, 0, :], add))
            tt(chunked(sc[32:36, 0, :]), chunked(sc[0:4, 1, :]), per(mrow[:, 0, :]), add)
            tt(chunked(sc[96:100, 0, :]), chunked(sc[0:4, 0, :]), per(mrow[:, 1, :]), add).then_inc(s.rows_c, 1)
            v.wait_ge(s.rowcols, 1)
            v.tensor_copy(sc[:, 2, :], bank(4, 2))
            v.tensor_copy(car.rearrange("p h t -> p (h t)"), ps[:, 3072:3072 + M_H * TB])
            stage(v, "mlstm_rows")
            rc = sc[:, 2, :].rearrange("p (t n) -> p t n", n=P)
            for t in range(TB):
                v.wait_ge(s.ktok_done, t + 1)
                o = 2048 + 512 * (t % 2)
                tt(mk[:, t], ps[:, o:o + M_W].rearrange("p (h d) -> p h d", h=M_H),
                   rc[:, t, 96:100].unsqueeze(2).to_broadcast([P, M_H, M_D]), mul).then_inc(s.ktok_copied, 1)
            stage(v, "mlstm_qk")
            for t in range(TB):
                v.wait_ge(s.ms_done, t + 1)
                if t >= 2:
                    v.wait_ge(s.mo_done, t - 1)
                row = sc[:, 3 * (t % 2), 0:512].rearrange("p (h n) -> p h n", h=M_H)
                sl = lambda b: ps[:, 512 * b:512 * b + 512].rearrange("p (h n) -> p h n", h=M_H)
                tt(row, sl(2 + t % 2), tri[:, :].unsqueeze(1).to_broadcast([P, M_H, P]), add).then_inc(s.md_done, 1)
                v.wait_ge(s.mexp_done, t + 1)
                tt(row, sl(t % 2), row, mul).then_inc(s.ms_weighted, 1)
                v.wait_ge(s.mo_done, t + 1)
                for h in range(M_H):
                    stt(ct[:, h, :], ct[:, h, :], car[0:M_D, h, t:t + 1], ps[0:M_D, 3072 + 97 * h:3169 + 97 * h], mul, add)
                v.wait_ge(s.mintra, t + 1)
                for h in range(M_H):
                    last = stt(mv[:, t, h, :], ps[:, 2048 + 97 * h:2145 + 97 * h], rc[:, t, 32 + h:33 + h],
                               intra[:, h, :], mul, add)
                last.then_inc(s.mstate, 1)
            stage(v, "mlstm_scanned")
            hn = mv.rearrange("p t h d -> p (t h) d")
            m0, m1, m2, m3 = (mst[:, i] for i in range(4))
            f0, f1, f2, f3 = (m.rearrange("p t h -> p (t h)") for m in (m0, m1, m2, m3))
            wide = lambda m: m.unsqueeze(2).to_broadcast([P, TB * M_H, M_D])
            chain(stt(f0, hn[:, :, M_D], -1.0, hn[:, :, M_D], mul, mx))
            chain(tt(m0, m0, rc[:, :, 64:68], mx))
            chain(v.reciprocal(f1, f0))
            chain(tt(hn[:, :, 0:M_D], hn[:, :, 0:M_D], wide(f1), mul))
            sqs = ht[:, 4:7, :].rearrange("p a b -> p (a b)").rearrange("p (a d) -> p a d", d=M_D)
            chain(tt(sqs, hn[:, :, 0:M_D], hn[:, :, 0:M_D], mul))
            v.tensor_reduce(f2, sqs, AX.X, add).then_inc(s.ms_sum, 1)
            v.wait_ge(s.ms_root, 1)
            chain(v.reciprocal(f1, f3))
            tt(hn[:, :, 0:M_D], hn[:, :, 0:M_D], wide(f1), mul).then_inc(s.ht_ready, 1)
            for n in range(2 * M_H):
                h, half = n // 2, n % 2
                c_ = slice(512 * half, 512 * half + 512)
                v.wait_ge(s.ht_done, n + 1)
                if n == 0:
                    v.wait_ge(s.ms_root, 1)
                tmp = sc[0:M_D, 3, c_]
                stt(tmp, ps[0:M_D, 512 * (n % 2):512 * (n % 2) + 512], cols[0:M_D, V_NG + h:V_NG + h + 1],
                    cu[:, h, c_], mul, add).then_inc(s.ht_copied, 1)
                v.wait_ge(s.ht_copied, n + 1)
                tt(mz[:, h, c_], tmp, mz[:, h, c_], mul)
            stage(v, "mlstm_out")
            for k in range(KC):
                sum_square(1, k)
            root(1)
            stage(v, "y_1")

            def first_added(k):
                chain(stt(ht[:, k, :], ht[:, k, :], misc[:, 48 + k:49 + k], sc[:, 3, :], mul, mul))
                tt(xt[:, k, :], xt[:, k, :], ht[:, k, :], add).then_inc(s.x_add, 1)

            added_and_squared(2, first_added)
            root(2)
            stage(v, "x_1")
            scaled(xt, V_MIX, ht)
            v.wait_ge(s.pw_made, 1)
            v.reciprocal(pw_rc, pw_rc)
            for kv in range(2):
                v.wait_ge(s.cmp_h1, kv + 1)
                v.tensor_copy(hbias[:, kv:kv + 1], ps[:, 3072:3073]).then_inc(s.cmp_bias, 1)
                for g in range(2):
                    v.wait_ge(s.cmp_h2, 2 * kv + g + 1)
                    src = ps[:, (3584, 3136)[g]:(3648, 3200)[g]]
                    if kv == 0:
                        ins = v.tensor_copy(kcmp[64 * g:64 * g + 64, 0:N_CMP], src[0:64, 0:N_CMP])
                    else:
                        ins = v.tensor_copy(vcmp[:, g, :], src[0:N_CMP, :])
                    ins.then_inc(s.cmp_copied, 1)
            v.memset(psum_p, 0.0)
            stage(v, "mixer_in")
            soft_attention(nsa_units, N_FIRST)
            stage(v, "mixer_attended")
            stage(v, "mixer_turned")

            def add_product(j0, bias, norm):
                def put(k):
                    j = j0 + k
                    v.wait_ge(s.g_out, j + 1)
                    src = bank(2 * (j % 2), 2)
                    if bias is None:
                        ins = tt(xt[:, k, :], src, xt[:, k, :], add)
                    else:
                        ins = stt(xt[:, k, :], src, cols[:, bias + k:bias + k + 1], xt[:, k, :], add, add)
                    ins.then_inc(g_free[j % 2], 1)
                added_and_squared(norm, put)
                root(norm)

            add_product(J_MIX, None, 3)
            stage(v, "x_2")

            def split_tile(l, i, q):
                t = T_F[l] + q
                v.wait_ge(w_ready[t % 2], i * 48 + arrives[t])
                raw = slot(t)[:, 0:KC * GC]
                v.tensor_copy(w_part[0][:, t % 2, :], raw).then_inc(s.w_hi, 1)
                v.wait_ge(s.w_hi, i * 6 + (G_T * l + q + 1))
                tt(w_part[1][:, t % 2, :], raw, w_part[0][:, t % 2, :].bitcast(F32), sub).then_inc(s.w_split, 1)

            def hidden(l, i, group_):
                for m in range(2):
                    n, c_ = N_F[l] + 2 * group_ + m, N_A[l] + 2 * group_ + m
                    v.wait_ge(s.up_out, i * 4 + (n + 1))
                    v.wait_ge(s.gate_free, i * 4 + (n + 2))
                    row = sc[:, 2 + m, :]
                    hi, lo = (act_part[p_][:, group_ % 2, m, :] for p_ in range(2))
                    tt(row, bank(4 + 2 * m, 2), sc[:, m, :], mul).then_inc(s.up_free, 1)
                    v.wait_ge(s.up_free, i * 4 + (n + 2))
                    v.tensor_copy(hi, row).then_inc(s.act_hi, 1)
                    v.wait_ge(s.act_hi, i * 4 + (c_ + 1))
                    tt(lo, row, hi.bitcast(F32), sub).then_inc(s.act_ready, 1)

            def add_down(l, i, group_, k):
                v.wait_ge(s.down_out, i * 16 + (N_DOWN[l] - 8 + 8 * group_ + k + 1))
                v.wait_ge(s.down_free, i * 16 + (N_DOWN[l] + 8 * (group_ - 1) + k + 1))
                tt(xt[:, k, :], bank(2 * (k % 4), 2), xt[:, k, :], add).then_inc(s.down_free, 1)

            def middle(l, i, group_, add_before=True):
                q = 3 * group_ - 1
                split_tile(l, i, q)
                if add_before:
                    for k in range(KC):
                        add_down(l, i, group_ - 2, k)
                split_tile(l, i, q + 1)
                v.wait_ge(s.gate_out, i * 4 + (N_F[l] + 2 * group_ + 2))
                split_tile(l, i, q + 2)
                hidden(l, i, group_)

            def ffn(l, norm, gain):
                t0 = T_F[l]
                split_tile(l, 0, 0)
                for k in range(KC + 1):
                    if k < KC:
                        if k >= 2:
                            v.wait_ge(s.h_ok, H_OK[norm] + k - 1)
                        stt(sc[:, k % 2, :], xt[:, k, :], cols[:, gain + k:gain + k + 1], sc[:, 3, :], mul, mul)\
                            .then_inc(s.h_mul, 1)
                    if k >= 1:
                        v.wait_ge(s.h_hi, 8 * l + k)
                        tt(h_part[1][:, k - 1, :], sc[:, (k - 1) % 2, :], h_part[0][:, k - 1, :].bitcast(F32), sub)\
                            .then_inc(s.h_ok, 1)
                split_tile(l, 0, 1)
                hidden(l, 0, 0)
                middle(l, 0, 1, add_before=False)
                middle(l, 0, 2)
                with nc.vector.Fori(0, (G_N - 3) // 2) as i:
                    for r in range(2):
                        middle(l, i, 3 + r)
                split_tile(l, 0, LAST)
                for k in range(KC):
                    add_down(l, 0, G_N - 2, k)
                added_and_squared(norm + 1, lambda k: add_down(l, 0, G_N - 1, k))
                root(norm + 1)

            ffn(0, 3, V_FFN)
            stage(v, "x_3")
            scaled(xt, V_MIX + 8, ht)
            taps = lambda t, n: cols[:, V_WDW + 8 * t + n:V_WDW + 8 * t + n + 1]
            v.wait_ge(s.pad_ok, 1)

            def gated(n):
                v.wait_ge(s.up_out, N_PW + n + 1)
                v.wait_ge(s.gate_free, N_PW + n + 2)
                stt(zp[:, n, CONV_W - 1:], bank(2, 2), cols[:, V_BPW1 + n:V_BPW1 + n + 1], sg, add, mul)\
                    .then_inc(s.up_free, 1)

            def convolve(n, t0, t1):
                if t0 == 0:
                    v.wait_ge(s.up_free, N_PW + n + 2)
                for t in range(t0, t1):
                    if t == 0:
                        ins = ts(zc[:, n, :], zp[:, n, 0:S], taps(0, n), cols[:, V_BDW + n:V_BDW + n + 1], mul, add)
                    else:
                        ins = stt(zc[:, n, :], zp[:, n, t:t + S], taps(t, n), zc[:, n, :], mul, add)
                    if t < CONV_W - 1:
                        chain(ins)
                    else:
                        ins.then_inc(s.zc_ok, 1)

            gated(0); gated(1)
            convolve(1, 0, 22); gated(2); convolve(1, 22, CONV_W)
            convolve(2, 0, 13); gated(3); convolve(2, 13, CONV_W)
            gated(4); convolve(4, 0, 21); gated(5); convolve(4, 21, CONV_W)
            gated(6); convolve(6, 0, 22); gated(7); convolve(6, 22, CONV_W)
            convolve(7, 0, CONV_W)
            stage(v, "convolved")
            v.wait_ge(s.mean_copied, 1)
            for k in range(KC):
                tt(zc[:, k, :], zc[:, k, :], sc[:, 2, :], sub).then_inc(s.xc_done, 1)
            root(5)
            for k in range(KC):
                tt(zc[:, k, :], zc[:, k, :], sc[:, 3, :], mul).then_inc(s.h_mul, 1)
            stage(v, "conv_normed")
            add_product(J_PW2, V_BPW2, 6)
            stage(v, "x_4")
            ffn(1, 6, V_FFN + 8)
            stage(v, "x_5")
            scaled(xt, V_FINAL, ht)

        @block.gpsimd
        def _(g):
            chained = [0]

            def chain(ins):
                chained[0] += 1
                ins.then_inc(s.pool_chain, 1)
                g.wait_ge(s.pool_chain, chained[0])

            def select(o, pattern, op, fill, base, mult):
                return g.affine_select(out=o, in_=o, pattern=pattern, compare_op=op, fill=fill, base=base,
                                       channel_multiplier=mult)

            g.memset(sc[:, 0, 384:512], 0.0).then_inc(s.const_ok, 1)
            g.memset(ones[:, :], 1.0)
            chain(g.memset(ident[:, :], 0.0))
            select(ident[:, :], [[-1, P]], ALU.not_equal, 1.0, 0, 1).then_inc(s.const_ok, 1)
            dist = ht[:, 0, 0:256]
            chain(g.iota(dist, [[-1, 256]], base=P, channel_multiplier=1, allow_small_or_imprecise_dtypes=True))
            for h in range(A_H):
                o = swa_bias[:, 256 * h:256 * h + 256]
                chain(g.tensor_scalar(o, dist, -a_slope(h), 0.0, ALU.mult, ALU.add))
                chain(select(o, [[-1, 256]], ALU.is_ge, NEG, P, 1))
                chain(select(o, [[1, 256]], ALU.is_gt, NEG, 0, -1))
            chain(g.memset(tri[:, :], 0.0))
            chain(select(tri[:, :], [[1, P]], ALU.is_ge, NEG, 0, -1))
            stage(g, "loaded")
            stage(g, "attention_in")
            for i, un in enumerate(stick_units):
                n = N_SWA + i
                g.wait_ge(s.l_done, n + 1)
                for row, fill in ((keep[:, n % 2, :], 1.0), (weights_row(n), 0.0)):
                    last = select(row[:, un.w - P:un.w], [[-1, P]], ALU.is_gt, fill, 0, 1)
                last.then_inc(s.z_masked, 1)
            stage(g, "attended")
            g.memset(mu[:, :, 0:3], 0.0).then_inc(s.mu_pad, 1)
            g.memset(selr, 0.0)
            chain(g.memset(ct, 0.0))
            for h in range(M_H):
                chain(select(selr[:, h, :], [[0, P]], ALU.not_equal, 1.0, -h, 1))
            chain(g.memset(mv[:, :, :, M_D], 1.0))
            stage(g, "mlstm_in")
            chain(g.iota(causal[:, :], [[1, S]], base=P - S, channel_multiplier=-1, allow_small_or_imprecise_dtypes=True))
            chain(select(causal[:, :], [[-1, S]], ALU.is_ge, NEG, S - P, 1))
            chain(g.iota(band[:, :], [[1, 640]], base=-512, channel_multiplier=-1, allow_small_or_imprecise_dtypes=True))
            chain(select(band[:, :], [[-1, 640]], ALU.is_ge, NEG, 512, 1))
            chain(select(band[:, :], [[1, 640]], ALU.is_gt, NEG, 0, -1))
            stage(g, "mlstm_rows")
            stage(g, "mlstm_qk")
            stage(g, "mlstm_scanned")
            stage(g, "mlstm_out")
            stage(g, "y_1")
            stage(g, "x_1")
            flat = cdist.rearrange("p a b -> p (a b)")
            chain(g.iota(flat, [[-P, TB], [16, N_CMP]], base=31, channel_multiplier=-1, allow_small_or_imprecise_dtypes=True))
            chain(select(cdist, [[P, TB], [-16, N_CMP]], ALU.is_ge, NEG, -31, 1))
            chain(g.memset(force, 0.0))
            for hb in range(2):
                o = force[64 * hb:64 * hb + 64]
                chain(select(o, [[2, TB], [-1, 16]], ALU.not_equal, 1e4, hb, 0))
                chain(select(o, [[2, TB], [-1, 16]], ALU.not_equal, 1e4, hb - 1, 0))
                chain(select(o, [[0, TB], [1, 16]], ALU.not_equal, 1e4, 0, 0))
                chain(select(o, [[2, TB], [-1, 16]], ALU.is_ge, NEG, hb, 0))
            g.iota(pw_rc, [[1, 16]], base=1, channel_multiplier=0, allow_small_or_imprecise_dtypes=True)\
                .then_inc(s.pw_made, 1)
            chain(g.memset(u[:, :, 0:16], 0.0))
            stage(g, "mixer_in")
            ta = ht[:, 0:2, :].rearrange("p a b -> p (a b)")
            tb = ht[:, 2:4, :].rearrange("p a b -> p (a b)")
            chain(g.memset(ta[:, 0:16], 0.0))
            chain(g.memset(tb[:, 0:16], 0.0))
            for gi_ in range(4):
                w = 2 ** (gi_ + 1)
                src, step = u[:, gi_, :], 1
                for k in range(gi_ + 1):
                    dst = (ta, tb)[k % 2]
                    chain(g.tensor_tensor(dst[:, 16:16 + S], src[:, 16:16 + S], src[:, 16 - step:16 - step + S], ALU.add))
                    src, step = dst, 2 * step
                rcw = pw_rc[:, 0:w]
                tw = misc[:, 192:192 + w]
                chain(g.tensor_scalar(tw, rcw, float(w), 1.0, ALU.mult, ALU.max))
                chain(g.tensor_tensor(src[:, 16:16 + w], src[:, 16:16 + w], tw, ALU.mult))
                chain(g.tensor_scalar(src[:, 16:16 + S], src[:, 16:16 + S], 1.0 / w, 1.0, ALU.mult, ALU.mult))
                chain(g.tensor_tensor(u[:, gi_, 16:16 + S], src[:, 16:16 + S], u[:, gi_, 16:16 + S], ALU.subtract))
            g.nop().then_inc(s.pool_d, 1)
            stage(g, "mixer_attended")
            stage(g, "mixer_turned")
            stage(g, "x_2")
            stage(g, "x_3")
            g.memset(zp[:, :, 0:CONV_W - 1], 0.0).then_inc(s.pad_ok, 1)
            g.wait_ge(s.pad_ok, 1)
            for n in POOL_CONV:
                g.wait_ge(s.up_free, N_PW + n + 2)
                taps = lambda t: cols[:, V_WDW + 8 * t + n:V_WDW + 8 * t + n + 1]
                chain(g.tensor_scalar(zc[:, n, :], zp[:, n, 0:S], taps(0), cols[:, V_BDW + n:V_BDW + n + 1],
                                      ALU.mult, ALU.add))
                for t in range(1, CONV_W):
                    chain(g.tensor_scalar(ptmp, zp[:, n, t:t + S], taps(t), 1.0, ALU.mult, ALU.mult))
                    chain(g.tensor_tensor(zc[:, n, :], zc[:, n, :], ptmp, ALU.add))
                g.nop().then_inc(s.zc_ok_pool, 1)
            stage(g, "convolved")
            for name in STAGES[STAGES.index("convolved") + 1:]:
                stage(g, name)


_INS = ["x", "c", "w_mod", "b_mod", "g_pre", "g_post", "w_in", "m_conv_w", "m_conv_b", "m_wq", "m_wk", "m_b_i", "m_b_f",
        "m_norm_g", "m_skip", "a_sinks", "w_out", "mix_norm_2", "ffn_norm_2", "nsa_w_in_2", "cmp_pos_k_2",
        "cmp_pos_v_2", "cmp_k_w1_2", "cmp_k_w2_2", "cmp_v_w1_2", "cmp_v_w2_2", "pool_w_2", "pool_scale_2",
        "mix_w_out_2", "conv_w_pw1_2", "conv_b_pw1_2", "conv_w_dw_2", "conv_b_dw_2", "conv_ln_g_2", "conv_ln_b_2",
        "conv_w_pw2_2", "conv_b_pw2_2", "ffn_w_gate_2", "ffn_w_up_2", "ffn_w_down_2", "final_norm_2"]
_OUTS = [((1, S, D), "float32")]


def kernel(**inputs):
    import numpy as _np
    import concourse.bacc as _bacc
    from concourse import mybir as _mybir
    from concourse.bass_utils import run_bass_kernel_spmd as _run

    nc = _bacc.Bacc("TRN2", target_bir_lowering=False, num_devices=1)
    arrays, args = {}, []
    for name in _INS:
        a = _np.ascontiguousarray(inputs[name])
        arrays[f"in_{name}_dram"] = a
        args.append(nc.dram_tensor(f"in_{name}_dram", a.shape, _mybir.dt.from_np(a.dtype), kind="ExternalInput").ap())
    for i, (shape, dtype) in enumerate(_OUTS):
        dt = _mybir.dt.from_np(_np.dtype(dtype))
        args.append(nc.dram_tensor(f"out_{i}_dram", shape, dt, kind="ExternalOutput").ap())
    build(nc, *args)
    r = _run(nc, [arrays], core_ids=[0])
    return r.results[0]["out_0_dram"]
```
